# Optimizing a Trainium2 kernel written in Bass

```python
import jax
import jax.numpy as jnp
from jax import lax
import numpy as np

D_MODEL = 1024
BATCH = 1
SEQ = 512
DEPTH = 2

N_EVEN = (DEPTH + 1) // 2
N_ODD = DEPTH // 2
F32 = jnp.float32
NORM_EPS = 1e-6
D_FF = 2816
CONV_WIDTH = 4

LRU_WIDTH = D_MODEL // 2
LRU_BLOCKS = 8
LRU_BLOCK = LRU_WIDTH // LRU_BLOCKS
LRU_C = 8.0

RWKV_WIDTH = D_MODEL // 2
RWKV_HEADS = 8
RWKV_HEAD_DIM = RWKV_WIDTH // RWKV_HEADS
DECAY_RANK = 64
ICLR_RANK = 64
GATE_RANK = 128
RWKV_GN_EPS = 64e-5
SHIFT_WIDTH = 3 * RWKV_WIDTH + DECAY_RANK + ICLR_RANK + GATE_RANK
AB_IN = 2 * LRU_WIDTH + SHIFT_WIDTH
AB_MIX = LRU_WIDTH + RWKV_WIDTH

DN_HEADS = 8
DN_HEAD_DIM = 128
DN_WIDTH = DN_HEADS * DN_HEAD_DIM
DN_CHUNK = 64
C_IN = 4 * DN_WIDTH + 2 * DN_HEADS

kernel_name = 'hybrid_rglru_rwkv7_gdn_macaron'

def rmsnorm(x, w, eps=NORM_EPS):
    xf = x.astype(F32)
    y = xf * lax.rsqrt(jnp.mean(xf * xf, axis=-1, keepdims=True) + eps)
    return (y * w.astype(F32)).astype(x.dtype)

def swiglu(x, w_gate, w_up, w_down):
    return (jax.nn.silu(x @ w_gate) * (x @ w_up)) @ w_down

def causal_dwconv(x, w):
    k_w = w.shape[0]
    s = x.shape[1]
    xp = jnp.pad(x, ((0, 0), (k_w - 1, 0), (0, 0)))
    return sum(w[j] * xp[:, j:j + s] for j in range(k_w))

def token_shift(x):
    return jnp.pad(x[:, :-1], ((0, 0), (1, 0), (0, 0)))

def rg_lru(x, gate_a_w, gate_a_b, gate_x_w, gate_x_b, a_param):
    b, s, _ = x.shape
    xb = x.reshape(b, s, LRU_BLOCKS, LRU_BLOCK)
    r = jax.nn.sigmoid(jnp.einsum('bsgi,gij->bsgj', xb, gate_a_w).reshape(b, s, LRU_WIDTH) + gate_a_b)
    i = jax.nn.sigmoid(jnp.einsum('bsgi,gij->bsgj', xb, gate_x_w).reshape(b, s, LRU_WIDTH) + gate_x_b)
    log_a = -LRU_C * r.astype(F32) * jax.nn.softplus(-a_param.astype(F32))
    a = jnp.exp(log_a)
    u = jnp.sqrt(-jnp.expm1(2.0 * log_a)) * (i * x).astype(F32)

    def combine(c1, c2):
        a1, b1 = c1
        a2, b2 = c2
        return a1 * a2, a2 * b1 + b2

    _, h = lax.associative_scan(combine, (a, u), axis=1)
    return h.astype(x.dtype)

def rwkv7_time_mix(p, w0, w2, a0, a2, g2, k_k, k_a, r_k, ln_w, ln_b):
    b, s, _ = p.shape
    R = RWKV_WIDTH
    r = p[..., :R]
    k = p[..., R:2 * R]
    v = p[..., 2 * R:3 * R]
    o1 = 3 * R
    wl = p[..., o1:o1 + DECAY_RANK]
    al = p[..., o1 + DECAY_RANK:o1 + DECAY_RANK + ICLR_RANK]
    gl = p[..., o1 + DECAY_RANK + ICLR_RANK:]
    w_log = -jax.nn.softplus(-(w0 + jnp.tanh(wl) @ w2)) - 0.5
    decay = jnp.exp(-jnp.exp(w_log.astype(F32)))
    a = jax.nn.sigmoid(a0 + al @ a2)
    g = jax.nn.sigmoid(gl) @ g2

    def heads(t):
        return t.astype(F32).reshape(b, s, RWKV_HEADS, RWKV_HEAD_DIM)

    kk = heads(k * k_k)
    kk = kk / jnp.maximum(jnp.sqrt(jnp.sum(kk * kk, axis=-1, keepdims=True)), 1e-12)
    k_mod = k * (1.0 + (a - 1.0) * k_a)

    def time_major(t):
        return jnp.moveaxis(t, 1, 0)

    xs = (time_major(heads(r)), time_major(heads(decay)), time_major(heads(k_mod)),
          time_major(heads(v)), time_major(kk), time_major(heads(a)))

    def step(state, inp):
        r_t, w_t, k_t, v_t, kk_t, a_t = inp
        sa = jnp.einsum('bhvk,bhk->bhv', state, kk_t)
        state = (state * w_t[:, :, None, :]
                 - sa[..., None] * (kk_t * a_t)[:, :, None, :]
                 + v_t[..., None] * k_t[:, :, None, :])
        return state, jnp.einsum('bhvk,bhk->bhv', state, r_t)

    state0 = jnp.zeros((b, RWKV_HEADS, RWKV_HEAD_DIM, RWKV_HEAD_DIM), F32)
    _, y = lax.scan(step, state0, xs)
    y = jnp.moveaxis(y, 0, 1)
    mean = jnp.mean(y, axis=-1, keepdims=True)
    var = jnp.mean(jnp.square(y - mean), axis=-1, keepdims=True)
    yn = ((y - mean) * lax.rsqrt(var + RWKV_GN_EPS)).reshape(b, s, R) * ln_w + ln_b
    bonus = jnp.sum(heads(r) * heads(k_mod) * r_k.astype(F32), axis=-1, keepdims=True) * heads(v)
    return (yn + bonus.reshape(b, s, R)).astype(p.dtype) * g

def mixer_ab(h, w_in, conv_w, conv_b, ga_w, ga_b, gx_w, gx_b, a_param, mu,
             w0, w2, a0, a2, g2, k_k, k_a, r_k, ln_w, ln_b, w_out):
    z = h @ w_in
    L = LRU_WIDTH
    lru_x = z[..., :L]
    lru_gate = z[..., L:2 * L]
    shift_in = z[..., 2 * L:]
    xc = causal_dwconv(lru_x, conv_w) + conv_b
    y_a = rg_lru(xc, ga_w, ga_b, gx_w, gx_b, a_param) * jax.nn.gelu(lru_gate)
    p = shift_in + mu * (token_shift(shift_in) - shift_in)
    y_b = rwkv7_time_mix(p, w0, w2, a0, a2, g2, k_k, k_a, r_k, ln_w, ln_b)
    return jnp.concatenate([y_a, y_b], axis=-1) @ w_out

def gated_delta_rule_chunked(q, k, v, g, beta):
    b, s, nh, dk = q.shape
    dv = v.shape[-1]
    C = DN_CHUNK
    n = s // C

    def chunks(t):
        t = jnp.moveaxis(t.astype(F32), 2, 1)
        return t.reshape(t.shape[:2] + (n, C) + t.shape[3:])

    q, k, v, g, beta = chunks(q), chunks(k), chunks(v), chunks(g), chunks(beta)
    gc = jnp.cumsum(g, axis=-1)
    causal = jnp.tril(jnp.ones((C, C), bool))
    strict = jnp.tril(jnp.ones((C, C), bool), -1)
    decay = jnp.exp(jnp.where(causal, gc[..., :, None] - gc[..., None, :], -jnp.inf))
    kk = jnp.einsum('bhnid,bhnjd->bhnij', k, k)
    A = jnp.where(strict, beta[..., :, None] * kk * decay, 0.0)
    eye = jnp.eye(C, dtype=F32)
    rhs = jnp.concatenate([v * beta[..., None], k * (beta * jnp.exp(gc))[..., None]], axis=-1)
    sol = lax.linalg.triangular_solve(A + eye, rhs, left_side=True, lower=True, unit_diagonal=True)
    u = sol[..., :dv]
    w = sol[..., dv:]
    attn = jnp.einsum('bhnid,bhnjd->bhnij', q, k) * decay
    q_dec = q * jnp.exp(gc)[..., None]
    k_dec = k * jnp.exp(gc[..., -1:] - gc)[..., None]
    chunk_decay = jnp.exp(gc[..., -1])
    xs = tuple(jnp.moveaxis(t, 2, 0) for t in (u, w, q_dec, k_dec, attn, chunk_decay))

    def step(state, inp):
        u_c, w_c, qd_c, kd_c, at_c, cd_c = inp
        v_new = u_c - jnp.einsum('bhck,bhkv->bhcv', w_c, state)
        o = jnp.einsum('bhck,bhkv->bhcv', qd_c, state) + jnp.einsum('bhij,bhjv->bhiv', at_c, v_new)
        state = state * cd_c[..., None, None] + jnp.einsum('bhck,bhcv->bhkv', kd_c, v_new)
        return state, o

    _, o = lax.scan(step, jnp.zeros((b, nh, dk, dv), F32), xs)
    o = jnp.moveaxis(o, 0, 2).reshape(b, nh, s, dv)
    return jnp.moveaxis(o, 1, 2)

def l2norm(t, eps=1e-6):
    tf = t.astype(F32)
    return tf * lax.rsqrt(jnp.sum(tf * tf, axis=-1, keepdims=True) + eps)

def mixer_c(h, w_in, conv_w, A_log, dt_bias, norm_w, w_out):
    b, s, _ = h.shape
    W = DN_WIDTH
    z = h @ w_in
    qkv = jax.nn.silu(causal_dwconv(z[..., :3 * W], conv_w))
    gate = z[..., 3 * W:4 * W].reshape(b, s, DN_HEADS, DN_HEAD_DIM)
    beta = jax.nn.sigmoid(z[..., 4 * W:4 * W + DN_HEADS].astype(F32))
    alpha = z[..., 4 * W + DN_HEADS:].astype(F32)
    g = -jnp.exp(A_log.astype(F32)) * jax.nn.softplus(alpha + dt_bias.astype(F32))
    q = l2norm(qkv[..., :W].reshape(b, s, DN_HEADS, DN_HEAD_DIM)) * (DN_HEAD_DIM ** -0.5)
    k = l2norm(qkv[..., W:2 * W].reshape(b, s, DN_HEADS, DN_HEAD_DIM))
    v = qkv[..., 2 * W:].reshape(b, s, DN_HEADS, DN_HEAD_DIM)
    o = gated_delta_rule_chunked(q, k, v, g, beta)
    o = rmsnorm(o, norm_w) * jax.nn.silu(gate.astype(F32))
    return o.reshape(b, s, W).astype(h.dtype) @ w_out

def setup_inputs(seed: int = 0) -> dict:
    key = jax.random.key(seed)
    ks = iter(jax.random.split(key, 48))

    def nrm(shape, scale):
        return jax.random.normal(next(ks), shape, F32) * scale

    def unif(shape, lo, hi):
        return jax.random.uniform(next(ks), shape, F32, lo, hi)

    E, O, D = N_EVEN, N_ODD, D_MODEL
    a_pow = unif((E, LRU_WIDTH), 0.9, 0.999)
    a_base = a_pow ** (1.0 / LRU_C)
    dt = jnp.exp(unif((O, DN_HEADS), float(np.log(1e-3)), float(np.log(1e-1))))
    return {
        'x': nrm((BATCH, SEQ, D), 1.0),
        'ffn_norm': 1.0 + nrm((DEPTH, 2, D), 0.02),
        'ffn_w_gate': nrm((DEPTH, 2, D, D_FF), D ** -0.5),
        'ffn_w_up': nrm((DEPTH, 2, D, D_FF), D ** -0.5),
        'ffn_w_down': nrm((DEPTH, 2, D_FF, D), D_FF ** -0.5),
        'mix_norm': 1.0 + nrm((DEPTH, D), 0.02),
        'final_norm': 1.0 + nrm((D,), 0.02),
        'ab_w_in': nrm((E, D, AB_IN), D ** -0.5),
        'lru_conv_w': nrm((E, CONV_WIDTH, LRU_WIDTH), CONV_WIDTH ** -0.5),
        'lru_conv_b': nrm((E, LRU_WIDTH), 0.02),
        'lru_gate_a_w': nrm((E, LRU_BLOCKS, LRU_BLOCK, LRU_BLOCK), LRU_BLOCK ** -0.5),
        'lru_gate_a_b': nrm((E, LRU_WIDTH), 0.02),
        'lru_gate_x_w': nrm((E, LRU_BLOCKS, LRU_BLOCK, LRU_BLOCK), LRU_BLOCK ** -0.5),
        'lru_gate_x_b': nrm((E, LRU_WIDTH), 0.02),
        'lru_a_param': jnp.log(a_base) - jnp.log1p(-a_base),
        'rwkv_mu': unif((E, SHIFT_WIDTH), 0.0, 1.0),
        'rwkv_w0': unif((E, RWKV_WIDTH), -6.0, -1.0),
        'rwkv_w2': nrm((E, DECAY_RANK, RWKV_WIDTH), 0.1 * DECAY_RANK ** -0.5),
        'rwkv_a0': nrm((E, RWKV_WIDTH), 0.1),
        'rwkv_a2': nrm((E, ICLR_RANK, RWKV_WIDTH), ICLR_RANK ** -0.5),
        'rwkv_g2': nrm((E, GATE_RANK, RWKV_WIDTH), GATE_RANK ** -0.5),
        'rwkv_k_k': 0.85 + nrm((E, RWKV_WIDTH), 0.02),
        'rwkv_k_a': 1.0 + nrm((E, RWKV_WIDTH), 0.02),
        'rwkv_r_k': nrm((E, RWKV_HEADS, RWKV_HEAD_DIM), 0.1),
        'rwkv_ln_w': 1.0 + nrm((E, RWKV_WIDTH), 0.02),
        'rwkv_ln_b': nrm((E, RWKV_WIDTH), 0.02),
        'ab_w_out': nrm((E, AB_MIX, D), AB_MIX ** -0.5),
        'c_w_in': nrm((O, D, C_IN), D ** -0.5),
        'dn_conv_w': nrm((O, CONV_WIDTH, 3 * DN_WIDTH), CONV_WIDTH ** -0.5),
        'dn_A_log': jnp.log(unif((O, DN_HEADS), 1.0, 16.0)),
        'dn_dt_bias': dt + jnp.log(-jnp.expm1(-dt)),
        'dn_norm': 1.0 + nrm((O, DN_HEAD_DIM), 0.02),
        'c_w_out': nrm((O, DN_WIDTH, D), DN_WIDTH ** -0.5),
    }

def reference(x, ffn_norm, ffn_w_gate, ffn_w_up, ffn_w_down, mix_norm, final_norm,
              ab_w_in, lru_conv_w, lru_conv_b, lru_gate_a_w, lru_gate_a_b, lru_gate_x_w,
              lru_gate_x_b, lru_a_param, rwkv_mu, rwkv_w0, rwkv_w2, rwkv_a0, rwkv_a2,
              rwkv_g2, rwkv_k_k, rwkv_k_a, rwkv_r_k, rwkv_ln_w, rwkv_ln_b, ab_w_out,
              c_w_in, dn_conv_w, dn_A_log, dn_dt_bias, dn_norm, c_w_out):
    for l in range(DEPTH):
        i = l // 2
        x = x + 0.5 * swiglu(rmsnorm(x, ffn_norm[l, 0]), ffn_w_gate[l, 0], ffn_w_up[l, 0], ffn_w_down[l, 0])
        h = rmsnorm(x, mix_norm[l])
        if l % 2 == 0:
            x = x + mixer_ab(h, ab_w_in[i], lru_conv_w[i], lru_conv_b[i], lru_gate_a_w[i],
                             lru_gate_a_b[i], lru_gate_x_w[i], lru_gate_x_b[i], lru_a_param[i],
                             rwkv_mu[i], rwkv_w0[i], rwkv_w2[i], rwkv_a0[i], rwkv_a2[i],
                             rwkv_g2[i], rwkv_k_k[i], rwkv_k_a[i], rwkv_r_k[i], rwkv_ln_w[i],
                             rwkv_ln_b[i], ab_w_out[i])
        else:
            x = x + mixer_c(h, c_w_in[i], dn_conv_w[i], dn_A_log[i], dn_dt_bias[i], dn_norm[i], c_w_out[i])
        x = x + 0.5 * swiglu(rmsnorm(x, ffn_norm[l, 1]), ffn_w_gate[l, 1], ffn_w_up[l, 1], ffn_w_down[l, 1])
    return rmsnorm(x, final_norm)


_drawn_inputs = setup_inputs


def setup_inputs(seed=0):
    import zlib

    import numpy as np

    out = dict(_drawn_inputs(seed))
    spreads = {}
    factors = {'ffn_norm': 3.126,
     'final_norm': 8.993,
     'lru_gate_a_b': 64.0,
     'lru_gate_x_b': 64.0,
     'rwkv_w2': 8.0,
     'rwkv_a0': 3.888,
     'rwkv_k_k': 23.712,
     'rwkv_k_a': 6.165,
     'rwkv_ln_w': 17.071,
     'rwkv_ln_b': 18.062,
     'dn_norm': 33.212,
     'lru_conv_b': 3.229}
    for name, (base, spread) in spreads.items():
        noise = np.random.default_rng([zlib.crc32(name.encode()), seed]).standard_normal(out[name].shape)
        drawn = base * np.exp(spread * noise) if base else spread * noise
        out[name] = jnp.asarray(drawn.astype(out[name].dtype))
    for name, factor in factors.items():
        out[name] = (out[name] * factor).astype(out[name].dtype)
    return out
```

```python
from contextlib import ExitStack, contextmanager

import concourse.bass as bass
import numpy as np
from concourse import mybir

ALU = mybir.AluOpType
ACT = mybir.ActivationFunctionType
F32 = mybir.dt.float32
F32R = mybir.dt.float32r

P = 128
SEQ = 512
D_MODEL = 1024
D_FF = 2816
KB = D_MODEL // P
FB = D_FF // P
HALF_FB = FB // 2
C_READS = 33
AB_BLOCKS = 22
C_BLOCKS = 32
AB_ORDER = [*range(8), 20, 21, *range(12, 20), *range(8, 12)]
CHUNK = 64
NCHUNK = SEQ // CHUNK
TT = SEQ // P
HEADS = 8
RING = 4
SPLIT = 2
UNIT = HALF_FB * P
EPS = 1e-6
DECAY_C = float(np.exp(-0.5))

PARAMS = {}


def _param(name, n, _at=[0]):
    PARAMS[name] = (_at[0], n)
    _at[0] += n


for _name, _n in [
    ("ffn_norm", 4 * KB), ("mix_norm", 2 * KB), ("final_norm", KB),
    ("lru_conv_w", 16), ("lru_conv_b", 4), ("lru_gate_a_b", 4), ("lru_gate_x_b", 4), ("lru_a_param", 4),
    ("rwkv_mu", 14), ("rwkv_w0", 4), ("rwkv_a0", 4), ("rwkv_k_k", 4), ("rwkv_k_a", 4), ("rwkv_r_k", 4),
    ("rwkv_ln_w", 4), ("rwkv_ln_b", 4), ("dn_conv_w", 96), ("dn_norm", 1), ("dn_A_log", 8), ("dn_dt_bias", 8),
]:
    _param(_name, _n)
NPARAM = sum(n for _, n in PARAMS.values())

CONSTS = ["ident", "ones", "ones_half", "upper", "strict", "pair1", "pair2", "pair4", "pair8", "pair16", "pair32"]
NCONST = len(CONSTS) * P + SEQ


def constants():
    s, t = np.meshgrid(np.arange(P), np.arange(P), indexing="ij")
    same = s // CHUNK == t // CHUNK
    mats = [s == t, s == s, same, same & (s <= t), same & (s < t)]
    for m in (1, 2, 4, 8, 16, 32):
        mats.append((s // (2 * m) == t // (2 * m)) & (s // m % 2 == 0) & (t // m % 2 == 1))
    restart = np.broadcast_to((np.arange(SEQ) % CHUNK != 0)[None, :], (P, SEQ))
    return np.ascontiguousarray(np.concatenate([*mats, restart], axis=1).astype(np.float32))


class Steps:

    def __init__(self, eng, sem):
        self.eng, self.sem, self.base, self.n = eng, sem, 0, 0

    def inc(self, ins):
        ins.then_inc(self.sem, 1)
        self.n += 1

    def wait(self):
        self.eng.wait_ge(self.sem, self.base + self.n)

    def link(self, ins):
        self.inc(ins)
        self.wait()


def layout(inputs):
    v = {k: np.asarray(a) for k, a in inputs.items()}

    def cols(a):
        return a.reshape(-1, P).transpose(1, 0)

    def blocks(w):
        k, n = w.shape
        return np.ascontiguousarray(w.reshape(k // P, P, n // P, P).transpose(2, 1, 0, 3)).reshape(n // P, P, k)

    packed = {
        "ffn_norm": cols(v["ffn_norm"]), "mix_norm": cols(v["mix_norm"]), "final_norm": cols(v["final_norm"]),
        "lru_conv_w": cols(v["lru_conv_w"]), "lru_conv_b": cols(v["lru_conv_b"]),
        "lru_gate_a_b": cols(v["lru_gate_a_b"]), "lru_gate_x_b": cols(v["lru_gate_x_b"]),
        "lru_a_param": cols(v["lru_a_param"]), "rwkv_mu": cols(v["rwkv_mu"]), "rwkv_w0": cols(v["rwkv_w0"]),
        "rwkv_a0": cols(v["rwkv_a0"]), "rwkv_k_k": cols(v["rwkv_k_k"]), "rwkv_k_a": cols(v["rwkv_k_a"]),
        "rwkv_r_k": cols(v["rwkv_r_k"]), "rwkv_ln_w": cols(v["rwkv_ln_w"]), "rwkv_ln_b": cols(v["rwkv_ln_b"]),
        "dn_conv_w": cols(v["dn_conv_w"]), "dn_norm": cols(v["dn_norm"]),
        "dn_A_log": np.broadcast_to(v["dn_A_log"], (P, HEADS)),
        "dn_dt_bias": np.broadcast_to(v["dn_dt_bias"], (P, HEADS)),
    }
    params = np.empty((P, NPARAM), np.float32)
    for name, (c, n) in PARAMS.items():
        params[:, c:c + n] = packed[name]
    gate, up = (np.stack([blocks(w) for w in v[k].reshape(4, D_MODEL, D_FF)]) for k in ("ffn_w_gate", "ffn_w_up"))
    down = np.stack([blocks(w) for w in v["ffn_w_down"].reshape(4, D_FF, D_MODEL)])
    lru_a, lru_x = (np.ascontiguousarray(v[k][0].reshape(4, 2, 64, 64).transpose(1, 2, 0, 3))
                    for k in ("lru_gate_a_w", "lru_gate_x_w"))
    c_w = v["c_w_in"][0]
    return {
        "x": np.ascontiguousarray(v["x"][0].reshape(SEQ, KB, P).transpose(2, 1, 0)),
        "params": params, "const": constants(),
        "w_gate": gate, "w_up": up, "w_down": down,
        "ab_in": blocks(v["ab_w_in"][0])[AB_ORDER], "ab_out": blocks(v["ab_w_out"][0]),
        "lru_a": lru_a, "lru_x": lru_x,
        "rwkv_wa": np.concatenate([v["rwkv_w2"][0], v["rwkv_a2"][0]], axis=0), "rwkv_g": v["rwkv_g2"][0],
        "c_in": blocks(c_w[:, :C_BLOCKS * P]),
        "c_tail": np.ascontiguousarray(c_w[:, C_BLOCKS * P:].reshape(KB, P, 2 * HEADS).transpose(1, 0, 2)),
        "c_out": blocks(v["c_w_out"][0]),
    }


def hybrid_trunk_kernel(nc, x, params, const, w_gate, w_up, w_down, ab_in, ab_out, lru_a, lru_x,
                        rwkv_wa, rwkv_g, c_in, c_tail, c_out, out, plan=("ffn0", "ab", "ffn1", "ffn2", "c", "ffn3")):
    units, base = [], {}
    for phase in plan:
        base[phase] = len(units)
        if phase.startswith("ffn"):
            n = int(phase[3])
            for f in range(FB):
                units += [(w_gate[n, f], KB * P), (w_up[n, f], KB * P)]
            for m in range(KB):
                units += [(w_down[n, m, :, h * UNIT:(h + 1) * UNIT], UNIT) for h in range(2)]
        else:
            first, last, count = (ab_in, ab_out, AB_BLOCKS) if phase == "ab" else (c_in, c_out, C_BLOCKS)
            units += [(first[b], KB * P) for b in range(count)]
            units += [(last[m], KB * P) for m in range(KB)]
    n_units = len(units)
    norm_of = {phase: n for n, phase in enumerate(plan)}
    n_norms = len(plan) + 1
    norm_cols = []
    for phase in plan:
        if phase.startswith("ffn"):
            norm_cols.append(PARAMS["ffn_norm"][0] + int(phase[3]) * KB)
        else:
            norm_cols.append(PARAMS["mix_norm"][0] + (0 if phase == "ab" else KB))
    norm_cols.append(PARAMS["final_norm"][0])
    ffn_index = {phase: n for n, phase in enumerate(q for q in plan if q.startswith("ffn"))}

    with ExitStack() as ctx:
        arena_words = 53180
        ctx.enter_context(nc.sbuf_tensor("arena", [P, arena_words], F32))
        arena_at = nc.sbuf_base - 4 * arena_words

        def at(name, offset, shape, dtype=F32):
            words = int(np.prod(shape[1:]))
            assert offset + words <= arena_words, name
            return nc.alloc_sbuf_tensor_at(name, list(shape), dtype, offset=arena_at + 4 * offset)

        Q = 4 * SEQ
        X_AT = 0
        H_AT = X_AT + KB * SEQ
        ACT_AT = H_AT + 2 * KB * SEQ
        RAW_AT = ACT_AT + 2 * FB * SEQ
        WS_AT = RAW_AT + RING * UNIT
        TMP_AT = WS_AT + 2 * SPLIT * UNIT
        RSTD_AT = TMP_AT + 4 * SEQ
        ACC_AT = RSTD_AT + SEQ
        CONST_AT = ACC_AT + SEQ
        PARAM_AT = CONST_AT + NCONST

        X = at("X", X_AT, [P, KB, SEQ])
        H = at("H", H_AT, [P, 2, KB, SEQ], F32R)
        H_PARTS = (H[:, 0], H[:, 1])
        HF = at("HF", H_AT, [P, KB, SEQ])
        A = at("A", ACT_AT, [P, 2, FB, SEQ], F32R)
        RAW = at("RAW", RAW_AT, [P, RING, UNIT])
        WS = at("WS", WS_AT, [P, 2, SPLIT, UNIT], F32R)
        GS = at("GS", TMP_AT, [P, 2, SEQ])
        US = at("US", TMP_AT + 2 * SEQ, [P, 2, SEQ])
        RSTD = at("RSTD", RSTD_AT, [P, SEQ])
        ACC = at("ACC", ACC_AT, [P, SEQ])
        CST = at("CST", CONST_AT, [P, NCONST])
        PRM = at("PRM", PARAM_AT, [P, NPARAM])

        def con(name):
            i = CONSTS.index(name) * P
            return CST[:, i:i + P]

        def par(name, i=0):
            c = PARAMS[name][0] + i
            return PRM[:, c:c + 1]

        BANK = [ctx.enter_context(nc.psum_tensor(f"bank{i}", [P, SEQ], F32)) for i in range(8)]
        GATE, UP, DOWN, SQ = BANK[0:2], BANK[2:4], BANK[4:6], BANK[6]

        def sem(name):
            return ctx.enter_context(nc.semaphore(name))

        landed = sem("params_landed")
        w_landed = [sem(f"weights_landed{s}") for s in range(RING)]
        hi_ready = sem("weights_hi_ready")
        lo_ready = sem("weights_lo_ready")
        unit_done = sem("unit_done")


        def pair_of(name):
            return [sem(f"{name}{b}") for b in range(2)]

        gs_ready, us_ready, silu_ready = pair_of("gs_ready"), pair_of("us_ready"), pair_of("silu_ready")
        prod_ready, ahi_ready, act_ready = pair_of("prod_ready"), pair_of("ahi_ready"), pair_of("act_ready")
        x_ready, sq_ready, acc_ready = pair_of("x_ready"), pair_of("sq_ready"), pair_of("acc_ready")
        hw_ready, hhi_ready, h_ready = pair_of("hw_ready"), pair_of("hhi_ready"), pair_of("h_ready")
        sum_ready, rms_ready, rstd_ready = sem("sum_ready"), sem("rms_ready"), sem("rstd_ready")
        acc_clear = sem("acc_clear")
        out_ready, stored = sem("out_ready"), sem("stored")
        vec_step, act_step = sem("vec_step"), sem("act_step")

        block = ctx.enter_context(nc.Block())

        def fits(value):
            return not isinstance(value, int) or value > 0


        def quad(name, at_word):
            return at(name, at_word, [P, 4, SEQ])

        XC, GG = quad("XC", ACT_AT), quad("GG", ACT_AT + Q)
        RG, IG = quad("RG", ACT_AT + 2 * Q), quad("IG", ACT_AT + 3 * Q)
        LA, LU = quad("LA", ACT_AT + 4 * Q), quad("LU", ACT_AT + 5 * Q)
        SIG, AL = quad("SIG", ACT_AT), quad("AL", ACT_AT + 2 * Q)
        CUM, CPRE = quad("CUM", ACT_AT + 3 * Q), quad("CPRE", ACT_AT + 4 * Q)
        PINV = quad("PINV", ACT_AT + 5 * Q)
        LOW = at("LOW", ACT_AT + 7 * Q, [P, 2, SEQ])
        LW = at("LW", ACT_AT + 7 * Q + 2 * SEQ, [P, 2, 4, P])
        WA2 = at("WA2", ACT_AT + 6 * Q, [P, SEQ])
        KF, VF, RF = quad("KF", ACT_AT + 8 * Q), quad("VF", ACT_AT + 9 * Q), quad("RF", ACT_AT + 10 * Q)
        BV, YI = quad("BV", H_AT + Q), quad("YI", H_AT + 3 * Q)
        KH = quad("KH", ACT_AT)
        KT, BT, VT, GT = (quad("KT", ACT_AT + 3 * Q), quad("BT", ACT_AT), quad("VT", ACT_AT + Q),
                          quad("GT", ACT_AT + 6 * Q))
        XTL, XTH = quad("XTL", ACT_AT + 5 * Q), quad("XTH", ACT_AT + 9 * Q)
        MBT = at("MBT", WS_AT, [P, HEADS, SEQ])
        SH = at("SH", ACT_AT + 2 * Q, [P, NCHUNK, 4, CHUNK])
        YF, DF = quad("YF", ACT_AT + 3 * Q), quad("DF", ACT_AT + 9 * Q)
        YA = quad("YA", H_AT)
        MIX_HI = at("MIX_HI", ACT_AT, [P, KB, SEQ], F32R)
        MIX_LO = at("MIX_LO", ACT_AT + 4 * Q, [P, KB, SEQ], F32R)
        INV = [{k: at(f"{k}{b}", RAW_AT + (5 * b + n) * SEQ, [P, TT, P]) for n, k in enumerate(("TT", "TM", "XX", "XT", "IU"))}
               for b in range(2)]
        TKM = [at(f"TKM{b}", TMP_AT + b * SEQ, [P, TT, P]) for b in range(2)]
        MKM = [at(f"MKM{b}", TMP_AT + (2 + b) * SEQ, [P, TT, P]) for b in range(2)]
        TMPQ = quad("TMPQ", TMP_AT)
        PAD = at("PAD", TMP_AT, [P, 2, 516])
        DIFF = at("DIFF", TMP_AT + 2 * 516, [P, SEQ])
        SPARE_AT = (PARAM_AT + NPARAM + 7) // 8 * 8
        G2 = at("G2", SPARE_AT, [P, SEQ])
        SMALL = at("SMALL", SPARE_AT + SEQ, [P, 16, 4])
        PEND = at("PEND", SPARE_AT + SEQ + 64, [P, 4, NCHUNK])
        SDEC = at("SDEC", SPARE_AT + SEQ + 96, [P, 4, CHUNK])
        LRU_SCALE = SMALL[:, 15, :]
        LRU_NSCALE = SMALL[:, 14, :]

        z_read = sem("z_read")
        small_weights, pad_zero = sem("small_weights"), sem("pad_zero")
        sp_act, sp_vec = sem("sp_act"), sem("sp_vec")
        conv_ready, silu_done, gate_mm, gate_read = sem("conv_ready"), sem("silu_done"), sem("gate_mm"), sem("gate_read")
        lru_sq, lru_u2, lru_root, ya_ready, ya_hi, ya_lo, ya_kept = (sem("lru_sq"), sem("lru_u2"), sem("lru_root"),
                                                            sem("ya_ready"), sem("ya_hi"), sem("ya_lo"), sem("ya_kept"))
        p_ready, low_ready, small_mm, low_read = sem("p_ready"), sem("low_ready"), sem("small_mm"), sem("low_read")
        cum_ready, exp_ready, kk_raw, kk_sq = sem("cum_ready"), sem("exp_ready"), sem("kk_raw"), sem("kk_sq")
        norm_sum_mm, ss_max, inv_norm_ready, bon_in, bon_mm = sem("norm_sum_mm"), sem("ss_max"), sem("inv_norm_ready"), sem("bon_in"), sem("bon_mm")
        bv_ready, fm_ready, tr_mm, tr_read = sem("bv_ready"), sem("fm_ready"), sem("tr_mm"), sem("tr_read")
        mat_mm, mat_ready, xt1_ready = pair_of("mat_mm"), pair_of("mat_ready"), pair_of("xt1_ready")
        x1_mm, x1_read, token_mm, token_read = pair_of("x1_mm"), pair_of("x1_read"), pair_of("token_mm"), pair_of("token_read")
        tm_ready, u_mm, iu_ready, xx_mm, xx_read = (pair_of("tm_ready"), pair_of("u_mm"), pair_of("iu_ready"),
                                                    pair_of("xx_mm"), pair_of("xx_read"))
        predict_mm, predict_added, solve_mm, solve_read, state_mm, state_ready = (sem("predict_mm"), sem("predict_added"), sem("solve_mm"), sem("solve_read"),
                                                    sem("state_mm"), sem("state_ready"))
        out_mm, out_read, mean_mm, dev_ready, out_sq_ready, out_sq_mm, decay_ready, g_mm, mixed_ready, mixed_hi, mixed_lo = (
            sem(k) for k in ("out_mm", "out_read", "mean_mm", "dev_ready", "out_sq_ready", "out_sq_mm", "decay_ready", "g_mm",
                             "mixed_ready", "mixed_hi", "mixed_lo"))
        pool_step = sem("pool_step")
        mixer_done = {"ab": sem("ab_core_done"), "c": sem("c_core_done")}

        def xt_of(h):
            return (XTL, XTH)[h // 4][:, h % 4, :].rearrange("p (t c) -> p t c", t=TT)

        QC, KC = at("QC", ACT_AT, [P, HEADS, SEQ]), at("KC", ACT_AT + 2 * Q, [P, HEADS, SEQ])
        VC, GC_ = at("VC", ACT_AT + 4 * Q, [P, HEADS, SEQ]), at("GATEC", ACT_AT + 6 * Q, [P, HEADS, SEQ])
        SQT = at("SQT", ACT_AT + 8 * Q, [P, 2, 2, SEQ])
        ATT = at("ATT", ACT_AT + 8 * Q, [P, HEADS, TT, P])
        DT, DS = at("DT", ACT_AT + 10 * Q, [P, 2, TT, P]), at("DS", ACT_AT + 10 * Q + 2 * SEQ, [P, 2, TT, P])
        KBETA, EROW = at("KBETA", TMP_AT, [P, 2, SEQ]), at("EROW", TMP_AT + 2 * SEQ, [P, 2, SEQ])
        XTC, KDT = at("XTC", H_AT, [P, HEADS, TT, P]), at("KDT", H_AT + 2 * Q, [P, HEADS, TT, P])
        VTK = at("VTK", WS_AT, [P, HEADS, TT, P])
        SC = at("SC", ACT_AT + 4 * Q, [P, 2, HEADS, P])
        CT = at("CT", SPARE_AT, [P, KB, 2 * HEADS])
        CTS = at("CTS", SPARE_AT + P, [P, 2, KB, 2 * HEADS], F32R)
        TL = at("TL", SPARE_AT + 3 * P, [P, 20, TT, HEADS])
        CD = at("CD", SPARE_AT + 3 * P + 640, [P, HEADS, NCHUNK])
        RTOK = at("RTOK", SPARE_AT + 3 * P + 704, [P, 8])
        BETA, GSUM, KDEC = TL[:, 0], TL[:, 1], TL[:, 2]

        c_tail_hi, c_tail_lo, sq_c, l2_done, gate_c = (sem(k) for k in (
            "c_tail_hi", "c_tail_lo", "sq_c", "l2_done", "gate_c"))
        tail_scaled, beta_ready, al_act, al_vec, gcum_mm, gtok_ready, kdec_ready, orn_ready = (sem(k) for k in (
            "tail_scaled", "beta_ready", "al_act", "al_vec", "gcum_mm", "gtok_ready", "kdec_ready", "orn_ready"))
        row_mm, kbeta_ready, dd_ready, erow_ready, dexp_ready, dmask_ready = (pair_of(k) for k in (
            "row_mm", "kbeta_ready", "dd_ready", "erow_ready", "dexp_ready", "dmask_ready"))
        kq_mm, att_ready, qk_scaled = (pair_of(k) for k in ("kq_mm", "att_ready", "qk_scaled"))
        inv_base = {"ab": 0, "c": HEADS // 2 if "ab" in plan else 0}
        mat_base = 4 * inv_base["c"]
        used = {k: v if "ab" in plan else 0 for k, v in (
            ("conv_ready", 4), ("silu_done", 4), ("norm_sum_mm", 4), ("inv_norm_ready", 1), ("small_mm", 8), ("decay_ready", 1), ("predict_mm", 14), ("predict_added", 14), ("solve_mm", 8), ("solve_read", 8), ("state_mm", 7), ("state_ready", 7), ("out_mm", 4), ("out_read", 4), ("out_sq_mm", 4), ("out_sq_ready", 4), ("mixed_ready", 4), ("mixed_hi", 4), ("mixed_lo", 4), ("token_mm", 8), ("token_read", 8), ("pad_zero", 2), ("small_weights", 96), ("z_read", 22))}

        def tiles(ap):
            return ap.unsqueeze(1).to_broadcast([P, TT, P])

        def flat(t):
            return t[:, :, :].rearrange("p a b -> p (a b)")

        def last_use(eng, phase):
            if phase.startswith("ffn"):
                for j in range(2):
                    eng.wait_ge(us_ready[j], (ffn_index[phase] + 1) * (FB // 2))
            else:
                eng.wait_ge(z_read, AB_BLOCKS if phase == "ab" else used["z_read"] + C_READS)

        @block.sync
        def _(sp):
            def load(u, slot, src, cols):
                if fits(u - RING + 1):
                    sp.wait_ge(lo_ready, u - RING + 1)
                sp.dma_start(RAW[:, slot, 0:cols], src).then_inc(w_landed[slot], 16)

            sp.dma_start(X[:, :, :], x).then_inc(landed, 16)
            sp.dma_start(PRM[:, :], params).then_inc(landed, 16)
            sp.dma_start(CST[:, :], const).then_inc(landed, 16)
            for phase in plan:
                u0 = base[phase]
                if phase.startswith("ffn"):
                    n = int(phase[3])
                    for j in range(4):
                        load(u0 + j, (u0 + j) % RING, *units[u0 + j])
                    with sp.Fori(1, FB // 2) as i:
                        for j in range(4):
                            src = (w_gate, w_up)[j % 2][n, 2 * i + j // 2]
                            load(u0 + 4 * i + j, (u0 + j) % RING, src, KB * P)
                    u1 = u0 + 2 * FB
                    with sp.Fori(0, KB // 2) as i:
                        for j in range(4):
                            src = w_down[n, 2 * i + j // 2, :, (j % 2) * UNIT:(j % 2 + 1) * UNIT]
                            load(u1 + 4 * i + j, (u1 + j) % RING, src, UNIT)
                else:
                    count = AB_BLOCKS if phase == "ab" else C_BLOCKS
                    for j in range(count + KB):
                        if phase == "ab" and j == RING:
                            sp.wait_ge(unit_done, u0)
                            for half in range(2):
                                rows = slice(half * CHUNK, (half + 1) * CHUNK)
                                sp.wait_ge(pad_zero, 1)
                                for k, w in enumerate((lru_a, lru_x)):
                                    sp.dma_start(LW[rows, k, :, rows], w[half]).then_inc(small_weights, 16)
                            sp.dma_start(WA2[:, :], rwkv_wa).then_inc(small_weights, 16)
                            sp.dma_start(G2[:, :], rwkv_g).then_inc(small_weights, 16)
                        if phase == "c" and j == RING:
                            sp.wait_ge(unit_done, u0)
                            sp.dma_start(CT[:, :, :], c_tail).then_inc(small_weights, 16)

                        if j == count:
                            sp.wait_ge(mixer_done[phase], 1)
                        load(u0 + j, (u0 + j) % RING, *units[u0 + j])
            for m in range(KB):
                sp.wait_ge(out_ready, m + 1)
                sp.dma_start(out[m], HF[:, m, :]).then_inc(stored, 16)
            sp.wait_ge(stored, 16 * KB)


        @block.tensor
        def _(pe):
            def unit(bank, c, i, src, rows, first, last, norm=None):
                s = c % SPLIT
                pe.wait_ge(lo_ready, c + 4 * i + 1)
                for j, r in enumerate(rows):
                    cols = slice(j * P, (j + 1) * P)
                    if norm is not None:
                        pe.wait_ge(h_ready[r % 2], KB // 2 * norm + r // 2 + 1)
                    pe.matmul(bank[:, :], WS[:, 0, s, cols], src[0][:, r, :], start=first and j == 0, stop=False)
                    pe.matmul(bank[:, :], WS[:, 0, s, cols], src[1][:, r, :], start=False, stop=False)
                    mm = pe.matmul(bank[:, :], WS[:, 1, s, cols], src[0][:, r, :],
                                   start=False, stop=last and j == len(rows) - 1)
                mm.then_inc(unit_done, 1)

            def norm_sum(n):
                pe.wait_ge(acc_ready[0], 4 * (n + 1))
                pe.wait_ge(acc_ready[1], 3 * (n + 1))
                pe.wait_ge(sq_ready[1], 4 * (n + 1))
                if n:
                    pe.wait_ge(rms_ready, n)
                pe.matmul(SQ[:, :], con("ones"), ACC[:, :], start=True, stop=False)
                pe.matmul(SQ[:, :], con("ones"), US[:, 1, :], start=False, stop=True).then_inc(sum_ready, 1)

            def ffn_up(phase, i, j, with_sum=False):
                q = ffn_index[phase] * (FB // 2)
                c = base[phase] + 2 * j
                if fits(q + i):
                    pe.wait_ge(gs_ready[j], q + i)
                unit(GATE[j], c, i, H_PARTS, range(KB), True, True, norm=norm_of[phase])
                if with_sum:
                    norm_sum(norm_of[phase])
                if fits(q + i):
                    pe.wait_ge(us_ready[j], q + i)
                unit(UP[j], c + 1, i, H_PARTS, range(KB), True, True)

            def ffn_down(phase, i, j):
                c = base[phase] + 2 * FB + 2 * j
                pe.wait_ge(x_ready[j], KB // 2 * (norm_of[phase] + 1) + i)
                for k in range(2):
                    unit(DOWN[j], c + k, i, (A[:, 0], A[:, 1]), range(k * HALF_FB, (k + 1) * HALF_FB), k == 0, k == 1)


            def pe_first_inverse(q):
                for s in range(2):
                    pe.wait_ge(xt1_ready[s], q + 1)
                    for j in range(TT):
                        tr = pe.transpose(BANK[4 * s][:, j * P:(j + 1) * P], INV[s]["XT"][:, j, :], con("ident"))
                    tr.then_inc(x1_mm[s], 1)

            def pe_inverse_level(q, l, masked, gy=0):
                for s in range(2):
                    pe.wait_ge(tm_ready[s], 5 * q + l + 1)
                    if l == 0:
                        pe.wait_ge(x1_read[s], q + 1)
                        pe.wait_ge(mat_ready[s], masked)
                    else:
                        pe.wait_ge(xx_read[s], 9 * q + 2 * l)
                    for j in range(TT):
                        mm = pe.matmul(BANK[4 * s + 3][:, j * P:(j + 1) * P], INV[s]["TM"][:, j, :], INV[s]["XX"][:, j, :],
                                       start=True, stop=True)
                    mm.then_inc(u_mm[s], 1)
                for s in range(2):
                    pe.wait_ge(iu_ready[s], 5 * q + l + 1)
                    if l == 0 and gy:
                        pe.wait_ge(token_read[s], gy)
                    if l < 4:
                        for j in range(TT):
                            mm = pe.matmul(BANK[4 * s][:, j * P:(j + 1) * P], INV[s]["XT"][:, j, :], INV[s]["IU"][:, j, :],
                                           start=True, stop=True)
                        mm.then_inc(xx_mm[s], 1)
                    for j in range(TT):
                        mm = pe.matmul(BANK[4 * s + 1][:, j * P:(j + 1) * P], INV[s]["IU"][:, j, :], INV[s]["XT"][:, j, :],
                                       start=True, stop=True)
                    mm.then_inc(xx_mm[s], 1)

            def mix_out(phase):
                count = AB_BLOCKS if phase == "ab" else C_BLOCKS
                for m in range(KB):
                    if m == 0:
                        pe.wait_ge(mixer_done[phase], 1)
                    pe.wait_ge(x_ready[m % 2], KB // 2 * (norm_of[phase] + 1) + m // 2)
                    unit(DOWN[m % 2], base[phase] + count + m, 0, (MIX_HI, MIX_LO), range(KB), True, True)

            pe.wait_ge(landed, 48)
            for phase in plan:
                if phase.startswith("ffn"):
                    ffn_up(phase, 0, 0, with_sum=True)
                    ffn_up(phase, 0, 1)
                    with pe.Fori(1, FB // 2) as i:
                        for j in range(2):
                            ffn_up(phase, i, j)
                    for j in range(2):
                        pe.wait_ge(act_ready[j], (ffn_index[phase] + 1) * (FB // 2))
                    with pe.Fori(0, KB // 2) as i:
                        for j in range(2):
                            ffn_down(phase, i, j)

                if phase == "ab":
                    n, u0 = norm_of[phase], base[phase]
                    for t in range(AB_BLOCKS):
                        if t >= 2:
                            pe.wait_ge(z_read, t - 1)
                        unit(BANK[t % 2], u0 + t, 0, H_PARTS, range(KB), True, True, norm=n if t == 0 else None)
                        if t == 0:
                            norm_sum(n)
                        if t in (8, 10):
                            k = (t - 8) // 2
                            pe.wait_ge(conv_ready, 4)
                            pe.wait_ge(small_weights, 16 * 6)
                            if k:
                                pe.wait_ge(gate_read, 4)
                            for b in range(4):
                                pe.matmul(BANK[2 + b][:, :], LW[:, k, b, :], XC[:, b, :],
                                          start=True, stop=True).then_inc(gate_mm, 1)
                    pe.wait_ge(low_ready, 1)
                    for k in range(2):
                        rows = slice(k * CHUNK, (k + 1) * CHUNK)
                        for b in range(4):
                            pe.wait_ge(gate_read if k == 0 else low_read, 8 if k == 0 else b + 1)
                            pe.matmul(BANK[2 + b][:, :], WA2[rows, b * P:(b + 1) * P], LOW[rows, 0, :],
                                      start=True, stop=True).then_inc(small_mm, 1)
                    for b in range(4):
                        pe.wait_ge(low_read, 5 + b)
                        pe.wait_ge(kk_sq, 1)
                        pe.matmul(BANK[2 + b][:, :], con("ones_half"), TMPQ[:, b, :], start=True, stop=True).then_inc(norm_sum_mm, 1)
                    for b in range(4):
                        pe.wait_ge(ss_max, b + 1)
                        pe.wait_ge(bon_in, b + 1)
                        pe.matmul(BANK[2 + b][:, :], con("ones_half"), TMPQ[:, b, :], start=True, stop=True).then_inc(bon_mm, 1)
                    for k, (src, need) in enumerate(((KH, 5), (PINV, 6), (VF, 6))):
                        pe.wait_ge(fm_ready, need)
                        for j in range(TT):
                            if 4 * k + j >= 2:
                                pe.wait_ge(tr_read, 4 * k + j - 1)
                            else:
                                pe.wait_ge(z_read, AB_BLOCKS)
                            bank = BANK[(4 * k + j) % 2]
                            for b in range(4):
                                tr = pe.transpose(bank[:, b * P:(b + 1) * P], src[:, b, j * P:(j + 1) * P], con("ident"))
                            tr.then_inc(tr_mm, 1)
                    pe.wait_ge(tr_read, 12)
                    pe.wait_ge(bv_ready, 4)

                    def matrices(h):
                        s, rows, b = h % 2, slice(h % 2 * CHUNK, (h % 2 + 1) * CHUNK), h // 2
                        if b:
                            pe.wait_ge(xx_read[s], 9 * b)
                            pe.wait_ge(token_read[s], 2 * b)
                        for k, (left, right) in enumerate(((AL, CPRE), (KF, CPRE), (KF, RF), (AL, RF))):
                            for j in range(TT):
                                c = slice(j * P, (j + 1) * P)
                                mm = pe.matmul(BANK[4 * s + k][:, c], left[rows, b, c], right[rows, b, c],
                                               start=True, stop=True)
                            mm.then_inc(mat_mm[s], 1)

                    def inside(h):
                        s, rows, b, w = h % 2, slice(h % 2 * CHUNK, (h % 2 + 1) * CHUNK), h // 2, slice(h * CHUNK, (h + 1) * CHUNK)
                        pe.wait_ge(mat_ready[s], 4 * b + 3)
                        for j in range(TT):
                            mm = pe.matmul(BANK[4 * s + 1][:, j * CHUNK:(j + 1) * CHUNK], TKM[s][:, j, :], VT[:, j, w],
                                           start=True, stop=True)
                        mm.then_inc(token_mm[s], 1)
                        for j in range(TT):
                            mm = pe.matmul(BANK[4 * s + 2][rows, j * P:(j + 1) * P], VT[:, j, w], MKM[s][:, j, :],
                                           start=True, stop=True)
                        mm.then_inc(token_mm[s], 1)

                    for p in range(HEADS // 2):
                        for s in range(2):
                            matrices(2 * p + s)
                        for s in range(2):
                            inside(2 * p + s)
                        pe_first_inverse(p)
                        for l in range(5):
                            pe_inverse_level(p, l, 4 * (p + 1), 2 * (p + 1))

                    for c in range(NCHUNK):
                        j, th = c // 2, slice(c % 2 * CHUNK, (c % 2 + 1) * CHUNK)
                        cc = slice(c * CHUNK, (c + 1) * CHUNK)
                        if c == 0:
                            for s in range(2):
                                pe.wait_ge(xx_read[s], 36)
                                pe.wait_ge(token_read[s], 8)
                        else:
                            pe.wait_ge(state_ready, c)
                            for s in range(2):
                                rows = slice(s * CHUNK, (s + 1) * CHUNK)
                                for b in range(4):
                                    mm = pe.matmul(BANK[s][th, b * CHUNK:(b + 1) * CHUNK], CPRE[rows, b, cc],
                                                   SH[rows, c, b, :], start=True, stop=True)
                                mm.then_inc(predict_mm, 1)
                        if c:
                            pe.wait_ge(predict_added, 2 * c)
                        for h in range(HEADS):
                            w = slice(h * CHUNK, (h + 1) * CHUNK)
                            mm = pe.matmul(BANK[2][th, w], xt_of(h)[th, j, th], GT[th, j, w], start=True, stop=True)
                        mm.then_inc(solve_mm, 1)
                        pe.wait_ge(solve_read, c + 1)
                        if c < NCHUNK - 1:
                            for h in range(HEADS):
                                w = slice(h * CHUNK, (h + 1) * CHUNK)
                                out_ = BANK[3][h % 2 * CHUNK:(h % 2 + 1) * CHUNK, h // 2 * CHUNK:(h // 2 + 1) * CHUNK]
                                pe.matmul(out_, KT[th, j, w], VT[th, j, w], start=True, stop=False)
                                mm = pe.matmul(out_, BT[th, j, w], GT[th, j, w], start=False, stop=True)
                            mm.then_inc(state_mm, 1)
                    for b in range(4):
                        for s in range(2):
                            h, rows, w = 2 * b + s, slice(s * CHUNK, (s + 1) * CHUNK), slice((2 * b + s) * CHUNK, (2 * b + s + 1) * CHUNK)
                            for j in range(TT):
                                mm = pe.matmul(BANK[4 + b][rows, j * P:(j + 1) * P], GT[:, j, w],
                                               MBT[:, h, j * P:(j + 1) * P], start=True, stop=False, skip_group_check=True)
                                for c in (2 * j, 2 * j + 1):
                                    if c:
                                        cc = slice(c * CHUNK, (c + 1) * CHUNK)
                                        mm = pe.matmul(BANK[4 + b][rows, cc], SH[rows, c, b, :], RF[rows, b, cc],
                                                       start=False, stop=c % 2 == 1, skip_group_check=True)
                        mm.then_inc(out_mm, 1)
                    pe.wait_ge(low_ready, 2)
                    for b in range(4):
                        pe.wait_ge(out_read, b + 1)
                        pe.matmul(BANK[b][:, :], con("ones_half"), YF[:, b, :], start=True, stop=True).then_inc(mean_mm, 1)
                    for b in range(4):
                        pe.wait_ge(out_sq_ready, b + 1)
                        pe.wait_ge(dev_ready, b + 1)
                        pe.matmul(BANK[4 + b][:, :], con("ones_half"), TMPQ[:, b, :], start=True, stop=True).then_inc(out_sq_mm, 1)
                    for b in range(4):
                        pe.matmul(BANK[b][:, :], G2[:, b * P:(b + 1) * P], LOW[:, 1, :], start=True, stop=True).then_inc(g_mm, 1)
                    mix_out(phase)
                if phase == "c":
                    n, u0, q0 = norm_of[phase], base[phase], inv_base[phase]
                    for t in range(C_BLOCKS):
                        if t >= 2:
                            pe.wait_ge(z_read, used["z_read"] + t - 1)
                        unit(BANK[t % 2], u0 + t, 0, H_PARTS, range(KB), True, True, norm=n if t == 0 else None)
                        if t == 0:
                            norm_sum(n)
                        if t >= 24:
                            for k in range(2):
                                if t >= 26:
                                    pe.wait_ge(inv_norm_ready, used["inv_norm_ready"] + 2 * (t - 26) + k + 1)
                                pe.wait_ge(sq_c, 2 * (t - 24) + k + 1)
                                pe.matmul(BANK[2 + 2 * (t % 2) + k][:, :], con("ones"), SQT[:, t % 2, k, :],
                                          start=True, stop=True).then_inc(norm_sum_mm, 1)
                    pe.wait_ge(c_tail_lo, 1)
                    for j in range(TT):
                        c, o = slice(j * P, (j + 1) * P), slice(j * 16, (j + 1) * 16)
                        for k in range(KB):
                            for a, b in ((0, 0), (1, 0), (0, 1)):
                                pe.matmul(BANK[7][:, o], H[:, a, k, c], CTS[:, b, k, :], start=k == 0 and a == b,
                                          stop=k == KB - 1 and b == 1)
                    pe.wait_ge(rms_ready, n + 1)
                    pe.wait_ge(rstd_ready, n + 1)
                    for j in range(TT):
                        mm = pe.matmul(BANK[6][:, 2 * j:2 * j + 1], RSTD[0:1, j * P:(j + 1) * P], con("ident")[0:1, 0:1],
                                       start=True, stop=True)
                    mm.then_inc(small_mm, 1)
                    pe.wait_ge(decay_ready, used["decay_ready"] + 1)
                    flat_g = TL[:, 3].rearrange("p t h -> p (t h)")
                    pe.matmul(BANK[7][:, 128:160], con("upper"), flat_g, start=True, stop=True)
                    pe.matmul(BANK[7][:, 192:224], con("ones_half"), flat_g, start=True, stop=True).then_inc(gcum_mm, 1)
                    for k in range(14, 16):
                        pe.wait_ge(inv_norm_ready, used["inv_norm_ready"] + k + 1)
                    pe.wait_ge(z_read, used["z_read"] + C_READS)

                    def rows(h, q):
                        s = h % 2
                        if q > q0:
                            pe.wait_ge(xx_read[s], 9 * q)
                            pe.wait_ge(att_ready[s], q - q0)
                        for k, (src, m) in enumerate(((BETA, "ident"), (TL[:, 3], "upper"))):
                            for j in range(TT):
                                mm = pe.matmul(BANK[4 * s + k][:, j * P:(j + 1) * P],
                                               src[:, j, h:h + 1].to_broadcast([P, P]), con(m), start=True, stop=True)
                            mm.then_inc(row_mm[s], 1)

                    def products(h, q):
                        s = h % 2
                        for k, (right, r) in enumerate(((KBETA, s), (QC, h))):
                            if k == 0:
                                pe.wait_ge(kbeta_ready[s], q - q0 + 1)
                            for j in range(TT):
                                c = slice(j * P, (j + 1) * P)
                                mm = pe.matmul(BANK[4 * s + 2 + k][:, c], KC[:, h, c], right[:, r, c], start=True, stop=True)
                            mm.then_inc(kq_mm[s], 1)

                    def token_major(h, q):
                        s = h % 2
                        for k, src in enumerate((KC, VC)):
                            if k == 0:
                                pe.wait_ge(kbeta_ready[s], q - q0 + 1)
                            else:
                                pe.wait_ge(dd_ready[s], q - q0 + 1)
                                pe.wait_ge(erow_ready[s], q - q0 + 1)
                            for j in range(TT):
                                c = slice(j * P, (j + 1) * P)
                                tr = pe.transpose(BANK[4 * s + k][:, c], src[:, h, c], con("ident"))
                            tr.then_inc(token_mm[s], 1)

                    pe.wait_ge(l2_done, 16)
                    pe.wait_ge(beta_ready, 1)
                    for p in range(HEADS // 2):
                        q = q0 + p
                        for s in range(2):
                            rows(2 * p + s, q)
                        for s in range(2):
                            products(2 * p + s, q)
                        for s in range(2):
                            token_major(2 * p + s, q)
                        for s in range(2):
                            pe.wait_ge(token_read[s], used["token_read"] + 2 * (p + 1))
                            pe.wait_ge(att_ready[s], p + 1)
                        pe_first_inverse(q)
                        for l in range(5):
                            pe_inverse_level(q, l, mat_base + p + 1)

                    for s in range(2):
                        pe.wait_ge(xx_read[s], 9 * (q0 + 4))
                        pe.wait_ge(qk_scaled[s], 8)
                    for c in range(NCHUNK):
                        j, th = c // 2, slice(c % 2 * CHUNK, (c % 2 + 1) * CHUNK)
                        cc = slice(c * CHUNK, (c + 1) * CHUNK)
                        if c:
                            for g in range(2):
                                pe.wait_ge(state_ready, used["state_ready"] + 2 * (c - 1) + g + 1)
                                for h in range(4 * g, 4 * g + 4):
                                    mm = pe.matmul(BANK[g][th, h % 4 * P:(h % 4 + 1) * P], KC[:, h, cc], SC[:, c % 2, h, :],
                                                   start=True, stop=True)
                                mm.then_inc(predict_mm, 1)
                        for g in range(2):
                            if c:
                                pe.wait_ge(predict_added, used["predict_added"] + 2 * (c - 1) + g + 1)
                            for h in range(4 * g, 4 * g + 4):
                                mm = pe.matmul(BANK[2 + g][th, h % 4 * P:(h % 4 + 1) * P], XTC[th, h, j, th], VTK[th, h, j, :],
                                               start=True, stop=True)
                            mm.then_inc(solve_mm, 1)
                        for g in range(2):
                            pe.wait_ge(solve_read, used["solve_read"] + 2 * c + g + 1)
                            if c < NCHUNK - 1:
                                for h in range(4 * g, 4 * g + 4):
                                    mm = pe.matmul(BANK[4 + g][:, h % 4 * P:(h % 4 + 1) * P], KDT[th, h, j, :], VTK[th, h, j, :],
                                                   start=True, stop=True)
                                mm.then_inc(state_mm, 1)
                        if c:
                            pe.wait_ge(out_read, used["out_read"] + c)
                        for h in range(HEADS):
                            o = slice(h * CHUNK, (h + 1) * CHUNK)
                            if c:
                                pe.matmul(BANK[6][:, o], SC[:, c % 2, h, :], QC[:, h, cc], start=True, stop=False)
                            mm = pe.matmul(BANK[6][:, o], VTK[th, h, j, :], ATT[th, h, j, th], start=c == 0, stop=True)
                        mm.then_inc(out_mm, 1)
                    for h in range(HEADS):
                        pe.wait_ge(out_sq_ready, used["out_sq_ready"] + h + 1)
                        if h >= 4:
                            pe.wait_ge(orn_ready, h - 3)
                        pe.matmul(BANK[h % 4][:, :], con("ones"), DT[:, :, :, :].rearrange("p a t c -> p a (t c)")[:, h % 2, :]
                                  if h % 4 < 2 else DS[:, :, :, :].rearrange("p a t c -> p a (t c)")[:, h % 2, :],
                                  start=True, stop=True).then_inc(out_sq_mm, 1)
                    mix_out(phase)
            norm_sum(n_norms - 1)

        @block.scalar
        def _(act):
            def split_hi(c, i):
                cols = units[c][1]
                act.wait_ge(w_landed[c % RING], 16 * (c // RING + i + 1))
                if fits(c + 4 * i - SPLIT + 1):
                    act.wait_ge(unit_done, c + 4 * i - SPLIT + 1)
                act.activation(WS[:, 0, c % SPLIT, 0:cols], RAW[:, c % RING, 0:cols], ACT.Copy).then_inc(hi_ready, 1)

            def residual(n, i, j):
                act.wait_ge(x_ready[j], KB // 2 * n + i + 1)
                if j == 0 and fits(KB // 2 * n + i):
                    act.wait_ge(acc_ready[0], KB // 2 * n + i)
                if j == 1 and fits(3 * n + i):
                    act.wait_ge(acc_ready[1], 3 * n + i)
                    if n:
                        act.wait_ge(sum_ready, n)
                act.activation(US[:, j, :], X[:, 2 * i + j, :], ACT.Square).then_inc(sq_ready[j], 1)
                if n < n_norms - 1:
                    act.wait_ge(hw_ready[j], KB // 2 * n + i + 1)
                    act.activation(H[:, 0, 2 * i + j, :], GS[:, j, :], ACT.Copy).then_inc(hhi_ready[j], 1)

            def root(n):
                act.wait_ge(sum_ready, n + 1)
                if n:
                    last_use(act, plan[n - 1])
                act.activation(RSTD[:, :], SQ[:, :], ACT.Sqrt, bias=EPS, scale=1.0 / D_MODEL).then_inc(rms_ready, 1)

            def ffn_act(phase, i, j):
                q = ffn_index[phase] * (FB // 2) + i
                act.wait_ge(gs_ready[j], q + 1)
                act.activation(GS[:, j, :], GS[:, j, :], ACT.Silu).then_inc(silu_ready[j], 1)

            def ffn_hi(phase, i, j):
                q = ffn_index[phase] * (FB // 2) + i
                act.wait_ge(prod_ready[j], q + 1)
                act.activation(A[:, 0, 2 * i + j, :], US[:, j, :], ACT.Copy).then_inc(ahi_ready[j], 1)


            def act_inverse(q, finals):
                for s in range(2):
                    act.wait_ge(x1_mm[s], q + 1)
                    act.activation(INV[s]["XX"][:, :, :], BANK[4 * s][:, :].rearrange("p (t c) -> p t c", t=TT),
                                   ACT.Copy).then_inc(x1_read[s], 1)
                for l in range(5):
                    for s in range(2):
                        if l < 4:
                            act.wait_ge(xx_mm[s], 9 * q + 2 * l + 1)
                            act.activation(INV[s]["XX"][:, :, :], BANK[4 * s][:, :].rearrange("p (t c) -> p t c", t=TT),
                                           ACT.Copy).then_inc(xx_read[s], 1)
                        act.wait_ge(xx_mm[s], 9 * q + 2 * l + (2 if l < 4 else 1))
                        dst = INV[s]["XT"][:, :, :] if l < 4 else finals[s]
                        act.activation(dst, BANK[4 * s + 1][:, :].rearrange("p (t c) -> p t c", t=TT),
                                       ACT.Copy).then_inc(xx_read[s], 1)

            def act_gate(h):
                act.wait_ge(z_read, used["z_read"] + 24 + h + 1)
                act.activation(GC_[:, h, :], GC_[:, h, :], ACT.Silu).then_inc(gate_c, 1)

            step = Steps(act, act_step)
            act.wait_ge(landed, 48)
            split_hi(0, 0)
            split_hi(1, 0)
            for i in range(KB // 2):
                for j in range(2):
                    residual(0, i, j)
            for phase in plan:
                root(norm_of[phase])
                if phase.startswith("ffn"):
                    def up(i, j):
                        split_hi(base[phase] + 2 * j + 2, i)
                        ffn_act(phase, i, j)
                        split_hi(base[phase] + 2 * j + 3, i)
                        ffn_hi(phase, i, j)

                    def down(i, j):
                        for k in range(2):
                            split_next(base[phase] + 2 * FB + 2 * j + 2 + k, i)
                        residual(norm_of[phase] + 1, i, j)

                    def split_next(c, i):
                        if isinstance(i, int):
                            c, i = c + 4 * i, 0
                        if not isinstance(i, int) or c < n_units:
                            split_hi(c, i)

                    with act.Fori(0, FB // 2 - 1) as i:
                        for j in range(2):
                            up(i, j)
                    i = FB // 2 - 1
                    up_last = base[phase] + 4 * i
                    for j in range(2):
                        split_hi(up_last + 2 * j + 2, 0)
                        ffn_act(phase, i, j)
                        split_hi(up_last + 2 * j + 3, 0)
                        ffn_hi(phase, i, j)
                    with act.Fori(0, KB // 2 - 1) as i:
                        for j in range(2):
                            down(i, j)
                    for j in range(2):
                        down(KB // 2 - 1, j)
                if phase == "ab":
                    n, u0 = norm_of[phase], base[phase]
                    ap = PRM[:, PARAMS["lru_a_param"][0]:PARAMS["lru_a_param"][0] + 4]
                    step.link(act.activation(SMALL[:, 0, :], ap, ACT.Abs))
                    act.activation(SMALL[:, 1, :], SMALL[:, 0, :], ACT.Exp, scale=-1.0).then_inc(sp_act, 1)
                    act.wait_ge(sp_vec, 1)
                    act.activation(SMALL[:, 3, :], SMALL[:, 2, :], ACT.Ln).then_inc(sp_act, 1)
                    for t in range(AB_BLOCKS):
                        if t + 2 < AB_BLOCKS:
                            split_hi(u0 + t + 2, 0)
                        if 4 <= t < 8:
                            act.wait_ge(z_read, t + 1)
                            act.activation(GG[:, t - 4, :], PAD[:, t % 2, 3:3 + SEQ], ACT.Gelu_apprx_tanh).then_inc(silu_done, 1)
                        if t in (9, 11):
                            k = (t - 9) // 2
                            for b in range(4):
                                act.wait_ge(gate_mm, 4 * k + b + 1)
                                act.activation((RG, IG)[k][:, b, :], BANK[2 + b][:, :], ACT.Sigmoid,
                                               bias=par(("lru_gate_a_b", "lru_gate_x_b")[k], b)).then_inc(gate_read, 1)
                        if t == 13:
                            act.wait_ge(gate_read, 4)
                            act.wait_ge(sp_vec, 2)
                            for b in range(4):
                                step.inc(act.activation(LA[:, b, :], RG[:, b, :], ACT.Exp, scale=LRU_NSCALE[:, b:b + 1]))
                            for b in range(4):
                                step.inc(act.activation(LU[:, b, :], RG[:, b, :], ACT.Tanh, scale=LRU_SCALE[:, b:b + 1]))
                            step.wait()
                            act.activation(RG[:, :, :], LA[:, :, :], ACT.Square).then_inc(lru_sq, 1)
                        if t == 15:
                            act.wait_ge(lru_u2, 1)
                            act.activation(LU[:, :, :], LU[:, :, :], ACT.Sqrt).then_inc(lru_root, 1)
                    act.wait_ge(p_ready, 2)
                    act.activation(LOW[0:CHUNK, 0, :], LOW[0:CHUNK, 0, :], ACT.Tanh).then_inc(low_ready, 1)
                    act.activation(LOW[:, 1, :], LOW[:, 1, :], ACT.Sigmoid).then_inc(low_ready, 1)
                    act.wait_ge(ya_ready, 1)
                    for k in range(2):
                        for b in range(4):
                            act.wait_ge(small_mm, 4 * k + b + 1)
                            act.activation((SIG, AL)[k][:, b, :], BANK[2 + b][:, :], ACT.Sigmoid,
                                           bias=par(("rwkv_w0", "rwkv_a0")[k], b)).then_inc(low_read, 1)
                    act.wait_ge(unit_done, u0 + AB_BLOCKS)
                    for b in range(4):
                        act.activation(YA[:, b, :], GG[:, b, :], ACT.Copy).then_inc(ya_kept, 1)
                    act.wait_ge(cum_ready, 1)
                    act.activation(PINV[:, :, :], CUM[:, :, :], ACT.Exp, scale=DECAY_C).then_inc(exp_ready, 1)
                    act.wait_ge(exp_ready, 1)
                    act.wait_ge(cum_ready, 2)
                    act.activation(CUM[:, :, :], CUM[:, :, :], ACT.Exp, scale=-DECAY_C).then_inc(exp_ready, 1)
                    act.activation(CPRE[:, :, :], CPRE[:, :, :], ACT.Exp, scale=-DECAY_C).then_inc(exp_ready, 1)
                    act.wait_ge(kk_raw, 4)
                    act.activation(TMPQ[:, :, :], SIG[:, :, :], ACT.Square).then_inc(kk_sq, 1)
                    act.wait_ge(ss_max, 4)
                    step.link(act.activation(TMPQ[:, :, :], TMPQ[:, :, :], ACT.Ln, scale=float(2.0 ** 20)))
                    act.activation(TMPQ[:, :, :], TMPQ[:, :, :], ACT.Exp, scale=-0.5,
                                   bias=float(10 * np.log(2.0))).then_inc(inv_norm_ready, 1)
                    for k, dst in enumerate((KT, BT, VT)):
                        for j in range(TT):
                            act.wait_ge(tr_mm, 4 * k + j + 1)
                            if (k, j) == (0, 0):
                                act.wait_ge(fm_ready, 6)
                            if (k, j) == (1, 0):
                                act.wait_ge(tr_mm, 4)
                            if (k, j) == (2, 0):
                                act.wait_ge(ya_kept, 4)
                            act.activation(dst[:, j, :], BANK[(4 * k + j) % 2][:, :], ACT.Copy).then_inc(tr_read, 1)
                    for p in range(HEADS // 2):
                        for s in range(2):
                            w = slice((2 * p + s) * CHUNK, (2 * p + s + 1) * CHUNK)
                            act.wait_ge(token_mm[s], 2 * p + 1)
                            act.activation(GT[:, :, w], BANK[4 * s + 1][:, 0:TT * CHUNK].rearrange("p (t c) -> p t c", t=TT),
                                           ACT.Copy).then_inc(token_read[s], 1)
                            act.wait_ge(token_mm[s], 2 * p + 2)
                            rows = slice(s * CHUNK, (s + 1) * CHUNK)
                            act.activation(YI[rows, p, :], BANK[4 * s + 2][rows, :], ACT.Copy).then_inc(token_read[s], 1)
                        act_inverse(p, [xt_of(2 * p + s) for s in range(2)])
                    for c in range(NCHUNK):
                        j, th = c // 2, slice(c % 2 * CHUNK, (c % 2 + 1) * CHUNK)
                        act.wait_ge(solve_mm, c + 1)
                        act.activation(GT[th, j, :], BANK[2][th, :], ACT.Copy).then_inc(solve_read, 1)
                    act.wait_ge(out_mm, 4)
                    act.activation(MIX_HI[:, 0:4, :], YA[:, :, :], ACT.Copy).then_inc(ya_hi, 1)
                    for b in range(4):
                        act.wait_ge(dev_ready, b + 1)
                        act.activation(TMPQ[:, b, :], DF[:, b, :], ACT.Square).then_inc(out_sq_ready, 1)
                    for b in range(4):
                        act.wait_ge(out_sq_mm, b + 1)
                        step.inc(act.activation(TMPQ[:, b, :], BANK[4 + b][:, :], ACT.Ln, scale=1.0 / CHUNK, bias=64e-5))
                    step.wait()
                    act.activation(TMPQ[:, :, :], TMPQ[:, :, :], ACT.Exp, scale=-0.5).then_inc(decay_ready, 1)
                    for b in range(4):
                        act.wait_ge(mixed_ready, b + 1)
                        act.activation(MIX_HI[:, 4 + b, :], YF[:, b, :], ACT.Copy).then_inc(mixed_hi, 1)
                if phase == "c":
                    n, u0, q0 = norm_of[phase], base[phase], inv_base[phase]
                    act.wait_ge(small_weights, used["small_weights"] + 16)
                    act.activation(CTS[:, 0, :, :], CT[:, :, :], ACT.Copy).then_inc(c_tail_hi, 1)
                    for t in range(C_BLOCKS):
                        if t + 2 < C_BLOCKS:
                            split_hi(u0 + t + 2, 0)
                        if t < 24:
                            act.wait_ge(conv_ready, used["conv_ready"] + t + 1)
                            dst = (QC, KC, VC)[t // 8][:, t % 8, :]
                            act.activation(dst, dst, ACT.Silu).then_inc(silu_done, 1)
                        else:
                            h = t - 24
                            for k, src in enumerate((QC, KC)):
                                act.wait_ge(silu_done, used["silu_done"] + 16)
                                if h >= 2:
                                    act.wait_ge(l2_done, 2 * (h - 2) + k + 1)
                                act.activation(SQT[:, t % 2, k, :], src[:, h, :], ACT.Square).then_inc(sq_c, 1)
                            if h:
                                act_gate(h - 1)
                            for k in range(2):
                                act.wait_ge(norm_sum_mm, used["norm_sum_mm"] + 2 * h + k + 1)
                                step.link(act.activation(SQT[:, t % 2, k, :], BANK[2 + 2 * (t % 2) + k][:, :], ACT.Ln, bias=EPS))
                                act.activation(SQT[:, t % 2, k, :], SQT[:, t % 2, k, :], ACT.Exp, scale=-0.5,
                                               bias=float(-0.5 * np.log(P)) if k == 0 else 0.0).then_inc(inv_norm_ready, 1)
                    act_gate(7)
                    act.wait_ge(tail_scaled, 2)
                    step.link(act.activation(TL[:, 5], TL[:, 4], ACT.Abs))
                    act.activation(TL[:, 6], TL[:, 5], ACT.Exp, scale=-1.0).then_inc(al_act, 1)
                    act.wait_ge(al_vec, 1)
                    act.activation(TL[:, 8], TL[:, 7], ACT.Ln).then_inc(al_act, 1)
                    al = PARAMS["dn_A_log"][0]
                    act.activation(TL[:, 9, 0, :], PRM[:, al:al + HEADS], ACT.Exp).then_inc(al_act, 1)
                    act.activation(BETA, TL[:, 10], ACT.Sigmoid).then_inc(beta_ready, 1)
                    act.wait_ge(gtok_ready, 2)
                    act.activation(KDEC, KDEC, ACT.Exp).then_inc(kdec_ready, 1)
                    act.wait_ge(kdec_ready, 1)
                    act.wait_ge(beta_ready, 1)
                    for p in range(HEADS // 2):
                        q = q0 + p
                        for s in range(2):
                            act.wait_ge(row_mm[s], 2 * p + 2)
                            if p:
                                act.wait_ge(qk_scaled[s], 2 * p)
                            act.wait_ge(dd_ready[s], p + 1)
                            act.activation(EROW[:, s, :], BANK[4 * s + 1][:, :], ACT.Exp).then_inc(erow_ready[s], 1)
                            act.activation(DT[:, s], DT[:, s], ACT.Exp).then_inc(dexp_ready[s], 1)
                        for s in range(2):
                            h = 2 * p + s
                            for k, (dst, factor) in enumerate(((KDT, KDEC), (VTK, BETA))):
                                act.wait_ge(token_mm[s], used["token_mm"] + 2 * p + k + 1)
                                for j in range(TT):
                                    ins = act.activation(dst[:, h, j, :], BANK[4 * s + k][:, j * P:(j + 1) * P], ACT.Copy,
                                                         scale=factor[:, j, h:h + 1])
                                ins.then_inc(token_read[s], 1)
                        act_inverse(q, [XTC[:, 2 * p + s] for s in range(2)])
                    for c in range(NCHUNK):
                        j, th = c // 2, slice(c % 2 * CHUNK, (c % 2 + 1) * CHUNK)
                        for g in range(2):
                            act.wait_ge(solve_mm, used["solve_mm"] + 2 * c + g + 1)
                            act.activation(VTK[th, 4 * g:4 * g + 4, j, :], BANK[2 + g][th, :].rearrange("p (h v) -> p h v", h=4),
                                           ACT.Copy).then_inc(solve_read, 1)
                        act.wait_ge(out_mm, used["out_mm"] + c + 1)
                        act.activation(KC[:, :, c * CHUNK:(c + 1) * CHUNK], BANK[6][:, :].rearrange("p (h t) -> p h t", h=HEADS),
                                       ACT.Copy).then_inc(out_read, 1)
                    act.wait_ge(out_read, used["out_read"] + NCHUNK)

                    def norm_buffer(h):
                        return (DT if h % 4 < 2 else DS)[:, h % 2].rearrange("p t c -> p (t c)")

                    def out_square(h):
                        if h >= 4:
                            act.wait_ge(mixed_ready, used["mixed_ready"] + h - 3)
                        act.activation(norm_buffer(h), KC[:, h, :], ACT.Square).then_inc(out_sq_ready, 1)

                    for h in range(4):
                        out_square(h)
                    for h in range(HEADS):
                        act.wait_ge(out_sq_mm, used["out_sq_mm"] + h + 1)
                        step.link(act.activation(norm_buffer(h), BANK[h % 4][:, :], ACT.Ln, scale=1.0 / P, bias=EPS))
                        act.activation(norm_buffer(h), norm_buffer(h), ACT.Exp, scale=-0.5).then_inc(orn_ready, 1)
                        if h >= 1:
                            act.wait_ge(mixed_ready, used["mixed_ready"] + h)
                            act.activation(MIX_HI[:, h - 1, :], KC[:, h - 1, :], ACT.Copy).then_inc(mixed_hi, 1)
                            if h + 3 < HEADS:
                                out_square(h + 3)
                    act.wait_ge(mixed_ready, used["mixed_ready"] + HEADS)
                    act.activation(MIX_HI[:, HEADS - 1, :], KC[:, HEADS - 1, :], ACT.Copy).then_inc(mixed_hi, 1)
                if phase in ("ab", "c"):
                    c0 = base[phase] + (AB_BLOCKS if phase == "ab" else C_BLOCKS)
                    act.wait_ge(mixer_done[phase], 1)
                    split_hi(c0, 0)
                    split_hi(c0 + 1, 0)
                    for m in range(KB):
                        if c0 + m + 2 < n_units:
                            split_hi(c0 + m + 2, 0)
                        residual(norm_of[phase] + 1, m // 2, m % 2)
            root(n_norms - 1)

        @block.gpsimd
        def _(pool):
            def residual(n, i, j):
                pool.wait_ge(sq_ready[j], KB // 2 * n + i + 1)
                if j == 0 and fits(3 * n + i):
                    pool.wait_ge(acc_ready[1], 3 * n + i)
                if j == 1:
                    pool.wait_ge(acc_ready[0], KB // 2 * n + i + 1)
                pool.tensor_tensor(ACC[:, :], ACC[:, :], US[:, j, :], ALU.add).then_inc(acc_ready[j], 1)

            def clear(n):
                if n:
                    pool.wait_ge(sum_ready, n)
                pool.memset(ACC[:, :], 0.0).then_inc(acc_clear, 1)
                pool.wait_ge(acc_clear, n + 1)

            def squares(n):
                clear(n)
                for j in range(2):
                    residual(n, 0, j)
                with pool.Fori(1, KB // 2 - 1) as i:
                    for j in range(2):
                        residual(n, i, j)
                residual(n, KB // 2 - 1, 0)


            def pool_inverse(q, masked):
                for s in range(2):
                    w = INV[s]
                    pool.wait_ge(mat_ready[s], masked)
                    if q:
                        pool.wait_ge(u_mm[s], 5 * q)
                        pool.wait_ge(xx_mm[s], 9 * q)
                    step.link(pool.tensor_tensor(w["TM"][:, :, :], w["TT"][:, :, :], tiles(con("pair1")), ALU.mult))
                    pool.tensor_tensor(w["XT"][:, :, :], tiles(con("ident")), w["TM"][:, :, :],
                                       ALU.subtract).then_inc(xt1_ready[s], 1)
                for l in range(5):
                    for s in range(2):
                        w = INV[s]
                        if l:
                            pool.wait_ge(u_mm[s], 5 * q + l)
                        else:
                            pool.wait_ge(xt1_ready[s], q + 1)
                        pool.tensor_tensor(w["TM"][:, :, :], w["TT"][:, :, :], tiles(con(f"pair{2 << l}")),
                                           ALU.mult).then_inc(tm_ready[s], 1)

            step = Steps(pool, pool_step)
            squares(0)
            for phase in plan:
                if phase == "ab":
                    for p in range(HEADS // 2):
                        pool_inverse(p, 4 * p + 1)
                if phase == "c":
                    for p in range(HEADS // 2):
                        for s in range(2):
                            pool.wait_ge(dexp_ready[s], p + 1)
                            if p:
                                pool.wait_ge(mat_ready[s], mat_base + p)
                            step.link(pool.tensor_tensor(DT[:, s], DT[:, s], tiles(con("upper")), ALU.mult))
                            pool.tensor_tensor(DS[:, s], DT[:, s], tiles(con("strict")), ALU.mult).then_inc(dmask_ready[s], 1)
                        pool_inverse(inv_base[phase] + p, mat_base + p + 1)
                squares(norm_of[phase] + 1)

        @block.vector
        def _(vec):
            def split_lo(c, i):
                cols = units[c][1]
                vec.wait_ge(hi_ready, c + 4 * i + 1)
                vec.tensor_tensor(WS[:, 1, c % SPLIT, 0:cols], RAW[:, c % RING, 0:cols],
                                  WS[:, 0, c % SPLIT, 0:cols].bitcast(F32), ALU.subtract).then_inc(lo_ready, 1)

            def split_next(c, i):
                if isinstance(i, int):
                    c, i = c + 4 * i, 0
                if not isinstance(i, int) or c < n_units:
                    split_lo(c, i)

            def residual_add(n, i, j, bank, factor, done):
                vec.wait_ge(unit_done, done)
                vec.scalar_tensor_tensor(X[:, 2 * i + j, :], bank[:, :], factor, X[:, 2 * i + j, :],
                                         ALU.mult, ALU.add).then_inc(x_ready[j], 1)

            def residual_split(n, i, j):
                q = KB // 2 * n + i
                vec.wait_ge(x_ready[j], q + 1)
                if fits(q):
                    vec.wait_ge(h_ready[j], q)
                w = norm_cols[n] + j + 2 * i
                vec.tensor_scalar(GS[:, j, :], X[:, 2 * i + j, :],
                                  PRM[:, w:w + 1] if isinstance(i, int) else PRM[:, bass.ds(w, 1)],
                                  None, ALU.mult).then_inc(hw_ready[j], 1)
                vec.wait_ge(hhi_ready[j], q + 1)
                vec.tensor_tensor(H[:, 1, 2 * i + j, :], GS[:, j, :], H[:, 0, 2 * i + j, :].bitcast(F32),
                                  ALU.subtract).then_inc(h_ready[j], 1)

            def inverse_root(n):
                vec.wait_ge(rms_ready, n + 1)
                vec.reciprocal(RSTD[:, :], RSTD[:, :]).then_inc(rstd_ready, 1)

            def scaled(phase, i, j, k):
                q = ffn_index[phase] * (FB // 2) + i
                vec.wait_ge(unit_done, base[phase] + 4 * i + 2 * j + k + 1)
                if fits(q):
                    vec.wait_ge((prod_ready, act_ready)[k][j], q)
                vec.tensor_tensor((GS, US)[k][:, j, :], (GATE, UP)[k][j][:, :], RSTD[:, :],
                                  ALU.mult).then_inc((gs_ready, us_ready)[k][j], 1)

            def product(phase, i, j):
                q = ffn_index[phase] * (FB // 2) + i
                vec.wait_ge(silu_ready[j], q + 1)
                vec.wait_ge(us_ready[j], q + 1)
                vec.tensor_tensor(US[:, j, :], GS[:, j, :], US[:, j, :], ALU.mult).then_inc(prod_ready[j], 1)

            def product_lo(phase, i, j):
                q = ffn_index[phase] * (FB // 2) + i
                vec.wait_ge(ahi_ready[j], q + 1)
                vec.tensor_tensor(A[:, 1, 2 * i + j, :], US[:, j, :], A[:, 0, 2 * i + j, :].bitcast(F32),
                                  ALU.subtract).then_inc(act_ready[j], 1)


            def vec_inverse(q):
                for l in range(5):
                    for s in range(2):
                        vec.wait_ge(u_mm[s], 5 * q + l + 1)
                        vec.tensor_tensor(INV[s]["IU"][:, :, :], tiles(con("ident")),
                                          BANK[4 * s + 3][:, :].rearrange("p (t c) -> p t c", t=TT),
                                          ALU.subtract).then_inc(iu_ready[s], 1)

            def unit_vectors(h):
                for k, t in enumerate((QC, KC)):
                    vec.wait_ge(inv_norm_ready, used["inv_norm_ready"] + 2 * h + k + 1)
                    vec.tensor_tensor(t[:, h, :], t[:, h, :], SQT[:, h % 2, k, :], ALU.mult).then_inc(l2_done, 1)

            step = Steps(vec, vec_step)
            vec.wait_ge(landed, 48)
            split_lo(0, 0)
            split_lo(1, 0)
            for i in range(KB // 2):
                for j in range(2):
                    vec.sem_inc(x_ready[j], 1)
                    residual_split(0, i, j)
            for phase in plan:
                inverse_root(norm_of[phase])
                vec.wait_ge(rstd_ready, norm_of[phase] + 1)
                if phase.startswith("ffn"):
                    def up(i, j, c):
                        scaled(phase, i, j, 0)
                        split_lo(c + 2 * j + 2, 0 if isinstance(i, int) else i)
                        scaled(phase, i, j, 1)
                        product(phase, i, j)
                        split_lo(c + 2 * j + 3, 0 if isinstance(i, int) else i)
                        product_lo(phase, i, j)

                    def down(i, j):
                        c = base[phase] + 2 * FB + 2 * j
                        split_next(c + 2, i)
                        residual_add(norm_of[phase] + 1, i, j, DOWN[j], 0.5, c + 4 * i + 2)
                        split_next(c + 3, i)
                        if norm_of[phase] + 1 < n_norms - 1:
                            residual_split(norm_of[phase] + 1, i, j)

                    for j in range(2):
                        up(0, j, base[phase])
                    with vec.Fori(1, FB // 2 - 1) as i:
                        for j in range(2):
                            up(i, j, base[phase])
                    for j in range(2):
                        up(FB // 2 - 1, j, base[phase] + 4 * (FB // 2 - 1))
                    with vec.Fori(0, KB // 2 - 1) as i:
                        for j in range(2):
                            down(i, j)
                    for j in range(2):
                        down(KB // 2 - 1, j)
                if phase == "ab":
                    n, u0 = norm_of[phase], base[phase]
                    vec.wait_ge(unit_done, u0)
                    vec.memset(LW[:, :, :, :], 0.0).then_inc(pad_zero, 1)
                    vec.wait_ge(h_ready[1], KB // 2 * (n + 1))
                    vec.wait_ge(sum_ready, n + 1)
                    vec.memset(PAD[:, :, 0:3], 0.0).then_inc(pad_zero, 1)
                    S = [SMALL[:, k, :] for k in range(16)]
                    vec.wait_ge(sp_act, 1)
                    step.link(vec.tensor_scalar(S[2], S[1], 1.0, None, ALU.add))
                    vec.sem_inc(sp_vec, 1)
                    step.link(vec.tensor_scalar(S[4], S[2], 1.0, None, ALU.subtract))
                    step.link(vec.tensor_scalar(S[5], S[4], 0.0, None, ALU.is_equal))
                    step.link(vec.tensor_tensor(S[4], S[4], S[5], ALU.add))
                    step.link(vec.reciprocal(S[6], S[4]))
                    vec.wait_ge(sp_act, 2)
                    step.link(vec.tensor_tensor(S[7], S[3], S[5], ALU.add))
                    step.link(vec.tensor_tensor(S[7], S[7], S[1], ALU.mult))
                    step.link(vec.tensor_tensor(S[7], S[7], S[6], ALU.mult))
                    ap = PRM[:, PARAMS["lru_a_param"][0]:PARAMS["lru_a_param"][0] + 4]
                    step.link(vec.tensor_scalar(S[8], ap, -1.0, 0.0, ALU.mult, ALU.max))
                    step.link(vec.tensor_tensor(S[7], S[7], S[8], ALU.add))
                    step.link(vec.tensor_scalar(LRU_SCALE, S[7], 8.0, None, ALU.mult))
                    vec.tensor_scalar(LRU_NSCALE, S[7], -8.0, None, ALU.mult).then_inc(sp_vec, 1)
                    vec.wait_ge(pad_zero, 2)
                    for t in range(AB_BLOCKS):
                        pad = PAD[:, t % 2, :]
                        z = pad[:, 3:3 + SEQ]
                        step.wait()
                        if 4 <= t - 2 < 8:
                            vec.wait_ge(silu_done, t - 2 - 3)
                        vec.wait_ge(unit_done, u0 + t + 1)
                        vec.tensor_tensor(z, BANK[t % 2][:, :], RSTD[:, :], ALU.mult).then_inc(z_read, 1)
                        if t + 2 < AB_BLOCKS:
                            split_lo(u0 + t + 2, 0)
                        vec.wait_ge(z_read, t + 1)
                        if t < 4:
                            dst = XC[:, t, :]
                            step.link(vec.tensor_scalar(dst, z, par("lru_conv_w", 12 + t), par("lru_conv_b", t), ALU.mult, ALU.add))
                            for k in (2, 1, 0):
                                ins = vec.scalar_tensor_tensor(dst, pad[:, k:k + SEQ], par("lru_conv_w", 4 * k + t), dst,
                                                               ALU.mult, ALU.add)
                                if k:
                                    step.link(ins)
                            ins.then_inc(conv_ready, 1)
                            vec.wait_ge(conv_ready, t + 1)
                        if t >= 8:
                            dst = ([LOW[:, 0, :], LOW[:, 1, :]] + [KF[:, b, :] for b in range(4)]
                                   + [VF[:, b, :] for b in range(4)] + [RF[:, b, :] for b in range(4)])[t - 8]
                            mu = ([12, 13] + list(range(4, 12)) + list(range(4)))[t - 8]
                            if t > 8:
                                vec.wait_ge(p_ready, t - 8)
                            step.link(vec.tensor_tensor(DIFF[:, :], pad[:, 2:2 + SEQ], z, ALU.subtract))
                            vec.scalar_tensor_tensor(dst, DIFF[:, :], par("rwkv_mu", mu), z,
                                                     ALU.mult, ALU.add).then_inc(p_ready, 1)
                            vec.wait_ge(p_ready, t - 7)
                        if t == 14:
                            vec.wait_ge(lru_sq, 1)
                            vec.scalar_tensor_tensor(flat(LU), flat(RG), 1.0, flat(LU), ALU.add, ALU.mult).then_inc(lru_u2, 1)
                            vec.wait_ge(gate_read, 8)
                            step.link(vec.tensor_tensor(IG[:, :, :], IG[:, :, :], XC[:, :, :], ALU.mult))
                        if t == 16:
                            vec.wait_ge(lru_root, 1)
                            step.link(vec.tensor_tensor(IG[:, :, :], IG[:, :, :], LU[:, :, :], ALU.mult))
                        if t in (17, 18):
                            for b in (2 * (t - 17), 2 * (t - 17) + 1):
                                step.link(vec.tensor_tensor_scan(XC[:, b, :], LA[:, b, :], IG[:, b, :], 0.0, ALU.mult, ALU.add))
                        if t == 19:
                            vec.wait_ge(silu_done, 4)
                            vec.tensor_tensor(GG[:, :, :], XC[:, :, :], GG[:, :, :], ALU.mult).then_inc(ya_ready, 1)
                    vec.wait_ge(low_read, 4)
                    for b in range(4):
                        step.inc(vec.tensor_tensor_scan(CUM[:, b, :], CST[:, NCONST - SEQ:NCONST], SIG[:, b, :], 0.0,
                                                        ALU.mult, ALU.add))
                    step.wait()
                    vec.sem_inc(cum_ready, 1)
                    vec.tensor_tensor(CPRE[:, :, :], CUM[:, :, :], SIG[:, :, :], ALU.subtract).then_inc(cum_ready, 1)
                    vec.wait_ge(cum_ready, 2)
                    for b in range(4):
                        vec.tensor_scalar(SIG[:, b, :], KF[:, b, :], par("rwkv_k_k", b), None, ALU.mult).then_inc(kk_raw, 1)
                    vec.wait_ge(low_read, 8)
                    for b in range(4):
                        vec.wait_ge(norm_sum_mm, 4)
                        vec.tensor_scalar(TMPQ[:, b, :], BANK[2 + b][:, :], 1e-24, None, ALU.max).then_inc(ss_max, 1)
                    vec.wait_ge(inv_norm_ready, 1)
                    step.link(vec.tensor_tensor(SIG[:, :, :], SIG[:, :, :], TMPQ[:, :, :], ALU.mult))
                    for b in range(4):
                        step.inc(vec.tensor_scalar(TMPQ[:, b, :], AL[:, b, :], -1.0, par("rwkv_k_a", b), ALU.add, ALU.mult))
                    step.wait()
                    step.link(vec.scalar_tensor_tensor(flat(KF), flat(TMPQ), 1.0, flat(KF), ALU.add, ALU.mult))
                    step.link(vec.tensor_tensor(AL[:, :, :], AL[:, :, :], SIG[:, :, :], ALU.mult))
                    for b in range(4):
                        vec.scalar_tensor_tensor(TMPQ[:, b, :], RF[:, b, :], par("rwkv_r_k", b), KF[:, b, :],
                                                 ALU.mult, ALU.mult).then_inc(bon_in, 1)
                    vec.wait_ge(exp_ready, 3)
                    vec.tensor_tensor(CPRE[:, :, :], CPRE[:, :, :], SIG[:, :, :], ALU.mult).then_inc(fm_ready, 1)
                    step.link(vec.tensor_copy(PEND[:, :, :], CUM[:, :, :].rearrange("p b (c k) -> p b c k", k=CHUNK)[:, :, :, CHUNK - 1]))
                    vec.wait_ge(bon_in, 4)
                    vec.tensor_tensor(RF[:, :, :], RF[:, :, :], CUM[:, :, :], ALU.mult).then_inc(fm_ready, 1)
                    vec.tensor_tensor(KF[:, :, :], KF[:, :, :], PINV[:, :, :], ALU.mult).then_inc(fm_ready, 1)
                    vec.tensor_tensor(AL[:, :, :], AL[:, :, :], PINV[:, :, :], ALU.mult).then_inc(fm_ready, 1)
                    vec.wait_ge(fm_ready, 4)
                    pend = PEND[:, :, :].rearrange("p b c -> p (b c)").unsqueeze(2).to_broadcast([P, 32, CHUNK])
                    chunks = [flat(t_).rearrange("p (c k) -> p c k", k=CHUNK) for t_ in (KH, KF, PINV, AL)]
                    vec.tensor_tensor(chunks[0], chunks[1], pend, ALU.mult).then_inc(fm_ready, 1)
                    vec.scalar_tensor_tensor(chunks[2], chunks[3], -1.0, pend, ALU.mult, ALU.mult).then_inc(fm_ready, 1)
                    for b in range(4):
                        vec.wait_ge(bon_mm, b + 1)
                        vec.tensor_tensor(BV[:, b, :], BANK[2 + b][:, :], VF[:, b, :], ALU.mult).then_inc(bv_ready, 1)
                    for p in range(HEADS // 2):
                        for s in range(2):
                            h = 2 * p + s
                            if p:
                                vec.wait_ge(tm_ready[s], 5 * p)
                                vec.wait_ge(token_mm[s], 2 * p)
                            else:
                                vec.wait_ge(bv_ready, 4)
                                vec.wait_ge(bon_mm, 4)
                            for k, (dst, mask) in enumerate(((INV[s]["TT"][:, :, :], "strict"), (TKM[s][:, :, :], "strict"),
                                                             (MKM[s][:, :, :], "upper"))):
                                vec.wait_ge(mat_mm[s], 4 * p + k + 1)
                                vec.tensor_tensor(dst, BANK[4 * s + k][:, :].rearrange("p (t c) -> p t c", t=TT),
                                                  tiles(con(mask)), ALU.mult).then_inc(mat_ready[s], 1)
                            vec.wait_ge(mat_mm[s], 4 * p + 4)
                            vec.scalar_tensor_tensor(MBT[:, h, :].rearrange("p (t c) -> p t c", t=TT),
                                                     BANK[4 * s + 3][:, :].rearrange("p (t c) -> p t c", t=TT), -1.0,
                                                     tiles(con("upper")), ALU.mult, ALU.mult).then_inc(mat_ready[s], 1)
                        vec_inverse(p)
                    for s in range(2):
                        vec.wait_ge(xx_read[s], 36)
                        vec.wait_ge(token_read[s], 8)
                    step.link(vec.memset(SH[:, 0, :, :], 0.0))
                    for c in range(NCHUNK):
                        j, th = c // 2, slice(c % 2 * CHUNK, (c % 2 + 1) * CHUNK)
                        if c:
                            for s in range(2):
                                vec.wait_ge(predict_mm, 2 * (c - 1) + s + 1)
                                g = GT[th, j, :].rearrange("p (b s v) -> p b s v", s=2, v=CHUNK)[:, :, s, :]
                                vec.tensor_tensor(g, g, BANK[s][th, 0:4 * CHUNK].rearrange("p (b v) -> p b v", v=CHUNK),
                                                  ALU.add).then_inc(predict_added, 1)
                        if c < NCHUNK - 1:
                            step.link(vec.tensor_tensor(SDEC[:, :, :], SH[:, c, :, :],
                                                        PEND[:, :, c].unsqueeze(2).to_broadcast([P, 4, CHUNK]), ALU.mult))
                            vec.wait_ge(state_mm, c + 1)
                            vec.tensor_tensor(SH[:, c + 1, :, :], SDEC[:, :, :],
                                              BANK[3][:, 0:4 * CHUNK].rearrange("p (b v) -> p b v", v=CHUNK),
                                              ALU.add).then_inc(state_ready, 1)
                            vec.wait_ge(state_ready, c + 1)
                    for b in range(4):
                        vec.wait_ge(out_mm, b + 1)
                        vec.tensor_tensor(YF[:, b, :], BANK[4 + b][:, :], YI[:, b, :], ALU.add).then_inc(out_read, 1)
                    for b in range(4):
                        vec.wait_ge(mean_mm, b + 1)
                        vec.wait_ge(out_read, b + 1)
                        vec.scalar_tensor_tensor(DF[:, b, :], BANK[b][:, :], -1.0 / CHUNK, YF[:, b, :],
                                                 ALU.mult, ALU.add).then_inc(dev_ready, 1)
                    vec.wait_ge(ya_hi, 1)
                    vec.tensor_tensor(MIX_LO[:, 0:4, :], YA[:, :, :], MIX_HI[:, 0:4, :].bitcast(F32), ALU.subtract).then_inc(ya_lo, 1)
                    vec.wait_ge(decay_ready, 1)
                    for b in range(4):
                        step.link(vec.tensor_tensor(DF[:, b, :], DF[:, b, :], TMPQ[:, b, :], ALU.mult))
                        step.link(vec.scalar_tensor_tensor(DF[:, b, :], DF[:, b, :], par("rwkv_ln_w", b), BV[:, b, :], ALU.mult, ALU.add))
                        vec.wait_ge(g_mm, b + 1)
                        vec.scalar_tensor_tensor(YF[:, b, :], DF[:, b, :], par("rwkv_ln_b", b), BANK[b][:, :],
                                                 ALU.add, ALU.mult).then_inc(mixed_ready, 1)
                    for b in range(4):
                        vec.wait_ge(mixed_hi, b + 1)
                        vec.tensor_tensor(MIX_LO[:, 4 + b, :], YF[:, b, :], MIX_HI[:, 4 + b, :].bitcast(F32),
                                          ALU.subtract).then_inc(mixed_lo, 1)
                    vec.wait_ge(mixed_lo, 4)
                    vec.wait_ge(ya_lo, 1)
                    vec.sem_inc(mixer_done[phase], 1)
                if phase == "c":
                    n, u0, q0 = norm_of[phase], base[phase], inv_base[phase]
                    vec.wait_ge(h_ready[1], KB // 2 * (n + 1))
                    vec.wait_ge(sum_ready, n + 1)
                    vec.memset(PAD[:, :, 0:3], 0.0).then_inc(pad_zero, 1)
                    vec.wait_ge(pad_zero, used["pad_zero"] + 1)
                    vec.wait_ge(c_tail_hi, 1)
                    vec.tensor_tensor(CTS[:, 1, :, :], CT[:, :, :], CTS[:, 0, :, :].bitcast(F32), ALU.subtract).then_inc(c_tail_lo, 1)
                    for t in range(C_BLOCKS):
                        step.wait()
                        vec.wait_ge(unit_done, u0 + t + 1)
                        if t < 24:
                            pad = PAD[:, t % 2, :]
                            z = pad[:, 3:3 + SEQ]
                            if t >= 2:
                                vec.wait_ge(conv_ready, used["conv_ready"] + t - 1)
                        else:
                            z = GC_[:, t - 24, :]
                        vec.tensor_tensor(z, BANK[t % 2][:, :], RSTD[:, :], ALU.mult).then_inc(z_read, 1)
                        if t + 2 < C_BLOCKS:
                            split_lo(u0 + t + 2, 0)
                        if t < 24:
                            vec.wait_ge(z_read, used["z_read"] + t + 1)
                            dst = (QC, KC, VC)[t // 8][:, t % 8, :]
                            step.link(vec.tensor_scalar(dst, z, par("dn_conv_w", 72 + t), None, ALU.mult))
                            for k in (2, 1, 0):
                                ins = vec.scalar_tensor_tensor(dst, pad[:, k:k + SEQ], par("dn_conv_w", 24 * k + t), dst,
                                                               ALU.mult, ALU.add)
                                if k:
                                    step.link(ins)
                            ins.then_inc(conv_ready, 1)
                        if t >= 25:
                            unit_vectors(t - 25)
                    unit_vectors(7)
                    vec.wait_ge(small_mm, used["small_mm"] + 1)
                    for j in range(TT):
                        step.inc(vec.tensor_copy(RTOK[:, j:j + 1], BANK[6][:, 2 * j:2 * j + 1]))
                    step.wait()
                    for j in range(TT):
                        o = BANK[7][:, j * 16:(j + 1) * 16]
                        step.inc(vec.tensor_scalar(TL[:, 10, j, :], o[:, 0:HEADS], RTOK[:, j:j + 1], None, ALU.mult))
                        step.inc(vec.tensor_scalar(TL[:, 11, j, :], o[:, HEADS:], RTOK[:, j:j + 1], None, ALU.mult))
                    step.wait()
                    vec.sem_inc(tail_scaled, 1)
                    db = PARAMS["dn_dt_bias"][0]
                    vec.tensor_tensor(TL[:, 4], TL[:, 11], PRM[:, db:db + HEADS].unsqueeze(1).to_broadcast([P, TT, HEADS]),
                                      ALU.add).then_inc(tail_scaled, 1)
                    vec.sem_inc(z_read, 1)
                    vec.wait_ge(al_act, 1)
                    step.link(vec.tensor_scalar(TL[:, 7], TL[:, 6], 1.0, None, ALU.add))
                    vec.sem_inc(al_vec, 1)
                    step.link(vec.tensor_scalar(TL[:, 12], TL[:, 7], 1.0, None, ALU.subtract))
                    step.link(vec.tensor_scalar(TL[:, 13], TL[:, 12], 0.0, None, ALU.is_equal))
                    step.link(vec.tensor_tensor(TL[:, 12], TL[:, 12], TL[:, 13], ALU.add))
                    step.link(vec.reciprocal(TL[:, 14], TL[:, 12]))
                    vec.wait_ge(al_act, 2)
                    step.link(vec.tensor_tensor(TL[:, 15], TL[:, 8], TL[:, 13], ALU.add))
                    step.link(vec.tensor_tensor(TL[:, 15], TL[:, 15], TL[:, 6], ALU.mult))
                    step.link(vec.tensor_tensor(TL[:, 15], TL[:, 15], TL[:, 14], ALU.mult))
                    vec.wait_ge(tail_scaled, 2)
                    step.link(vec.tensor_scalar(TL[:, 16], TL[:, 4], 0.0, None, ALU.max))
                    step.link(vec.tensor_tensor(TL[:, 15], TL[:, 15], TL[:, 16], ALU.add))
                    vec.wait_ge(al_act, 3)
                    vec.scalar_tensor_tensor(TL[:, 3], TL[:, 15], -1.0, TL[:, 9, 0:1, :].to_broadcast([P, TT, HEADS]),
                                             ALU.mult, ALU.mult).then_inc(decay_ready, 1)
                    vec.wait_ge(gcum_mm, 1)
                    vec.tensor_copy(GSUM, BANK[7][:, 128:160].rearrange("p (t h) -> p t h", t=TT)).then_inc(gtok_ready, 1)
                    vec.wait_ge(gtok_ready, 1)
                    vec.tensor_tensor(KDEC, BANK[7][:, 192:224].rearrange("p (t h) -> p t h", t=TT), GSUM,
                                      ALU.subtract).then_inc(gtok_ready, 1)
                    for p in range(HEADS // 2):
                        q = q0 + p
                        for s in range(2):
                            h = 2 * p + s
                            vec.wait_ge(row_mm[s], 2 * p + 1)
                            if p:
                                vec.wait_ge(qk_scaled[s], 2 * p)
                            vec.tensor_tensor(KBETA[:, s, :], BANK[4 * s][:, :], KC[:, h, :], ALU.mult).then_inc(kbeta_ready[s], 1)
                            vec.wait_ge(row_mm[s], 2 * p + 2)
                            if p:
                                vec.wait_ge(att_ready[s], p)
                            for j in range(TT):
                                ins = vec.tensor_scalar(DT[:, s, j, :], BANK[4 * s + 1][:, j * P:(j + 1) * P],
                                                        GSUM[:, j, h:h + 1], 0.0, ALU.subtract, ALU.min)
                            ins.then_inc(dd_ready[s], 1)
                        for s in range(2):
                            h = 2 * p + s
                            vec.wait_ge(dmask_ready[s], p + 1)
                            vec.wait_ge(kq_mm[s], 2 * p + 1)
                            if q:
                                vec.wait_ge(tm_ready[s], 5 * q)
                            vec.tensor_tensor(INV[s]["TT"][:, :, :], BANK[4 * s + 2][:, :].rearrange("p (t c) -> p t c", t=TT),
                                              DS[:, s], ALU.mult).then_inc(mat_ready[s], 1)
                            vec.wait_ge(kq_mm[s], 2 * p + 2)
                            vec.tensor_tensor(ATT[:, h], BANK[4 * s + 3][:, :].rearrange("p (t c) -> p t c", t=TT),
                                              DT[:, s], ALU.mult).then_inc(att_ready[s], 1)
                            vec.wait_ge(erow_ready[s], p + 1)
                            step.link(vec.tensor_copy(CD[:, h, :], EROW[:, s, :].rearrange("p (c k) -> p c k", k=CHUNK)[:, :, CHUNK - 1]))
                            vec.tensor_tensor(QC[:, h, :], QC[:, h, :], EROW[:, s, :], ALU.mult).then_inc(qk_scaled[s], 1)
                            vec.wait_ge(token_mm[s], used["token_mm"] + 2 * p + 1)
                            vec.wait_ge(kbeta_ready[s], p + 1)
                            vec.tensor_tensor(KC[:, h, :], KBETA[:, s, :], EROW[:, s, :], ALU.mult).then_inc(qk_scaled[s], 1)
                        vec_inverse(q)
                    for s in range(2):
                        vec.wait_ge(token_mm[s], used["token_mm"] + 8)
                    step.link(vec.memset(SC[:, 0, :, :], 0.0))
                    for c in range(NCHUNK):
                        j, th = c // 2, slice(c % 2 * CHUNK, (c % 2 + 1) * CHUNK)
                        if c:
                            for g in range(2):
                                vec.wait_ge(predict_mm, used["predict_mm"] + 2 * (c - 1) + g + 1)
                                if c == 1:
                                    for s in range(2):
                                        vec.wait_ge(token_read[s], used["token_read"] + 8)
                                v = VTK[th, 4 * g:4 * g + 4, j, :]
                                vec.tensor_tensor(v, v, BANK[g][th, :].rearrange("p (h v) -> p h v", h=4),
                                                  ALU.subtract).then_inc(predict_added, 1)
                        if c < NCHUNK - 1:
                            for g in range(2):
                                vec.wait_ge(state_mm, used["state_mm"] + 2 * c + g + 1)
                                if c:
                                    vec.wait_ge(out_mm, used["out_mm"] + c)
                                for h in range(4 * g, 4 * g + 4):
                                    ins = vec.scalar_tensor_tensor(SC[:, (c + 1) % 2, h, :], SC[:, c % 2, h, :], CD[:, h, c:c + 1],
                                                                   BANK[4 + g][:, h % 4 * P:(h % 4 + 1) * P], ALU.mult, ALU.add)
                                ins.then_inc(state_ready, 1)
                            vec.wait_ge(state_ready, used["state_ready"] + 2 * c + 2)
                    for h in range(HEADS):
                        vec.wait_ge(orn_ready, h + 1)
                        rn = (DT if h % 4 < 2 else DS)[:, h % 2].rearrange("p t c -> p (t c)")
                        step.link(vec.scalar_tensor_tensor(KC[:, h, :], KC[:, h, :], par("dn_norm"), rn, ALU.mult, ALU.mult))
                        vec.wait_ge(gate_c, h + 1)
                        vec.tensor_tensor(KC[:, h, :], KC[:, h, :], GC_[:, h, :], ALU.mult).then_inc(mixed_ready, 1)
                        if h:
                            vec.wait_ge(mixed_hi, used["mixed_hi"] + h)
                            vec.tensor_tensor(MIX_LO[:, h - 1, :], KC[:, h - 1, :], MIX_HI[:, h - 1, :].bitcast(F32),
                                              ALU.subtract).then_inc(mixed_lo, 1)
                    vec.wait_ge(mixed_hi, used["mixed_hi"] + HEADS)
                    vec.tensor_tensor(MIX_LO[:, HEADS - 1, :], KC[:, HEADS - 1, :], MIX_HI[:, HEADS - 1, :].bitcast(F32),
                                      ALU.subtract).then_inc(mixed_lo, 1)
                    vec.wait_ge(mixed_lo, used["mixed_lo"] + HEADS)
                    vec.sem_inc(mixer_done[phase], 1)
                if phase in ("ab", "c"):
                    c0 = base[phase] + (AB_BLOCKS if phase == "ab" else C_BLOCKS)
                    split_lo(c0, 0)
                    split_lo(c0 + 1, 0)
                    for m in range(KB):
                        residual_add(norm_of[phase] + 1, m // 2, m % 2, DOWN[m % 2], 1.0, c0 + m + 1)
                        if c0 + m + 2 < n_units:
                            split_lo(c0 + m + 2, 0)
                        if norm_of[phase] + 1 < n_norms - 1:
                            residual_split(norm_of[phase] + 1, m // 2, m % 2)
            n = n_norms - 1
            inverse_root(n)
            vec.wait_ge(rstd_ready, n + 1)
            for m in range(KB):
                w = norm_cols[n] + m
                vec.scalar_tensor_tensor(HF[:, m, :], X[:, m, :], PRM[:, w:w + 1], RSTD[:, :],
                                         ALU.mult, ALU.mult).then_inc(out_ready, 1)


def kernel(**inputs):
    import numpy as _np
    import concourse.bacc as _bacc
    from concourse import mybir as _mybir
    from concourse.bass_utils import run_bass_kernel_spmd as _run

    arrays = layout(inputs)
    nc = _bacc.Bacc("TRN2", target_bir_lowering=False, num_devices=1)
    args = [nc.dram_tensor(f"in_{k}", a.shape, _mybir.dt.from_np(a.dtype), kind="ExternalInput").ap()
            for k, a in arrays.items()]
    args.append(nc.dram_tensor("out_0_dram", (KB, P, SEQ), _mybir.dt.float32, kind="ExternalOutput").ap())
    hybrid_trunk_kernel(nc, *args)
    r = _run(nc, [{f"in_{k}": a for k, a in arrays.items()}], core_ids=[0])
    got = r.results[0]["out_0_dram"]
    return _np.ascontiguousarray(got.reshape(D_MODEL, SEQ).transpose(1, 0)).reshape(1, SEQ, D_MODEL)
```

```python
from contextlib import ExitStack, contextmanager

import concourse.bass as bass
import numpy as np
from concourse import mybir

ALU = mybir.AluOpType
ACT = mybir.ActivationFunctionType
F32 = mybir.dt.float32
F32R = mybir.dt.float32r

P = 128
SEQ = 512
D_MODEL = 1024
D_FF = 2816
KB = D_MODEL // P
FB = D_FF // P
HALF_FB = FB // 2
AB_BLOCKS = 22
C_BLOCKS = 32
AB_ORDER = [*range(8), 20, 21, *range(12, 20), *range(8, 12)]
CHUNK = 64
NCHUNK = SEQ // CHUNK
TT = SEQ // P
HEADS = 8
RING = 4
SPLIT = 2
UNIT = HALF_FB * P
EPS = 1e-6
DECAY_C = float(np.exp(-0.5))

PARAMS = {}


def _param(name, n, _at=[0]):
    PARAMS[name] = (_at[0], n)
    _at[0] += n


for _name, _n in [
    ("ffn_norm", 4 * KB), ("mix_norm", 2 * KB), ("final_norm", KB),
    ("lru_conv_w", 16), ("lru_conv_b", 4), ("lru_gate_a_b", 4), ("lru_gate_x_b", 4), ("lru_a_param", 4),
    ("rwkv_mu", 14), ("rwkv_w0", 4), ("rwkv_a0", 4), ("rwkv_k_k", 4), ("rwkv_k_a", 4), ("rwkv_r_k", 4),
    ("rwkv_ln_w", 4), ("rwkv_ln_b", 4), ("dn_conv_w", 96), ("dn_norm", 1), ("dn_A_log", 8), ("dn_dt_bias", 8),
]:
    _param(_name, _n)
NPARAM = sum(n for _, n in PARAMS.values())

CONSTS = ["ident", "ones", "ones_half", "upper", "strict", "pair1", "pair2", "pair4", "pair8", "pair16", "pair32"]
NCONST = len(CONSTS) * P + SEQ


def constants():
    s, t = np.meshgrid(np.arange(P), np.arange(P), indexing="ij")
    same = s // CHUNK == t // CHUNK
    mats = [s == t, s == s, same, same & (s <= t), same & (s < t)]
    for m in (1, 2, 4, 8, 16, 32):
        mats.append((s // (2 * m) == t // (2 * m)) & (s // m % 2 == 0) & (t // m % 2 == 1))
    restart = np.broadcast_to((np.arange(SEQ) % CHUNK != 0)[None, :], (P, SEQ))
    return np.ascontiguousarray(np.concatenate([*mats, restart], axis=1).astype(np.float32))


class Steps:

    def __init__(self, eng, sem):
        self.eng, self.sem, self.base, self.n = eng, sem, 0, 0

    def inc(self, ins):
        ins.then_inc(self.sem, 1)
        self.n += 1

    def wait(self):
        self.eng.wait_ge(self.sem, self.base + self.n)

    def link(self, ins):
        self.inc(ins)
        self.wait()


def layout(inputs):
    v = {k: np.asarray(a) for k, a in inputs.items()}

    def cols(a):
        return a.reshape(-1, P).transpose(1, 0)

    def blocks(w):
        k, n = w.shape
        return np.ascontiguousarray(w.reshape(k // P, P, n // P, P).transpose(2, 1, 0, 3)).reshape(n // P, P, k)

    packed = {
        "ffn_norm": cols(v["ffn_norm"]), "mix_norm": cols(v["mix_norm"]), "final_norm": cols(v["final_norm"]),
        "lru_conv_w": cols(v["lru_conv_w"]), "lru_conv_b": cols(v["lru_conv_b"]),
        "lru_gate_a_b": cols(v["lru_gate_a_b"]), "lru_gate_x_b": cols(v["lru_gate_x_b"]),
        "lru_a_param": cols(v["lru_a_param"]), "rwkv_mu": cols(v["rwkv_mu"]), "rwkv_w0": cols(v["rwkv_w0"]),
        "rwkv_a0": cols(v["rwkv_a0"]), "rwkv_k_k": cols(v["rwkv_k_k"]), "rwkv_k_a": cols(v["rwkv_k_a"]),
        "rwkv_r_k": cols(v["rwkv_r_k"]), "rwkv_ln_w": cols(v["rwkv_ln_w"]), "rwkv_ln_b": cols(v["rwkv_ln_b"]),
        "dn_conv_w": cols(v["dn_conv_w"]), "dn_norm": cols(v["dn_norm"]),
        "dn_A_log": np.broadcast_to(v["dn_A_log"], (P, HEADS)),
        "dn_dt_bias": np.broadcast_to(v["dn_dt_bias"], (P, HEADS)),
    }
    params = np.empty((P, NPARAM), np.float32)
    for name, (c, n) in PARAMS.items():
        params[:, c:c + n] = packed[name]
    gate, up = (np.stack([blocks(w) for w in v[k].reshape(4, D_MODEL, D_FF)]) for k in ("ffn_w_gate", "ffn_w_up"))
    down = np.stack([blocks(w) for w in v["ffn_w_down"].reshape(4, D_FF, D_MODEL)])
    lru_a, lru_x = (np.ascontiguousarray(v[k][0].reshape(4, 2, 64, 64).transpose(1, 2, 0, 3))
                    for k in ("lru_gate_a_w", "lru_gate_x_w"))
    c_w = v["c_w_in"][0]
    return {
        "x": np.ascontiguousarray(v["x"][0].reshape(SEQ, KB, P).transpose(2, 1, 0)),
        "params": params, "const": constants(),
        "w_gate": gate, "w_up": up, "w_down": down,
        "ab_in": blocks(v["ab_w_in"][0])[AB_ORDER], "ab_out": blocks(v["ab_w_out"][0]),
        "lru_a": lru_a, "lru_x": lru_x,
        "rwkv_wa": np.concatenate([v["rwkv_w2"][0], v["rwkv_a2"][0]], axis=0), "rwkv_g": v["rwkv_g2"][0],
        "c_in": blocks(c_w[:, :C_BLOCKS * P]),
        "c_tail": np.ascontiguousarray(c_w[:, C_BLOCKS * P:].reshape(KB, P, 2 * HEADS).transpose(1, 0, 2)),
        "c_out": blocks(v["c_w_out"][0]),
    }


def hybrid_trunk_kernel(nc, x, params, const, w_gate, w_up, w_down, ab_in, ab_out, lru_a, lru_x,
                        rwkv_wa, rwkv_g, c_in, c_tail, c_out, out, plan=("ffn0", "ab", "ffn1", "ffn2", "c", "ffn3")):
    units, base = [], {}
    for phase in plan:
        base[phase] = len(units)
        if phase.startswith("ffn"):
            n = int(phase[3])
            for f in range(FB):
                units += [(w_gate[n, f], KB * P), (w_up[n, f], KB * P)]
            for m in range(KB):
                units += [(w_down[n, m, :, h * UNIT:(h + 1) * UNIT], UNIT) for h in range(2)]
        else:
            first, last, count = (ab_in, ab_out, AB_BLOCKS) if phase == "ab" else (c_in, c_out, C_BLOCKS)
            units += [(first[b], KB * P) for b in range(count)]
            units += [(last[m], KB * P) for m in range(KB)]
    n_units = len(units)
    norm_of = {phase: n for n, phase in enumerate(plan)}
    n_norms = len(plan) + 1
    norm_cols = []
    for phase in plan:
        if phase.startswith("ffn"):
            norm_cols.append(PARAMS["ffn_norm"][0] + int(phase[3]) * KB)
        else:
            norm_cols.append(PARAMS["mix_norm"][0] + (0 if phase == "ab" else KB))
    norm_cols.append(PARAMS["final_norm"][0])
    ffn_index = {phase: n for n, phase in enumerate(q for q in plan if q.startswith("ffn"))}

    with ExitStack() as ctx:
        arena_words = 53180
        ctx.enter_context(nc.sbuf_tensor("arena", [P, arena_words], F32))
        arena_at = nc.sbuf_base - 4 * arena_words

        def at(name, offset, shape, dtype=F32):
            words = int(np.prod(shape[1:]))
            assert offset + words <= arena_words, name
            return nc.alloc_sbuf_tensor_at(name, list(shape), dtype, offset=arena_at + 4 * offset)

        Q = 4 * SEQ
        X_AT = 0
        H_AT = X_AT + KB * SEQ
        ACT_AT = H_AT + 2 * KB * SEQ
        RAW_AT = ACT_AT + 2 * FB * SEQ
        WS_AT = RAW_AT + RING * UNIT
        TMP_AT = WS_AT + 2 * SPLIT * UNIT
        RSTD_AT = TMP_AT + 4 * SEQ
        ACC_AT = RSTD_AT + SEQ
        CONST_AT = ACC_AT + SEQ
        PARAM_AT = CONST_AT + NCONST

        X = at("X", X_AT, [P, KB, SEQ])
        H = at("H", H_AT, [P, 2, KB, SEQ], F32R)
        H_PARTS = (H[:, 0], H[:, 1])
        HF = at("HF", H_AT, [P, KB, SEQ])
        A = at("A", ACT_AT, [P, 2, FB, SEQ], F32R)
        RAW = at("RAW", RAW_AT, [P, RING, UNIT])
        WS = at("WS", WS_AT, [P, 2, SPLIT, UNIT], F32R)
        GS = at("GS", TMP_AT, [P, 2, SEQ])
        US = at("US", TMP_AT + 2 * SEQ, [P, 2, SEQ])
        RSTD = at("RSTD", RSTD_AT, [P, SEQ])
        ACC = at("ACC", ACC_AT, [P, SEQ])
        CST = at("CST", CONST_AT, [P, NCONST])
        PRM = at("PRM", PARAM_AT, [P, NPARAM])

        def con(name):
            i = CONSTS.index(name) * P
            return CST[:, i:i + P]

        def par(name, i=0):
            c = PARAMS[name][0] + i
            return PRM[:, c:c + 1]

        BANK = [ctx.enter_context(nc.psum_tensor(f"bank{i}", [P, SEQ], F32)) for i in range(8)]
        GATE, UP, DOWN, SQ = BANK[0:2], BANK[2:4], BANK[4:6], BANK[6]

        def sem(name):
            return ctx.enter_context(nc.semaphore(name))

        landed = sem("constants_landed")
        x_landed = [sem(f"x_landed{i}") for i in range(KB // 2)]
        w_landed = [sem(f"weights_landed{s}") for s in range(RING)]
        hi_ready = sem("weights_hi_ready")
        lo_ready = sem("weights_lo_ready")
        unit_done = sem("unit_done")


        def pair_of(name):
            return [sem(f"{name}{b}") for b in range(2)]

        gs_ready, us_ready, silu_ready = pair_of("gs_ready"), pair_of("us_ready"), pair_of("silu_ready")
        prod_ready, ahi_ready, act_ready = pair_of("prod_ready"), pair_of("ahi_ready"), pair_of("act_ready")
        x_ready, sq_ready, acc_ready = pair_of("x_ready"), pair_of("sq_ready"), pair_of("acc_ready")
        hw_ready, hhi_ready, h_ready = pair_of("hw_ready"), pair_of("hhi_ready"), pair_of("h_ready")
        sum_ready, rms_ready, rstd_ready = sem("sum_ready"), sem("rms_ready"), sem("rstd_ready")
        acc_clear = sem("acc_clear")
        out_ready, stored = sem("out_ready"), sem("stored")
        vec_step, act_step = sem("vec_step"), sem("act_step")

        block = ctx.enter_context(nc.Block())

        def fits(value):
            return not isinstance(value, int) or value > 0


        def quad(name, at_word):
            return at(name, at_word, [P, 4, SEQ])

        XC, GG = quad("XC", ACT_AT), quad("GG", ACT_AT + Q)
        RG, IG = quad("RG", ACT_AT + 2 * Q), quad("IG", ACT_AT + 3 * Q)
        LA, LU = quad("LA", ACT_AT + 4 * Q), quad("LU", ACT_AT + 5 * Q)
        SIG, AL = quad("SIG", ACT_AT), quad("AL", ACT_AT + 2 * Q)
        CUM, CPRE = quad("CUM", ACT_AT + 3 * Q), quad("CPRE", ACT_AT + 4 * Q)
        PINV = quad("PINV", ACT_AT + 5 * Q)
        LOW = at("LOW", ACT_AT + 7 * Q, [P, 2, SEQ])
        LW = at("LW", ACT_AT + 7 * Q + 2 * SEQ, [P, 2, 4, P])
        WA2 = at("WA2", ACT_AT + 6 * Q, [P, SEQ])
        KF, VF, RF = quad("KF", ACT_AT + 8 * Q), quad("VF", ACT_AT + 9 * Q), quad("RF", ACT_AT + 10 * Q)
        BV, T2, YI = quad("BV", H_AT + Q), quad("T2", H_AT + 2 * Q), quad("YI", H_AT + 3 * Q)
        KKSQ = quad("KKSQ", ACT_AT + 5 * Q)
        KH = quad("KH", H_AT + 3 * Q)
        KT, BT, VT, GT = (quad("KT", ACT_AT + 3 * Q), quad("BT", ACT_AT), quad("VT", ACT_AT + Q),
                          quad("GT", ACT_AT + 6 * Q))
        XTL, XTH = quad("XTL", ACT_AT + 5 * Q), quad("XTH", ACT_AT + 9 * Q)
        MBT = at("MBT", WS_AT, [P, HEADS, SEQ])
        SH = at("SH", ACT_AT + 2 * Q, [P, NCHUNK, 4, CHUNK])
        YF, DF = quad("YF", ACT_AT + 3 * Q), quad("DF", ACT_AT + 9 * Q)
        YA = quad("YA", H_AT)
        MIX_HI = at("MIX_HI", ACT_AT, [P, KB, SEQ], F32R)
        MIX_LO = at("MIX_LO", ACT_AT + 4 * Q, [P, KB, SEQ], F32R)
        INV = [{k: at(f"{k}{b}", RAW_AT + (5 * b + n) * SEQ, [P, TT, P]) for n, k in enumerate(("TT", "TM", "XX", "XT", "IU"))}
               for b in range(2)]
        TKM = [at(f"TKM{b}", TMP_AT + b * SEQ, [P, TT, P]) for b in range(2)]
        MKM = [at(f"MKM{b}", TMP_AT + (2 + b) * SEQ, [P, TT, P]) for b in range(2)]
        TMPQ = quad("TMPQ", TMP_AT)
        PAD = at("PAD", TMP_AT, [P, 2, 516])
        DIFF = at("DIFF", TMP_AT + 2 * 516, [P, SEQ])
        SPARE_AT = (PARAM_AT + NPARAM + 7) // 8 * 8
        G2 = at("G2", SPARE_AT, [P, SEQ])
        SMALL = at("SMALL", SPARE_AT + SEQ, [P, 16, 4])
        PEND = at("PEND", SPARE_AT + SEQ + 64, [P, 4, NCHUNK])
        SDEC = at("SDEC", SPARE_AT + SEQ + 96, [P, 4, CHUNK])
        LRU_SCALE = SMALL[:, 15, :]
        LRU_NSCALE = SMALL[:, 14, :]

        z_read = sem("z_read")
        small_weights, pad_zero = sem("small_weights"), sem("pad_zero")
        sp_act, sp_vec = sem("sp_act"), sem("sp_vec")
        conv_ready, silu_done, gate_mm, gate_read = sem("conv_ready"), sem("silu_done"), sem("gate_mm"), sem("gate_read")
        lru_sq, lru_u2, lru_root, ya_ready, ya_hi, ya_lo, ya_kept = (sem("lru_sq"), sem("lru_u2"), sem("lru_root"),
                                                            sem("ya_ready"), sem("ya_hi"), sem("ya_lo"), sem("ya_kept"))
        p_ready, low_ready, small_mm, low_read = sem("p_ready"), sem("low_ready"), sem("small_mm"), sem("low_read")
        cum_ready, exp_ready, kk_raw, kk_sq = sem("cum_ready"), sem("exp_ready"), sem("kk_raw"), sem("kk_sq")
        norm_sum_mm, ss_max, inv_norm_ready, bon_in, bon_mm = sem("norm_sum_mm"), sem("ss_max"), sem("inv_norm_ready"), sem("bon_in"), sem("bon_mm")
        bv_ready, fm_ready, tr_mm, tr_read = sem("bv_ready"), sem("fm_ready"), sem("tr_mm"), sem("tr_read")
        mat_mm, mat_ready, xt1_ready = pair_of("mat_mm"), pair_of("mat_ready"), pair_of("xt1_ready")
        x1_mm, x1_read, token_mm, token_read = pair_of("x1_mm"), pair_of("x1_read"), pair_of("token_mm"), pair_of("token_read")
        tm_ready, u_mm, iu_ready, xx_mm, xx_read = (pair_of("tm_ready"), pair_of("u_mm"), pair_of("iu_ready"),
                                                    pair_of("xx_mm"), pair_of("xx_read"))
        predict_mm, predict_added, solve_mm, solve_read, state_mm, state_ready = (sem("predict_mm"), sem("predict_added"), sem("solve_mm"), sem("solve_read"),
                                                    sem("state_mm"), sem("state_ready"))
        out_mm, out_read, mean_mm, dev_ready, out_sq_ready, out_sq_mm, decay_ready, g_mm, mixed_ready, mixed_hi, mixed_lo = (
            sem(k) for k in ("out_mm", "out_read", "mean_mm", "dev_ready", "out_sq_ready", "out_sq_mm", "decay_ready", "g_mm",
                             "mixed_ready", "mixed_hi", "mixed_lo"))
        pool_step = sem("pool_step")
        mixer_done = {"ab": sem("ab_core_done"), "c": sem("c_core_done")}

        def xt_of(h):
            return (XTL, XTH)[h // 4][:, h % 4, :].rearrange("p (t c) -> p t c", t=TT)

        QC, KC = at("QC", ACT_AT, [P, HEADS, SEQ]), at("KC", ACT_AT + 2 * Q, [P, HEADS, SEQ])
        VC, GC_ = at("VC", ACT_AT + 4 * Q, [P, HEADS, SEQ]), at("GATEC", ACT_AT + 6 * Q, [P, HEADS, SEQ])
        SQT = at("SQT", ACT_AT + 8 * Q, [P, 4, 2, SEQ])
        ATT = at("ATT", ACT_AT + 8 * Q, [P, HEADS, TT, P])
        DT, DS = at("DT", ACT_AT + 10 * Q, [P, 2, TT, P]), at("DS", ACT_AT + 10 * Q + 2 * SEQ, [P, 2, TT, P])
        KBETA, EROW = at("KBETA", TMP_AT, [P, 2, SEQ]), at("EROW", TMP_AT + 2 * SEQ, [P, 2, SEQ])
        XTC, KDT = at("XTC", H_AT, [P, HEADS, TT, P]), at("KDT", H_AT + 2 * Q, [P, HEADS, TT, P])
        VTK = at("VTK", WS_AT, [P, HEADS, TT, P])
        SC = at("SC", ACT_AT + 4 * Q, [P, 2, HEADS, P])
        CT = at("CT", SPARE_AT, [P, KB, 2 * HEADS])
        CTS = at("CTS", SPARE_AT + P, [P, 2, KB, 2 * HEADS], F32R)
        TL = at("TL", SPARE_AT + 3 * P, [P, 20, TT, HEADS])
        CD = at("CD", SPARE_AT + 3 * P + 640, [P, HEADS, NCHUNK])
        TF = at("TF", TMP_AT + 4 * SEQ - SEQ, [P, SEQ])
        BETA, GSUM, KDEC = TL[:, 0], TL[:, 1], TL[:, 2]

        tf_ready = sem("tail_scaled_features")
        c_tail_hi, c_tail_lo, sq_c, l2_done, gate_c = (sem(k) for k in (
            "c_tail_hi", "c_tail_lo", "sq_c", "l2_done", "gate_c"))
        tail_scaled, beta_ready, al_act, al_vec, gcum_mm, gtok_ready, kdec_ready, orn_ready = (sem(k) for k in (
            "tail_scaled", "beta_ready", "al_act", "al_vec", "gcum_mm", "gtok_ready", "kdec_ready", "orn_ready"))
        row_mm, kbeta_ready, dd_ready, erow_ready, dexp_ready, dmask_ready = (pair_of(k) for k in (
            "row_mm", "kbeta_ready", "dd_ready", "erow_ready", "dexp_ready", "dmask_ready"))
        kq_mm, att_ready, qk_scaled = (pair_of(k) for k in ("kq_mm", "att_ready", "qk_scaled"))
        inv_base = {"ab": 0, "c": HEADS // 2 if "ab" in plan else 0}
        mat_base = 4 * inv_base["c"]
        used = {k: v if "ab" in plan else 0 for k, v in (
            ("conv_ready", 4), ("silu_done", 4), ("norm_sum_mm", 4), ("inv_norm_ready", 1), ("small_mm", 8), ("decay_ready", 1), ("predict_mm", 14), ("predict_added", 14), ("solve_mm", 8), ("solve_read", 8), ("state_mm", 7), ("state_ready", 7), ("out_mm", 4), ("out_read", 4), ("out_sq_mm", 4), ("out_sq_ready", 4), ("mixed_ready", 4), ("mixed_hi", 4), ("mixed_lo", 4), ("token_mm", 8), ("token_read", 8), ("pad_zero", 2), ("small_weights", 96), ("z_read", 22))}

        def tiles(ap):
            return ap.unsqueeze(1).to_broadcast([P, TT, P])

        def flat(t):
            return t[:, :, :].rearrange("p a b -> p (a b)")

        def last_use(eng, phase):
            if phase.startswith("ffn"):
                for j in range(2):
                    eng.wait_ge(us_ready[j], (ffn_index[phase] + 1) * (FB // 2))
            else:
                eng.wait_ge(z_read, AB_BLOCKS if phase == "ab" else used["z_read"] + C_BLOCKS)

        @block.sync
        def _(sp):
            def load(u, slot, src, cols):
                if fits(u - RING + 1):
                    sp.wait_ge(lo_ready, u - RING + 1)
                sp.dma_start(RAW[:, slot, 0:cols], src).then_inc(w_landed[slot], 16)

            sp.dma_start(PRM[:, :], params).then_inc(x_landed[0], 16)
            for i in range(KB // 2):
                sp.dma_start(X[:, 2 * i:2 * i + 2, :], x[:, 2 * i:2 * i + 2, :]).then_inc(x_landed[i], 16)
                if i == 0:
                    load(0, 0, *units[0])
            sp.dma_start(CST[:, :], const).then_inc(landed, 16)
            for phase in plan:
                u0 = base[phase]
                if phase.startswith("ffn"):
                    n = int(phase[3])
                    for j in range(0 if u0 else 1, 4):
                        load(u0 + j, (u0 + j) % RING, *units[u0 + j])
                    with sp.Fori(1, FB // 2) as i:
                        for j in range(4):
                            src = (w_gate, w_up)[j % 2][n, 2 * i + j // 2]
                            load(u0 + 4 * i + j, (u0 + j) % RING, src, KB * P)
                    u1 = u0 + 2 * FB
                    with sp.Fori(0, KB // 2) as i:
                        for j in range(4):
                            src = w_down[n, 2 * i + j // 2, :, (j % 2) * UNIT:(j % 2 + 1) * UNIT]
                            load(u1 + 4 * i + j, (u1 + j) % RING, src, UNIT)
                else:
                    count = AB_BLOCKS if phase == "ab" else C_BLOCKS
                    for j in range(0 if u0 else 1, count + KB):
                        if phase == "ab" and j == RING:
                            sp.wait_ge(unit_done, u0)
                            for half in range(2):
                                rows = slice(half * CHUNK, (half + 1) * CHUNK)
                                sp.wait_ge(pad_zero, 1)
                                for k, w in enumerate((lru_a, lru_x)):
                                    sp.dma_start(LW[rows, k, :, rows], w[half]).then_inc(small_weights, 16)
                            sp.dma_start(WA2[:, :], rwkv_wa).then_inc(small_weights, 16)
                            sp.dma_start(G2[:, :], rwkv_g).then_inc(small_weights, 16)
                        if phase == "c" and j == RING:
                            sp.wait_ge(unit_done, u0)
                            sp.dma_start(CT[:, :, :], c_tail).then_inc(small_weights, 16)

                        if j == count:
                            for s in range(2):
                                sp.wait_ge(xx_mm[s], 9 * (inv_base[phase] + HEADS // 2))
                        load(u0 + j, (u0 + j) % RING, *units[u0 + j])
            for m in range(KB):
                sp.wait_ge(out_ready, m + 1)
                sp.dma_start(out[m], HF[:, m, :]).then_inc(stored, 16)
            sp.wait_ge(stored, 16 * KB)


        @block.tensor
        def _(pe):
            def unit(bank, c, i, src, rows, first, last, norm=None, ready=None, at_col=0, done=True):
                s = c % SPLIT
                pe.wait_ge(lo_ready, c + 4 * i + 1)
                for j, r in enumerate(rows):
                    cols = slice((at_col + j) * P, (at_col + j + 1) * P)
                    if norm is not None:
                        pe.wait_ge(h_ready[r % 2], KB // 2 * norm + r // 2 + 1)
                    if ready is not None:
                        ready(r)
                    pe.matmul(bank[:, :], WS[:, 0, s, cols], src[0][:, r, :], start=first and j == 0, stop=False)
                    pe.matmul(bank[:, :], WS[:, 0, s, cols], src[1][:, r, :], start=False, stop=False)
                    mm = pe.matmul(bank[:, :], WS[:, 1, s, cols], src[0][:, r, :],
                                   start=False, stop=last and j == len(rows) - 1)
                if done:
                    mm.then_inc(unit_done, 1)

            def first_two(phase, banks):
                c, n = base[phase], norm_of[phase]
                for k in range(2):
                    unit(banks[k], c + k, 0, H_PARTS, range(KB - 1), True, False, norm=n, done=False)
                for k in range(2):
                    unit(banks[k], c + k, 0, H_PARTS, [KB - 1], False, True, norm=n, at_col=KB - 1)
                    if k == 0:
                        norm_sum(n)

            def norm_sum(n):
                if n == 0:
                    pe.wait_ge(landed, 16)
                pe.wait_ge(acc_ready[0], 4 * (n + 1))
                pe.wait_ge(acc_ready[1], 3 * (n + 1))
                pe.wait_ge(sq_ready[1], 4 * (n + 1))
                if n:
                    pe.wait_ge(rms_ready, n)
                pe.matmul(SQ[:, :], con("ones"), ACC[:, :], start=True, stop=False)
                pe.matmul(SQ[:, :], con("ones"), US[:, 1, :], start=False, stop=True).then_inc(sum_ready, 1)

            def ffn_up(phase, i, j):
                q = ffn_index[phase] * (FB // 2)
                c = base[phase] + 2 * j
                if fits(q + i):
                    pe.wait_ge(gs_ready[j], q + i)
                unit(GATE[j], c, i, H_PARTS, range(KB), True, True)
                if fits(q + i):
                    pe.wait_ge(us_ready[j], q + i)
                unit(UP[j], c + 1, i, H_PARTS, range(KB), True, True)

            def ffn_down(phase, i, j, first=False):
                c = base[phase] + 2 * FB + 2 * j
                pe.wait_ge(x_ready[j], KB // 2 * (norm_of[phase] + 1) + i)
                for k in range(2):
                    if first:
                        for b in range(2):
                            pe.wait_ge(act_ready[b], ffn_index[phase] * (FB // 2) + (HALF_FB + 1 - b) // 2 if k == 0
                                       else (ffn_index[phase] + 1) * (FB // 2))
                    unit(DOWN[j], c + k, i, (A[:, 0], A[:, 1]), range(k * HALF_FB, (k + 1) * HALF_FB), k == 0, k == 1)


            def pe_first_inverse(q):
                for s in range(2):
                    pe.wait_ge(xt1_ready[s], q + 1)
                    for j in range(TT):
                        tr = pe.transpose(BANK[4 * s][:, j * P:(j + 1) * P], INV[s]["XT"][:, j, :], con("ident"))
                    tr.then_inc(x1_mm[s], 1)

            def pe_inverse_level(q, l, masked, gy=0):
                for s in range(2):
                    pe.wait_ge(tm_ready[s], 5 * q + l + 1)
                    if l == 0:
                        pe.wait_ge(x1_read[s], q + 1)
                        pe.wait_ge(mat_ready[s], masked)
                    else:
                        pe.wait_ge(xx_read[s], 9 * q + 2 * l)
                    for j in range(TT):
                        mm = pe.matmul(BANK[4 * s + 3][:, j * P:(j + 1) * P], INV[s]["TM"][:, j, :], INV[s]["XX"][:, j, :],
                                       start=True, stop=True)
                    mm.then_inc(u_mm[s], 1)
                for s in range(2):
                    pe.wait_ge(iu_ready[s], 5 * q + l + 1)
                    if l == 0 and gy:
                        pe.wait_ge(token_read[s], gy)
                    if l < 4:
                        for j in range(TT):
                            mm = pe.matmul(BANK[4 * s][:, j * P:(j + 1) * P], INV[s]["XT"][:, j, :], INV[s]["IU"][:, j, :],
                                           start=True, stop=True)
                        mm.then_inc(xx_mm[s], 1)
                    for j in range(TT):
                        mm = pe.matmul(BANK[4 * s + 1][:, j * P:(j + 1) * P], INV[s]["IU"][:, j, :], INV[s]["XT"][:, j, :],
                                       start=True, stop=True)
                    mm.then_inc(xx_mm[s], 1)

            def mix_out(phase, ready):
                count = AB_BLOCKS if phase == "ab" else C_BLOCKS
                for m in range(KB):
                    pe.wait_ge(x_ready[m % 2], KB // 2 * (norm_of[phase] + 1) + m // 2)
                    unit(DOWN[m % 2], base[phase] + count + m, 0, (MIX_HI, MIX_LO), range(KB), True, True,
                         ready=ready if m == 0 else None)

            for phase in plan:
                if phase.startswith("ffn"):
                    q = ffn_index[phase] * (FB // 2)
                    if q:
                        pe.wait_ge(gs_ready[0], q)
                        pe.wait_ge(us_ready[0], q)
                    first_two(phase, (GATE[0], UP[0]))
                    ffn_up(phase, 0, 1)
                    with pe.Fori(1, FB // 2) as i:
                        for j in range(2):
                            ffn_up(phase, i, j)
                    ffn_down(phase, 0, 0, first=True)
                    ffn_down(phase, 0, 1)
                    with pe.Fori(1, KB // 2) as i:
                        for j in range(2):
                            ffn_down(phase, i, j)

                if phase == "ab":
                    n, u0 = norm_of[phase], base[phase]
                    for t in range(AB_BLOCKS):
                        if t >= 2:
                            pe.wait_ge(z_read, t - 1)
                        unit(BANK[t % 2], u0 + t, 0, H_PARTS, range(KB), True, True, norm=n if t == 0 else None)
                        if t == 0:
                            norm_sum(n)
                        if t in (8, 10):
                            k = (t - 8) // 2
                            pe.wait_ge(conv_ready, 4)
                            pe.wait_ge(small_weights, 16 * 6)
                            if k:
                                pe.wait_ge(gate_read, 4)
                            for b in range(4):
                                pe.matmul(BANK[2 + b][:, :], LW[:, k, b, :], XC[:, b, :],
                                          start=True, stop=True).then_inc(gate_mm, 1)
                        if t >= AB_BLOCKS - 2:
                            k = t - (AB_BLOCKS - 2)
                            rows = slice(k * CHUNK, (k + 1) * CHUNK)
                            pe.wait_ge(low_ready, 1)
                            for b in range(4):
                                pe.wait_ge(gate_read if k == 0 else low_read, 8 if k == 0 else b + 1)
                                pe.matmul(BANK[2 + b][:, :], WA2[rows, b * P:(b + 1) * P], LOW[rows, 0, :],
                                          start=True, stop=True).then_inc(small_mm, 1)
                    for b in range(4):
                        pe.wait_ge(z_read, AB_BLOCKS)
                        pe.wait_ge(kk_sq, 4)
                        pe.matmul(BANK[(6, 7, 0, 1)[b]][:, :], con("ones_half"), KKSQ[:, b, :], start=True, stop=True).then_inc(norm_sum_mm, 1)
                    for b in range(4):
                        pe.wait_ge(low_read, 5 + b)
                        pe.wait_ge(bon_in, b + 1)
                        pe.matmul(BANK[2 + b][:, :], con("ones_half"), T2[:, b, :], start=True, stop=True).then_inc(bon_mm, 1)
                    for k, (src, need) in enumerate(((VF, 0), (KH, 3), (PINV, 6))):
                        if need:
                            pe.wait_ge(fm_ready, need)
                        else:
                            pe.wait_ge(p_ready, 14)
                            pe.wait_ge(ss_max, 4)
                        for j in range(TT):
                            if 4 * k + j >= 2:
                                pe.wait_ge(tr_read, 4 * k + j - 1)
                            else:
                                pe.wait_ge(z_read, AB_BLOCKS)
                            bank = BANK[(4 * k + j) % 2]
                            for b in range(4):
                                tr = pe.transpose(bank[:, b * P:(b + 1) * P], src[:, b, j * P:(j + 1) * P], con("ident"))
                            tr.then_inc(tr_mm, 1)
                    pe.wait_ge(tr_read, 12)
                    pe.wait_ge(bv_ready, 4)

                    def matrices(h):
                        s, rows, b = h % 2, slice(h % 2 * CHUNK, (h % 2 + 1) * CHUNK), h // 2
                        if b:
                            pe.wait_ge(xx_read[s], 9 * b)
                            pe.wait_ge(token_read[s], 2 * b)
                        for k, (left, right) in enumerate(((AL, CPRE), (KF, CPRE), (KF, RF), (AL, RF))):
                            for j in range(TT):
                                c = slice(j * P, (j + 1) * P)
                                mm = pe.matmul(BANK[4 * s + k][:, c], left[rows, b, c], right[rows, b, c],
                                               start=True, stop=True)
                            mm.then_inc(mat_mm[s], 1)

                    def inside(h):
                        s, rows, b, w = h % 2, slice(h % 2 * CHUNK, (h % 2 + 1) * CHUNK), h // 2, slice(h * CHUNK, (h + 1) * CHUNK)
                        pe.wait_ge(mat_ready[s], 4 * b + 3)
                        for j in range(TT):
                            mm = pe.matmul(BANK[4 * s + 1][:, j * CHUNK:(j + 1) * CHUNK], TKM[s][:, j, :], VT[:, j, w],
                                           start=True, stop=True)
                        mm.then_inc(token_mm[s], 1)
                        for j in range(TT):
                            mm = pe.matmul(BANK[4 * s + 2][rows, j * P:(j + 1) * P], VT[:, j, w], MKM[s][:, j, :],
                                           start=True, stop=True)
                        mm.then_inc(token_mm[s], 1)

                    for p in range(HEADS // 2):
                        for s in range(2):
                            matrices(2 * p + s)
                        for s in range(2):
                            inside(2 * p + s)
                        pe_first_inverse(p)
                        for l in range(5):
                            pe_inverse_level(p, l, 4 * (p + 1), 2 * (p + 1))

                    def outputs(j, heads):
                        for h in heads:
                            b, rows, w = h // 2, slice(h % 2 * CHUNK, (h % 2 + 1) * CHUNK), slice(h * CHUNK, (h + 1) * CHUNK)
                            mm = pe.matmul(BANK[4 + b][rows, j * P:(j + 1) * P], GT[:, j, w],
                                           MBT[:, h, j * P:(j + 1) * P], start=True, stop=False, skip_group_check=True)
                            for c in (2 * j, 2 * j + 1):
                                if c:
                                    cc = slice(c * CHUNK, (c + 1) * CHUNK)
                                    mm = pe.matmul(BANK[4 + b][rows, cc], SH[rows, c, b, :], RF[rows, b, cc],
                                                   start=False, stop=c % 2 == 1, skip_group_check=True)
                            if j == TT - 1 and h % 2:
                                mm.then_inc(out_mm, 1)

                    for c in range(NCHUNK):
                        j, th = c // 2, slice(c % 2 * CHUNK, (c % 2 + 1) * CHUNK)
                        cc = slice(c * CHUNK, (c + 1) * CHUNK)
                        if c == 0:
                            for s in range(2):
                                pe.wait_ge(xx_read[s], 36)
                                pe.wait_ge(token_read[s], 8)
                        else:
                            pe.wait_ge(state_ready, c)
                            for s in range(2):
                                rows = slice(s * CHUNK, (s + 1) * CHUNK)
                                for b in range(4):
                                    mm = pe.matmul(BANK[s][th, b * CHUNK:(b + 1) * CHUNK], CPRE[rows, b, cc],
                                                   SH[rows, c, b, :], start=True, stop=True)
                                mm.then_inc(predict_mm, 1)
                        done = range(4 * (c % 2), 4 * (c % 2) + 4)
                        if c >= 2:
                            outputs(c // 2 - 1, done[:2])
                        if c:
                            pe.wait_ge(predict_added, 2 * c)
                        for h in range(HEADS):
                            w = slice(h * CHUNK, (h + 1) * CHUNK)
                            mm = pe.matmul(BANK[2][th, w], xt_of(h)[th, j, th], GT[th, j, w], start=True, stop=True)
                        mm.then_inc(solve_mm, 1)
                        if c >= 2:
                            outputs(c // 2 - 1, done[2:])
                        pe.wait_ge(solve_read, c + 1)
                        if c < NCHUNK - 1:
                            for h in range(HEADS):
                                w = slice(h * CHUNK, (h + 1) * CHUNK)
                                out_ = BANK[3][h % 2 * CHUNK:(h % 2 + 1) * CHUNK, h // 2 * CHUNK:(h // 2 + 1) * CHUNK]
                                pe.matmul(out_, KT[th, j, w], VT[th, j, w], start=True, stop=False)
                                mm = pe.matmul(out_, BT[th, j, w], GT[th, j, w], start=False, stop=True)
                            mm.then_inc(state_mm, 1)
                    outputs(TT - 1, range(HEADS))
                    pe.wait_ge(low_ready, 2)
                    for b in range(4):
                        pe.wait_ge(out_read, b + 1)
                        pe.matmul(BANK[b][:, :], con("ones_half"), YF[:, b, :], start=True, stop=True).then_inc(mean_mm, 1)
                    for b in range(4):
                        pe.wait_ge(out_sq_ready, b + 1)
                        pe.wait_ge(dev_ready, b + 1)
                        pe.matmul(BANK[4 + b][:, :], con("ones_half"), TMPQ[:, b, :], start=True, stop=True).then_inc(out_sq_mm, 1)
                    for b in range(4):
                        pe.matmul(BANK[b][:, :], G2[:, b * P:(b + 1) * P], LOW[:, 1, :], start=True, stop=True).then_inc(g_mm, 1)

                    def branch_split(r):
                        if r < 4:
                            pe.wait_ge(ya_lo, 1)
                        else:
                            pe.wait_ge(mixed_lo, r - 3)

                    pe.wait_ge(dev_ready, 4)
                    pe.wait_ge(decay_ready, 1)
                    mix_out(phase, branch_split)
                if phase == "c":
                    n, u0, q0 = norm_of[phase], base[phase], inv_base[phase]
                    def tail_products():
                        pe.wait_ge(c_tail_lo, 1)
                        pe.wait_ge(rms_ready, n + 1)
                        for k in range(KB):
                            for a, b in ((0, 0), (1, 0), (0, 1)):
                                mm = pe.matmul(BANK[6][0:2 * HEADS, :], CTS[:, b, k, :], H_PARTS[a][:, k, :],
                                               start=k == 0 and a == b, stop=k == KB - 1 and b == 1)
                        mm.then_inc(small_mm, 1)

                    def tail_token_major():
                        pe.wait_ge(tf_ready, 1)
                        for j in range(TT):
                            tr = pe.transpose(BANK[7][:, j * 16:(j + 1) * 16], TF[0:2 * HEADS, j * P:(j + 1) * P],
                                              con("ident")[0:2 * HEADS, 0:2 * HEADS])
                        tr.then_inc(small_mm, 1)

                    def decay_sums():
                        pe.wait_ge(decay_ready, used["decay_ready"] + 1)
                        flat_g = TL[:, 3].rearrange("p t h -> p (t h)")
                        pe.matmul(BANK[7][:, 128:160], con("upper"), flat_g, start=True, stop=True)
                        pe.matmul(BANK[7][:, 192:224], con("ones_half"), flat_g, start=True, stop=True).then_inc(gcum_mm, 1)

                    for t in range(C_BLOCKS):
                        if t >= 2:
                            pe.wait_ge(z_read, used["z_read"] + t - 1)
                        unit(BANK[t % 2], u0 + t, 0, H_PARTS, range(KB), True, True, norm=n if t == 0 else None)
                        if t == 0:
                            norm_sum(n)
                        h = (t - 13) // 2
                        if t >= 13 and t % 2 and h < HEADS:
                            for k in range(2):
                                if h >= 2:
                                    pe.wait_ge(inv_norm_ready, used["inv_norm_ready"] + 2 * (h - 1))
                                pe.wait_ge(sq_c, 2 * h + k + 1)
                                pe.matmul(BANK[2 + 2 * (h % 2) + k][:, :], con("ones"), SQT[:, h % 4, k, :],
                                          start=True, stop=True).then_inc(norm_sum_mm, 1)
                        if t == 26:
                            tail_products()
                        if t == 28:
                            tail_token_major()
                        if t == C_BLOCKS - 1:
                            decay_sums()
                    pe.wait_ge(inv_norm_ready, used["inv_norm_ready"] + 16)
                    pe.wait_ge(z_read, used["z_read"] + C_BLOCKS)
                    pe.wait_ge(gtok_ready, 2)

                    def rows(h, q):
                        s = h % 2
                        if q > q0:
                            pe.wait_ge(xx_read[s], 9 * q)
                            pe.wait_ge(att_ready[s], q - q0)
                        for k, (src, m) in enumerate(((BETA, "ident"), (TL[:, 3], "upper"))):
                            for j in range(TT):
                                mm = pe.matmul(BANK[4 * s + k][:, j * P:(j + 1) * P],
                                               src[:, j, h:h + 1].to_broadcast([P, P]), con(m), start=True, stop=True)
                            mm.then_inc(row_mm[s], 1)

                    def products(h, q):
                        s = h % 2
                        for k, (right, r) in enumerate(((KBETA, s), (QC, h))):
                            if k == 0:
                                pe.wait_ge(kbeta_ready[s], q - q0 + 1)
                            for j in range(TT):
                                c = slice(j * P, (j + 1) * P)
                                mm = pe.matmul(BANK[4 * s + 2 + k][:, c], KC[:, h, c], right[:, r, c], start=True, stop=True)
                            mm.then_inc(kq_mm[s], 1)

                    def token_major(h, q):
                        s = h % 2
                        for k, src in enumerate((KC, VC)):
                            if k == 0:
                                pe.wait_ge(kbeta_ready[s], q - q0 + 1)
                            else:
                                pe.wait_ge(dd_ready[s], q - q0 + 1)
                                pe.wait_ge(erow_ready[s], q - q0 + 1)
                            for j in range(TT):
                                c = slice(j * P, (j + 1) * P)
                                tr = pe.transpose(BANK[4 * s + k][:, c], src[:, h, c], con("ident"))
                            tr.then_inc(token_mm[s], 1)

                    pe.wait_ge(l2_done, 16)
                    pe.wait_ge(beta_ready, 1)
                    for p in range(HEADS // 2):
                        q = q0 + p
                        for s in range(2):
                            rows(2 * p + s, q)
                        for s in range(2):
                            products(2 * p + s, q)
                        for s in range(2):
                            token_major(2 * p + s, q)
                        for s in range(2):
                            pe.wait_ge(token_read[s], used["token_read"] + 2 * (p + 1))
                            pe.wait_ge(att_ready[s], p + 1)
                        pe_first_inverse(q)
                        for l in range(5):
                            pe_inverse_level(q, l, mat_base + p + 1)

                    for s in range(2):
                        pe.wait_ge(xx_read[s], 9 * (q0 + 4))
                        pe.wait_ge(qk_scaled[s], 8)
                        pe.wait_ge(dmask_ready[s], HEADS // 2)
                    def outputs(c, heads):
                        j, th = c // 2, slice(c % 2 * CHUNK, (c % 2 + 1) * CHUNK)
                        cc = slice(c * CHUNK, (c + 1) * CHUNK)
                        if c >= 2 and heads[0] == 0:
                            pe.wait_ge(out_read, used["out_read"] + c - 1)
                        for h in heads:
                            o = slice(h * CHUNK, (h + 1) * CHUNK)
                            if c:
                                pe.matmul(BANK[6 + c % 2][:, o], SC[:, c % 2, h, :], QC[:, h, cc], start=True, stop=False)
                            mm = pe.matmul(BANK[6 + c % 2][:, o], VTK[th, h, j, :], ATT[th, h, j, th], start=c == 0, stop=True)
                        if heads[-1] == HEADS - 1:
                            mm.then_inc(out_mm, 1)

                    for c in range(NCHUNK):
                        j, th = c // 2, slice(c % 2 * CHUNK, (c % 2 + 1) * CHUNK)
                        cc = slice(c * CHUNK, (c + 1) * CHUNK)
                        if c:
                            for g in range(2):
                                pe.wait_ge(state_ready, used["state_ready"] + 2 * (c - 1) + g + 1)
                                for h in range(4 * g, 4 * g + 4):
                                    mm = pe.matmul(BANK[g][th, h % 4 * P:(h % 4 + 1) * P], KC[:, h, cc], SC[:, c % 2, h, :],
                                                   start=True, stop=True)
                                mm.then_inc(predict_mm, 1)
                        if c:
                            outputs(c - 1, range(0, 4))
                        for g in range(2):
                            if c:
                                pe.wait_ge(predict_added, used["predict_added"] + 2 * (c - 1) + g + 1)
                            for h in range(4 * g, 4 * g + 4):
                                mm = pe.matmul(BANK[2 + g][th, h % 4 * P:(h % 4 + 1) * P], XTC[th, h, j, th], VTK[th, h, j, :],
                                               start=True, stop=True)
                            mm.then_inc(solve_mm, 1)
                        if c:
                            outputs(c - 1, range(4, HEADS))
                        for g in range(2):
                            pe.wait_ge(solve_read, used["solve_read"] + 2 * c + g + 1)
                            if c < NCHUNK - 1:
                                for h in range(4 * g, 4 * g + 4):
                                    mm = pe.matmul(BANK[4 + g][:, h % 4 * P:(h % 4 + 1) * P], KDT[th, h, j, :], VTK[th, h, j, :],
                                                   start=True, stop=True)
                                mm.then_inc(state_mm, 1)
                    outputs(NCHUNK - 1, range(HEADS))
                    for h in range(HEADS):
                        pe.wait_ge(out_sq_ready, used["out_sq_ready"] + h + 1)
                        if h >= 4:
                            pe.wait_ge(orn_ready, h - 3)
                        pe.matmul(BANK[h % 4][:, :], con("ones"), DT[:, :, :, :].rearrange("p a t c -> p a (t c)")[:, h % 2, :]
                                  if h % 4 < 2 else DS[:, :, :, :].rearrange("p a t c -> p a (t c)")[:, h % 2, :],
                                  start=True, stop=True).then_inc(out_sq_mm, 1)

                    def head_split(h):
                        pe.wait_ge(mixed_lo, used["mixed_lo"] + h + 1)

                    mix_out(phase, head_split)
            norm_sum(n_norms - 1)

        @block.scalar
        def _(act):
            def split_hi(c, i):
                cols = units[c][1]
                act.wait_ge(w_landed[c % RING], 16 * (c // RING + i + 1))
                if fits(c + 4 * i - SPLIT + 1):
                    act.wait_ge(unit_done, c + 4 * i - SPLIT + 1)
                act.activation(WS[:, 0, c % SPLIT, 0:cols], RAW[:, c % RING, 0:cols], ACT.Copy).then_inc(hi_ready, 1)

            def residual(n, i, j):
                act.wait_ge(x_ready[j], KB // 2 * n + i + 1)
                if j == 0 and fits(KB // 2 * n + i):
                    act.wait_ge(acc_ready[0], KB // 2 * n + i)
                if j == 1 and fits(3 * n + i):
                    act.wait_ge(acc_ready[1], 3 * n + i)
                    if n:
                        act.wait_ge(sum_ready, n)
                act.activation(US[:, j, :], X[:, 2 * i + j, :], ACT.Square).then_inc(sq_ready[j], 1)
                if n < n_norms - 1:
                    act.wait_ge(hw_ready[j], KB // 2 * n + i + 1)
                    act.activation(H[:, 0, 2 * i + j, :], GS[:, j, :], ACT.Copy).then_inc(hhi_ready[j], 1)

            def root(n):
                act.wait_ge(sum_ready, n + 1)
                if n:
                    last_use(act, plan[n - 1])
                act.activation(RSTD[:, :], SQ[:, :], ACT.Sqrt, bias=EPS, scale=1.0 / D_MODEL).then_inc(rms_ready, 1)

            def ffn_act(phase, i, j):
                q = ffn_index[phase] * (FB // 2) + i
                act.wait_ge(gs_ready[j], q + 1)
                act.activation(GS[:, j, :], GS[:, j, :], ACT.Silu).then_inc(silu_ready[j], 1)

            def ffn_hi(phase, i, j):
                q = ffn_index[phase] * (FB // 2) + i
                act.wait_ge(prod_ready[j], q + 1)
                act.activation(A[:, 0, 2 * i + j, :], US[:, j, :], ACT.Copy).then_inc(ahi_ready[j], 1)


            def act_inverse(q, finals):
                for s in range(2):
                    act.wait_ge(x1_mm[s], q + 1)
                    act.activation(INV[s]["XX"][:, :, :], BANK[4 * s][:, :].rearrange("p (t c) -> p t c", t=TT),
                                   ACT.Copy).then_inc(x1_read[s], 1)
                for l in range(5):
                    for s in range(2):
                        if l < 4:
                            act.wait_ge(xx_mm[s], 9 * q + 2 * l + 1)
                            act.activation(INV[s]["XX"][:, :, :], BANK[4 * s][:, :].rearrange("p (t c) -> p t c", t=TT),
                                           ACT.Copy).then_inc(xx_read[s], 1)
                        act.wait_ge(xx_mm[s], 9 * q + 2 * l + (2 if l < 4 else 1))
                        dst = INV[s]["XT"][:, :, :] if l < 4 else finals[s]
                        act.activation(dst, BANK[4 * s + 1][:, :].rearrange("p (t c) -> p t c", t=TT),
                                       ACT.Copy).then_inc(xx_read[s], 1)

            def act_gate(h):
                act.wait_ge(z_read, used["z_read"] + 24 + h + 1)
                act.activation(GC_[:, h, :], GC_[:, h, :], ACT.Silu).then_inc(gate_c, 1)

            step = Steps(act, act_step)
            act.wait_ge(x_landed[0], 32)
            for i in range(KB // 2):
                if i == 1:
                    split_hi(0, 0)
                if i == 3:
                    split_hi(1, 0)
                for j in range(2):
                    residual(0, i, j)
            for phase in plan:
                split_hi(base[phase] + 2, 0)
                root(norm_of[phase])
                if phase.startswith("ffn"):
                    def up(i, j, first=False):
                        if first:
                            split_hi(base[phase] + 3, 0)
                        else:
                            split_hi(base[phase] + 2 * j + 2, i)
                        ffn_act(phase, i, j)
                        if not first:
                            split_hi(base[phase] + 2 * j + 3, i)
                        ffn_hi(phase, i, j)

                    def down(i, j):
                        for k in range(2):
                            split_next(base[phase] + 2 * FB + 2 * j + 2 + k, i)
                        residual(norm_of[phase] + 1, i, j)

                    def split_next(c, i):
                        if isinstance(i, int):
                            c, i = c + 4 * i, 0
                        if not isinstance(i, int) or c < n_units:
                            split_hi(c, i)

                    up(0, 0, first=True)
                    up(0, 1)
                    with act.Fori(1, FB // 2 - 1) as i:
                        for j in range(2):
                            up(i, j)
                    i = FB // 2 - 1
                    up_last = base[phase] + 4 * i
                    for j in range(2):
                        split_hi(up_last + 2 * j + 2, 0)
                        ffn_act(phase, i, j)
                        split_hi(up_last + 2 * j + 3, 0)
                        ffn_hi(phase, i, j)
                    with act.Fori(0, KB // 2 - 1) as i:
                        for j in range(2):
                            down(i, j)
                    for j in range(2):
                        down(KB // 2 - 1, j)
                if phase == "ab":
                    n, u0 = norm_of[phase], base[phase]
                    ap = PRM[:, PARAMS["lru_a_param"][0]:PARAMS["lru_a_param"][0] + 4]
                    step.link(act.activation(SMALL[:, 0, :], ap, ACT.Abs))
                    act.activation(SMALL[:, 1, :], SMALL[:, 0, :], ACT.Exp, scale=-1.0).then_inc(sp_act, 1)
                    act.wait_ge(sp_vec, 1)
                    act.activation(SMALL[:, 3, :], SMALL[:, 2, :], ACT.Ln).then_inc(sp_act, 1)
                    for t in range(AB_BLOCKS):
                        if 0 < t < AB_BLOCKS - 2:
                            split_hi(u0 + t + 2, 0)
                        if 4 <= t < 8:
                            act.wait_ge(z_read, t + 1)
                            act.activation(GG[:, t - 4, :], PAD[:, t % 2, 3:3 + SEQ], ACT.Gelu_apprx_tanh).then_inc(silu_done, 1)
                        if t in (9, 11):
                            k = (t - 9) // 2
                            for b in range(4):
                                act.wait_ge(gate_mm, 4 * k + b + 1)
                                act.activation((RG, IG)[k][:, b, :], BANK[2 + b][:, :], ACT.Sigmoid,
                                               bias=par(("lru_gate_a_b", "lru_gate_x_b")[k], b)).then_inc(gate_read, 1)
                        if t == 13:
                            act.wait_ge(gate_read, 4)
                            act.wait_ge(sp_vec, 2)
                            for b in range(4):
                                step.inc(act.activation(LA[:, b, :], RG[:, b, :], ACT.Exp, scale=LRU_NSCALE[:, b:b + 1]))
                            for b in range(4):
                                step.inc(act.activation(LU[:, b, :], RG[:, b, :], ACT.Tanh, scale=LRU_SCALE[:, b:b + 1]))
                            step.wait()
                            act.activation(RG[:, :, :], LA[:, :, :], ACT.Square).then_inc(lru_sq, 1)
                        if t == 15:
                            act.wait_ge(lru_u2, 1)
                            act.activation(LU[:, :, :], LU[:, :, :], ACT.Sqrt).then_inc(lru_root, 1)
                    act.wait_ge(p_ready, 2)
                    act.activation(LOW[0:CHUNK, 0, :], LOW[0:CHUNK, 0, :], ACT.Tanh).then_inc(low_ready, 1)
                    act.activation(LOW[:, 1, :], LOW[:, 1, :], ACT.Sigmoid).then_inc(low_ready, 1)
                    act.wait_ge(ya_ready, 1)
                    for b in range(4):
                        act.activation(KKSQ[:, b, :], KF[:, b, :], ACT.Square, scale=par("rwkv_k_k", b)).then_inc(kk_sq, 1)
                    for k in range(2):
                        for b in range(4):
                            act.wait_ge(small_mm, 4 * k + b + 1)
                            act.activation((SIG, AL)[k][:, b, :], BANK[2 + b][:, :], ACT.Sigmoid,
                                           bias=par(("rwkv_w0", "rwkv_a0")[k], b)).then_inc(low_read, 1)
                    act.wait_ge(norm_sum_mm, 4)
                    act.wait_ge(cum_ready, 1)
                    act.activation(PINV[:, :, :], CUM[:, :, :], ACT.Exp, scale=DECAY_C).then_inc(exp_ready, 1)
                    act.wait_ge(exp_ready, 1)
                    act.wait_ge(cum_ready, 2)
                    act.activation(CUM[:, :, :], CUM[:, :, :], ACT.Exp, scale=-DECAY_C).then_inc(exp_ready, 1)
                    act.activation(CPRE[:, :, :], CPRE[:, :, :], ACT.Exp, scale=-DECAY_C).then_inc(exp_ready, 1)
                    act.wait_ge(ss_max, 4)
                    step.link(act.activation(TMPQ[:, :, :], TMPQ[:, :, :], ACT.Ln, scale=float(2.0 ** 20)))
                    act.activation(TMPQ[:, :, :], TMPQ[:, :, :], ACT.Exp, scale=-0.5,
                                   bias=float(10 * np.log(2.0))).then_inc(inv_norm_ready, 1)
                    act.wait_ge(unit_done, u0 + AB_BLOCKS)
                    for b in range(4):
                        act.activation(YA[:, b, :], GG[:, b, :], ACT.Copy).then_inc(ya_kept, 1)
                    act.wait_ge(ya_kept, 4)
                    act.wait_ge(fm_ready, 1)
                    for k, dst in enumerate((VT, KT, BT)):
                        for j in range(TT):
                            act.wait_ge(tr_mm, 4 * k + j + 1)
                            act.activation(dst[:, j, :], BANK[(4 * k + j) % 2][:, :], ACT.Copy).then_inc(tr_read, 1)
                    for p in range(HEADS // 2):
                        for s in range(2):
                            w = slice((2 * p + s) * CHUNK, (2 * p + s + 1) * CHUNK)
                            act.wait_ge(token_mm[s], 2 * p + 1)
                            act.activation(GT[:, :, w], BANK[4 * s + 1][:, 0:TT * CHUNK].rearrange("p (t c) -> p t c", t=TT),
                                           ACT.Copy).then_inc(token_read[s], 1)
                            act.wait_ge(token_mm[s], 2 * p + 2)
                            rows = slice(s * CHUNK, (s + 1) * CHUNK)
                            act.activation(YI[rows, p, :], BANK[4 * s + 2][rows, :], ACT.Copy).then_inc(token_read[s], 1)
                        act_inverse(p, [xt_of(2 * p + s) for s in range(2)])
                    for c in range(NCHUNK):
                        j, th = c // 2, slice(c % 2 * CHUNK, (c % 2 + 1) * CHUNK)
                        act.wait_ge(solve_mm, c + 1)
                        act.activation(GT[th, j, :], BANK[2][th, :], ACT.Copy).then_inc(solve_read, 1)
                    act.wait_ge(out_mm, 4)
                    split_hi(u0 + AB_BLOCKS, 0)
                    act.activation(MIX_HI[:, 0:4, :], YA[:, :, :], ACT.Copy).then_inc(ya_hi, 1)
                    for b in range(4):
                        act.wait_ge(dev_ready, b + 1)
                        act.activation(TMPQ[:, b, :], DF[:, b, :], ACT.Square).then_inc(out_sq_ready, 1)
                    split_hi(u0 + AB_BLOCKS + 1, 0)
                    for b in range(4):
                        act.wait_ge(out_sq_mm, b + 1)
                        step.inc(act.activation(TMPQ[:, b, :], BANK[4 + b][:, :], ACT.Ln, scale=1.0 / CHUNK, bias=64e-5))
                    step.wait()
                    act.activation(TMPQ[:, :, :], TMPQ[:, :, :], ACT.Exp, scale=-0.5).then_inc(decay_ready, 1)
                    for b in range(4):
                        act.wait_ge(mixed_ready, b + 1)
                        act.activation(MIX_HI[:, 4 + b, :], YF[:, b, :], ACT.Copy).then_inc(mixed_hi, 1)
                if phase == "c":
                    n, u0, q0 = norm_of[phase], base[phase], inv_base[phase]
                    act.wait_ge(small_weights, used["small_weights"] + 16)
                    act.activation(CTS[:, 0, :, :], CT[:, :, :], ACT.Copy).then_inc(c_tail_hi, 1)
                    for t in range(-1, C_BLOCKS):
                        if 0 <= t < C_BLOCKS - 3:
                            split_hi(u0 + t + 3, 0)
                        if 0 <= t < 24:
                            act.wait_ge(conv_ready, used["conv_ready"] + t + 1)
                            dst = (QC, KC, VC)[t // 8][:, t % 8, :]
                            act.activation(dst, dst, ACT.Silu).then_inc(silu_done, 1)
                        h = (t - 10) // 2
                        if t >= 14 and t % 2 == 0 and h - 2 < HEADS:
                            for k in range(2):
                                act.wait_ge(norm_sum_mm, used["norm_sum_mm"] + 2 * (h - 2) + k + 1)
                                step.inc(act.activation(SQT[:, (h - 2) % 4, k, :], BANK[2 + 2 * (h % 2) + k][:, :],
                                                        ACT.Ln, bias=EPS))
                            step.wait()
                            for k in range(2):
                                act.activation(SQT[:, (h - 2) % 4, k, :], SQT[:, (h - 2) % 4, k, :], ACT.Exp, scale=-0.5,
                                               bias=float(-0.5 * np.log(P)) if k == 0 else 0.0).then_inc(inv_norm_ready, 1)
                        if t >= 10 and t % 2 == 0 and h < HEADS:
                            act.wait_ge(silu_done, used["silu_done"] + 9 + h)
                            if h >= 4:
                                act.wait_ge(l2_done, 2 * (h - 3))
                            for k, src in enumerate((QC, KC)):
                                act.activation(SQT[:, h % 4, k, :], src[:, h, :], ACT.Square).then_inc(sq_c, 1)
                        if t == 29:
                            act.wait_ge(tail_scaled, 2)
                            step.link(act.activation(TL[:, 5], TL[:, 4], ACT.Abs))
                            act.activation(TL[:, 6], TL[:, 5], ACT.Exp, scale=-1.0).then_inc(al_act, 1)
                            al = PARAMS["dn_A_log"][0]
                            act.activation(TL[:, 9, 0, :], PRM[:, al:al + HEADS], ACT.Exp).then_inc(al_act, 1)
                            act.wait_ge(al_vec, 1)
                            act.activation(TL[:, 8], TL[:, 7], ACT.Ln).then_inc(al_act, 1)
                            act.activation(BETA, TL[:, 10], ACT.Sigmoid).then_inc(beta_ready, 1)
                    act.wait_ge(gtok_ready, 2)
                    act.activation(KDEC, KDEC, ACT.Exp).then_inc(kdec_ready, 1)
                    act.wait_ge(kdec_ready, 1)
                    act.wait_ge(beta_ready, 1)
                    for p in range(HEADS // 2):
                        q = q0 + p
                        for s in range(2):
                            act.wait_ge(row_mm[s], 2 * p + 2)
                            if p:
                                act.wait_ge(qk_scaled[s], 2 * p)
                            act.wait_ge(dd_ready[s], p + 1)
                            act.activation(EROW[:, s, :], BANK[4 * s + 1][:, :], ACT.Exp).then_inc(erow_ready[s], 1)
                            act.activation(DT[:, s], DT[:, s], ACT.Exp).then_inc(dexp_ready[s], 1)
                        for s in range(2):
                            h = 2 * p + s
                            for k, (dst, factor) in enumerate(((KDT, KDEC), (VTK, BETA))):
                                act.wait_ge(token_mm[s], used["token_mm"] + 2 * p + k + 1)
                                for j in range(TT):
                                    ins = act.activation(dst[:, h, j, :], BANK[4 * s + k][:, j * P:(j + 1) * P], ACT.Copy,
                                                         scale=factor[:, j, h:h + 1])
                                ins.then_inc(token_read[s], 1)
                        act_inverse(q, [XTC[:, 2 * p + s] for s in range(2)])
                    def out_copy(c):
                        act.wait_ge(out_mm, used["out_mm"] + c + 1)
                        act.activation(KC[:, :, c * CHUNK:(c + 1) * CHUNK], BANK[6 + c % 2][:, :].rearrange("p (h t) -> p h t", h=HEADS),
                                       ACT.Copy).then_inc(out_read, 1)
                        act_gate(c)

                    for c in range(NCHUNK):
                        j, th = c // 2, slice(c % 2 * CHUNK, (c % 2 + 1) * CHUNK)
                        for g in range(2):
                            act.wait_ge(solve_mm, used["solve_mm"] + 2 * c + g + 1)
                            act.activation(VTK[th, 4 * g:4 * g + 4, j, :], BANK[2 + g][th, :].rearrange("p (h v) -> p h v", h=4),
                                           ACT.Copy).then_inc(solve_read, 1)
                        if c:
                            out_copy(c - 1)
                    out_copy(NCHUNK - 1)
                    act.wait_ge(out_read, used["out_read"] + NCHUNK)
                    split_hi(u0 + C_BLOCKS, 0)
                    split_hi(u0 + C_BLOCKS + 1, 0)

                    def norm_buffer(h):
                        return (DT if h % 4 < 2 else DS)[:, h % 2].rearrange("p t c -> p (t c)")

                    def out_square(h):
                        if h >= 4:
                            act.wait_ge(mixed_ready, used["mixed_ready"] + h - 3)
                        act.activation(norm_buffer(h), KC[:, h, :], ACT.Square).then_inc(out_sq_ready, 1)

                    for h in range(4):
                        out_square(h)
                    for g in range(2):
                        for h in range(4 * g, 4 * g + 4):
                            act.wait_ge(out_sq_mm, used["out_sq_mm"] + h + 1)
                            step.inc(act.activation(norm_buffer(h), BANK[h % 4][:, :], ACT.Ln, scale=1.0 / P, bias=EPS))
                        step.wait()
                        for h in range(4 * g, 4 * g + 4):
                            act.activation(norm_buffer(h), norm_buffer(h), ACT.Exp, scale=-0.5).then_inc(orn_ready, 1)
                        for h in range(4 * g, 4 * g + 4):
                            act.wait_ge(mixed_ready, used["mixed_ready"] + h + 1)
                            act.activation(MIX_HI[:, h, :], KC[:, h, :], ACT.Copy).then_inc(mixed_hi, 1)
                            if g == 0:
                                out_square(h + 4)
                if phase in ("ab", "c"):
                    c0 = base[phase] + (AB_BLOCKS if phase == "ab" else C_BLOCKS)
                    act.wait_ge(mixer_done[phase], 1)
                    for m in range(KB):
                        if c0 + m + 2 < n_units:
                            split_hi(c0 + m + 2, 0)
                        residual(norm_of[phase] + 1, m // 2, m % 2)
            root(n_norms - 1)

        @block.gpsimd
        def _(pool):
            def residual(n, i, j):
                pool.wait_ge(sq_ready[j], KB // 2 * n + i + 1)
                if j == 0 and fits(3 * n + i):
                    pool.wait_ge(acc_ready[1], 3 * n + i)
                if j == 1:
                    pool.wait_ge(acc_ready[0], KB // 2 * n + i + 1)
                pool.tensor_tensor(ACC[:, :], ACC[:, :], US[:, j, :], ALU.add).then_inc(acc_ready[j], 1)

            def clear(n):
                if n:
                    pool.wait_ge(sum_ready, n)
                pool.memset(ACC[:, :], 0.0).then_inc(acc_clear, 1)
                pool.wait_ge(acc_clear, n + 1)

            def squares(n):
                clear(n)
                for j in range(2):
                    residual(n, 0, j)
                with pool.Fori(1, KB // 2 - 1) as i:
                    for j in range(2):
                        residual(n, i, j)
                residual(n, KB // 2 - 1, 0)


            def pool_inverse(q, masked):
                for s in range(2):
                    w = INV[s]
                    pool.wait_ge(mat_ready[s], masked)
                    if q:
                        pool.wait_ge(u_mm[s], 5 * q)
                        pool.wait_ge(xx_mm[s], 9 * q)
                    step.link(pool.tensor_tensor(w["TM"][:, :, :], w["TT"][:, :, :], tiles(con("pair1")), ALU.mult))
                    pool.tensor_tensor(w["XT"][:, :, :], tiles(con("ident")), w["TM"][:, :, :],
                                       ALU.subtract).then_inc(xt1_ready[s], 1)
                for l in range(5):
                    for s in range(2):
                        w = INV[s]
                        if l:
                            pool.wait_ge(u_mm[s], 5 * q + l)
                        else:
                            pool.wait_ge(xt1_ready[s], q + 1)
                        pool.tensor_tensor(w["TM"][:, :, :], w["TT"][:, :, :], tiles(con(f"pair{2 << l}")),
                                           ALU.mult).then_inc(tm_ready[s], 1)

            step = Steps(pool, pool_step)
            squares(0)
            for phase in plan:
                if phase == "ab":
                    for p in range(HEADS // 2):
                        pool_inverse(p, 4 * p + 1)
                if phase == "c":
                    for p in range(HEADS // 2):
                        pool_inverse(inv_base[phase] + p, mat_base + p + 1)
                        for s in range(2):
                            pool.wait_ge(att_ready[s], p + 1)
                            pool.tensor_tensor(ATT[:, 2 * p + s], ATT[:, 2 * p + s], tiles(con("upper")),
                                               ALU.mult).then_inc(dmask_ready[s], 1)
                squares(norm_of[phase] + 1)

        @block.vector
        def _(vec):
            def split_lo(c, i):
                cols = units[c][1]
                vec.wait_ge(hi_ready, c + 4 * i + 1)
                vec.tensor_tensor(WS[:, 1, c % SPLIT, 0:cols], RAW[:, c % RING, 0:cols],
                                  WS[:, 0, c % SPLIT, 0:cols].bitcast(F32), ALU.subtract).then_inc(lo_ready, 1)

            def split_next(c, i):
                if isinstance(i, int):
                    c, i = c + 4 * i, 0
                if not isinstance(i, int) or c < n_units:
                    split_lo(c, i)

            def residual_add(n, i, j, bank, factor, done):
                vec.wait_ge(unit_done, done)
                vec.scalar_tensor_tensor(X[:, 2 * i + j, :], bank[:, :], factor, X[:, 2 * i + j, :],
                                         ALU.mult, ALU.add).then_inc(x_ready[j], 1)

            def residual_split(n, i, j):
                q = KB // 2 * n + i
                vec.wait_ge(x_ready[j], q + 1)
                if fits(q):
                    vec.wait_ge(h_ready[j], q)
                w = norm_cols[n] + j + 2 * i
                vec.tensor_scalar(GS[:, j, :], X[:, 2 * i + j, :],
                                  PRM[:, w:w + 1] if isinstance(i, int) else PRM[:, bass.ds(w, 1)],
                                  None, ALU.mult).then_inc(hw_ready[j], 1)
                vec.wait_ge(hhi_ready[j], q + 1)
                vec.tensor_tensor(H[:, 1, 2 * i + j, :], GS[:, j, :], H[:, 0, 2 * i + j, :].bitcast(F32),
                                  ALU.subtract).then_inc(h_ready[j], 1)

            def inverse_root(n):
                vec.wait_ge(rms_ready, n + 1)
                vec.reciprocal(RSTD[:, :], RSTD[:, :]).then_inc(rstd_ready, 1)

            def scaled(phase, i, j, k):
                q = ffn_index[phase] * (FB // 2) + i
                vec.wait_ge(unit_done, base[phase] + 4 * i + 2 * j + k + 1)
                if fits(q):
                    vec.wait_ge((prod_ready, act_ready)[k][j], q)
                vec.tensor_tensor((GS, US)[k][:, j, :], (GATE, UP)[k][j][:, :], RSTD[:, :],
                                  ALU.mult).then_inc((gs_ready, us_ready)[k][j], 1)

            def product(phase, i, j):
                q = ffn_index[phase] * (FB // 2) + i
                vec.wait_ge(silu_ready[j], q + 1)
                vec.wait_ge(us_ready[j], q + 1)
                vec.tensor_tensor(US[:, j, :], GS[:, j, :], US[:, j, :], ALU.mult).then_inc(prod_ready[j], 1)

            def product_lo(phase, i, j):
                q = ffn_index[phase] * (FB // 2) + i
                vec.wait_ge(ahi_ready[j], q + 1)
                vec.tensor_tensor(A[:, 1, 2 * i + j, :], US[:, j, :], A[:, 0, 2 * i + j, :].bitcast(F32),
                                  ALU.subtract).then_inc(act_ready[j], 1)


            def vec_inverse(q):
                for l in range(5):
                    for s in range(2):
                        vec.wait_ge(u_mm[s], 5 * q + l + 1)
                        vec.tensor_tensor(INV[s]["IU"][:, :, :], tiles(con("ident")),
                                          BANK[4 * s + 3][:, :].rearrange("p (t c) -> p t c", t=TT),
                                          ALU.subtract).then_inc(iu_ready[s], 1)

            def unit_vectors(h):
                for k, t in enumerate((QC, KC)):
                    vec.wait_ge(inv_norm_ready, used["inv_norm_ready"] + 2 * h + k + 1)
                    vec.tensor_tensor(t[:, h, :], t[:, h, :], SQT[:, h % 4, k, :], ALU.mult).then_inc(l2_done, 1)

            step = Steps(vec, vec_step)
            for i in range(KB // 2):
                vec.wait_ge(x_landed[i], 32 if i == 0 else 16)
                if i == 1:
                    split_lo(0, 0)
                if i == 3:
                    split_lo(1, 0)
                for j in range(2):
                    vec.sem_inc(x_ready[j], 1)
                    residual_split(0, i, j)
            vec.wait_ge(landed, 16)
            for phase in plan:
                split_lo(base[phase] + 2, 0)
                inverse_root(norm_of[phase])
                vec.wait_ge(rstd_ready, norm_of[phase] + 1)
                if phase.startswith("ffn"):
                    def up(i, j, c, first=False):
                        if first:
                            split_lo(c + 3, 0)
                        scaled(phase, i, j, 0)
                        if not first:
                            split_lo(c + 2 * j + 2, 0 if isinstance(i, int) else i)
                        scaled(phase, i, j, 1)
                        product(phase, i, j)
                        if not first:
                            split_lo(c + 2 * j + 3, 0 if isinstance(i, int) else i)
                        product_lo(phase, i, j)

                    def down(i, j):
                        c = base[phase] + 2 * FB + 2 * j
                        split_next(c + 2, i)
                        residual_add(norm_of[phase] + 1, i, j, DOWN[j], 0.5, c + 4 * i + 2)
                        split_next(c + 3, i)
                        if norm_of[phase] + 1 < n_norms - 1:
                            residual_split(norm_of[phase] + 1, i, j)

                    for j in range(2):
                        up(0, j, base[phase], first=j == 0)
                    with vec.Fori(1, FB // 2 - 1) as i:
                        for j in range(2):
                            up(i, j, base[phase])
                    for j in range(2):
                        up(FB // 2 - 1, j, base[phase] + 4 * (FB // 2 - 1))
                    with vec.Fori(0, KB // 2 - 1) as i:
                        for j in range(2):
                            down(i, j)
                    for j in range(2):
                        down(KB // 2 - 1, j)
                if phase == "ab":
                    n, u0 = norm_of[phase], base[phase]
                    vec.wait_ge(unit_done, u0)
                    vec.memset(LW[:, :, :, :], 0.0).then_inc(pad_zero, 1)
                    vec.wait_ge(h_ready[1], KB // 2 * (n + 1))
                    vec.wait_ge(sum_ready, n + 1)
                    vec.memset(PAD[:, :, 0:3], 0.0).then_inc(pad_zero, 1)
                    S = [SMALL[:, k, :] for k in range(16)]
                    vec.wait_ge(sp_act, 1)
                    step.link(vec.tensor_scalar(S[2], S[1], 1.0, None, ALU.add))
                    vec.sem_inc(sp_vec, 1)
                    step.link(vec.tensor_scalar(S[4], S[2], 1.0, None, ALU.subtract))
                    step.link(vec.tensor_scalar(S[5], S[4], 0.0, None, ALU.is_equal))
                    step.link(vec.tensor_tensor(S[4], S[4], S[5], ALU.add))
                    step.link(vec.reciprocal(S[6], S[4]))
                    vec.wait_ge(sp_act, 2)
                    step.link(vec.tensor_tensor(S[7], S[3], S[5], ALU.add))
                    step.link(vec.tensor_tensor(S[7], S[7], S[1], ALU.mult))
                    step.link(vec.tensor_tensor(S[7], S[7], S[6], ALU.mult))
                    ap = PRM[:, PARAMS["lru_a_param"][0]:PARAMS["lru_a_param"][0] + 4]
                    step.link(vec.tensor_scalar(S[8], ap, -1.0, 0.0, ALU.mult, ALU.max))
                    step.link(vec.tensor_tensor(S[7], S[7], S[8], ALU.add))
                    step.link(vec.tensor_scalar(LRU_SCALE, S[7], 8.0, None, ALU.mult))
                    vec.tensor_scalar(LRU_NSCALE, S[7], -8.0, None, ALU.mult).then_inc(sp_vec, 1)
                    vec.wait_ge(pad_zero, 2)
                    for t in range(AB_BLOCKS):
                        pad = PAD[:, t % 2, :]
                        z = pad[:, 3:3 + SEQ]
                        step.wait()
                        if 4 <= t - 2 < 8:
                            vec.wait_ge(silu_done, t - 2 - 3)
                        vec.wait_ge(unit_done, u0 + t + 1)
                        vec.tensor_tensor(z, BANK[t % 2][:, :], RSTD[:, :], ALU.mult).then_inc(z_read, 1)
                        if 0 < t < AB_BLOCKS - 2:
                            split_lo(u0 + t + 2, 0)
                        vec.wait_ge(z_read, t + 1)
                        if t < 4:
                            dst = XC[:, t, :]
                            step.link(vec.tensor_scalar(dst, z, par("lru_conv_w", 12 + t), par("lru_conv_b", t), ALU.mult, ALU.add))
                            for k in (2, 1, 0):
                                ins = vec.scalar_tensor_tensor(dst, pad[:, k:k + SEQ], par("lru_conv_w", 4 * k + t), dst,
                                                               ALU.mult, ALU.add)
                                if k:
                                    step.link(ins)
                            ins.then_inc(conv_ready, 1)
                            vec.wait_ge(conv_ready, t + 1)
                        if t >= 8:
                            dst = ([LOW[:, 0, :], LOW[:, 1, :]] + [KF[:, b, :] for b in range(4)]
                                   + [VF[:, b, :] for b in range(4)] + [RF[:, b, :] for b in range(4)])[t - 8]
                            mu = ([12, 13] + list(range(4, 12)) + list(range(4)))[t - 8]
                            if t > 8:
                                vec.wait_ge(p_ready, t - 8)
                            step.link(vec.tensor_tensor(DIFF[:, :], pad[:, 2:2 + SEQ], z, ALU.subtract))
                            vec.scalar_tensor_tensor(dst, DIFF[:, :], par("rwkv_mu", mu), z,
                                                     ALU.mult, ALU.add).then_inc(p_ready, 1)
                            vec.wait_ge(p_ready, t - 7)
                        if t == 14:
                            vec.wait_ge(lru_sq, 1)
                            vec.scalar_tensor_tensor(flat(LU), flat(RG), 1.0, flat(LU), ALU.add, ALU.mult).then_inc(lru_u2, 1)
                            vec.wait_ge(gate_read, 8)
                            step.link(vec.tensor_tensor(IG[:, :, :], IG[:, :, :], XC[:, :, :], ALU.mult))
                        if t == 16:
                            vec.wait_ge(lru_root, 1)
                            step.link(vec.tensor_tensor(IG[:, :, :], IG[:, :, :], LU[:, :, :], ALU.mult))
                        if t in (17, 18):
                            for b in (2 * (t - 17), 2 * (t - 17) + 1):
                                step.link(vec.tensor_tensor_scan(XC[:, b, :], LA[:, b, :], IG[:, b, :], 0.0, ALU.mult, ALU.add))
                        if t == 19:
                            vec.wait_ge(silu_done, 4)
                            vec.tensor_tensor(GG[:, :, :], XC[:, :, :], GG[:, :, :], ALU.mult).then_inc(ya_ready, 1)
                    vec.wait_ge(low_read, 4)
                    for b in range(4):
                        step.inc(vec.tensor_tensor_scan(CUM[:, b, :], CST[:, NCONST - SEQ:NCONST], SIG[:, b, :], 0.0,
                                                        ALU.mult, ALU.add))
                    step.wait()
                    vec.sem_inc(cum_ready, 1)
                    vec.tensor_tensor(CPRE[:, :, :], CUM[:, :, :], SIG[:, :, :], ALU.subtract).then_inc(cum_ready, 1)
                    vec.wait_ge(cum_ready, 2)
                    for b in range(4):
                        vec.tensor_scalar(SIG[:, b, :], KF[:, b, :], par("rwkv_k_k", b), None, ALU.mult).then_inc(kk_raw, 1)
                    for b in range(4):
                        vec.wait_ge(norm_sum_mm, b + 1)
                        vec.tensor_scalar(TMPQ[:, b, :], BANK[(6, 7, 0, 1)[b]][:, :], 1e-24, None, ALU.max).then_inc(ss_max, 1)
                    vec.wait_ge(kk_raw, 4)
                    vec.wait_ge(unit_done, u0 + AB_BLOCKS)
                    for b in range(4):
                        vec.wait_ge(low_read, 5 + b)
                        step.inc(vec.tensor_scalar(T2[:, b, :], AL[:, b, :], -1.0, par("rwkv_k_a", b), ALU.add, ALU.mult))
                    step.wait()
                    step.link(vec.scalar_tensor_tensor(flat(KF), flat(T2), 1.0, flat(KF), ALU.add, ALU.mult))
                    for b in range(4):
                        vec.scalar_tensor_tensor(T2[:, b, :], RF[:, b, :], par("rwkv_r_k", b), KF[:, b, :],
                                                 ALU.mult, ALU.mult).then_inc(bon_in, 1)
                    vec.wait_ge(exp_ready, 2)
                    step.link(vec.tensor_copy(PEND[:, :, :], CUM[:, :, :].rearrange("p b (c k) -> p b c k", k=CHUNK)[:, :, :, CHUNK - 1]))
                    vec.wait_ge(bon_in, 4)
                    vec.tensor_tensor(RF[:, :, :], RF[:, :, :], CUM[:, :, :], ALU.mult).then_inc(fm_ready, 1)
                    vec.tensor_tensor(KF[:, :, :], KF[:, :, :], PINV[:, :, :], ALU.mult).then_inc(fm_ready, 1)
                    vec.wait_ge(fm_ready, 2)
                    pend = PEND[:, :, :].rearrange("p b c -> p (b c)").unsqueeze(2).to_broadcast([P, 32, CHUNK])
                    chunks = [flat(t_).rearrange("p (c k) -> p c k", k=CHUNK) for t_ in (KH, KF, PINV, AL)]
                    vec.tensor_tensor(chunks[0], chunks[1], pend, ALU.mult).then_inc(fm_ready, 1)
                    vec.wait_ge(inv_norm_ready, 1)
                    step.link(vec.tensor_tensor(SIG[:, :, :], SIG[:, :, :], TMPQ[:, :, :], ALU.mult))
                    step.link(vec.tensor_tensor(AL[:, :, :], AL[:, :, :], SIG[:, :, :], ALU.mult))
                    vec.wait_ge(exp_ready, 3)
                    vec.tensor_tensor(CPRE[:, :, :], CPRE[:, :, :], SIG[:, :, :], ALU.mult).then_inc(fm_ready, 1)
                    vec.tensor_tensor(AL[:, :, :], AL[:, :, :], PINV[:, :, :], ALU.mult).then_inc(fm_ready, 1)
                    vec.wait_ge(fm_ready, 5)
                    vec.scalar_tensor_tensor(chunks[2], chunks[3], -1.0, pend, ALU.mult, ALU.mult).then_inc(fm_ready, 1)
                    for b in range(4):
                        vec.wait_ge(bon_mm, b + 1)
                        vec.tensor_tensor(BV[:, b, :], BANK[2 + b][:, :], VF[:, b, :], ALU.mult).then_inc(bv_ready, 1)
                    for p in range(HEADS // 2):
                        for s in range(2):
                            h = 2 * p + s
                            if p:
                                vec.wait_ge(tm_ready[s], 5 * p)
                                vec.wait_ge(token_mm[s], 2 * p)
                            else:
                                vec.wait_ge(bv_ready, 4)
                                vec.wait_ge(bon_mm, 4)
                            for k, (dst, mask) in enumerate(((INV[s]["TT"][:, :, :], "strict"), (TKM[s][:, :, :], "strict"),
                                                             (MKM[s][:, :, :], "upper"))):
                                vec.wait_ge(mat_mm[s], 4 * p + k + 1)
                                vec.tensor_tensor(dst, BANK[4 * s + k][:, :].rearrange("p (t c) -> p t c", t=TT),
                                                  tiles(con(mask)), ALU.mult).then_inc(mat_ready[s], 1)
                            vec.wait_ge(mat_mm[s], 4 * p + 4)
                            vec.scalar_tensor_tensor(MBT[:, h, :].rearrange("p (t c) -> p t c", t=TT),
                                                     BANK[4 * s + 3][:, :].rearrange("p (t c) -> p t c", t=TT), -1.0,
                                                     tiles(con("upper")), ALU.mult, ALU.mult).then_inc(mat_ready[s], 1)
                        vec_inverse(p)
                    for s in range(2):
                        vec.wait_ge(xx_read[s], 36)
                        vec.wait_ge(token_read[s], 8)
                    step.link(vec.memset(SH[:, 0, :, :], 0.0))
                    for c in range(NCHUNK):
                        j, th = c // 2, slice(c % 2 * CHUNK, (c % 2 + 1) * CHUNK)
                        if c:
                            for s in range(2):
                                vec.wait_ge(predict_mm, 2 * (c - 1) + s + 1)
                                g = GT[th, j, :].rearrange("p (b s v) -> p b s v", s=2, v=CHUNK)[:, :, s, :]
                                vec.tensor_tensor(g, g, BANK[s][th, 0:4 * CHUNK].rearrange("p (b v) -> p b v", v=CHUNK),
                                                  ALU.add).then_inc(predict_added, 1)
                        if c < NCHUNK - 1:
                            step.link(vec.tensor_tensor(SDEC[:, :, :], SH[:, c, :, :],
                                                        PEND[:, :, c].unsqueeze(2).to_broadcast([P, 4, CHUNK]), ALU.mult))
                            vec.wait_ge(state_mm, c + 1)
                            vec.tensor_tensor(SH[:, c + 1, :, :], SDEC[:, :, :],
                                              BANK[3][:, 0:4 * CHUNK].rearrange("p (b v) -> p b v", v=CHUNK),
                                              ALU.add).then_inc(state_ready, 1)
                            vec.wait_ge(state_ready, c + 1)
                    for b in range(4):
                        vec.wait_ge(out_mm, b + 1)
                        vec.tensor_tensor(YF[:, b, :], BANK[4 + b][:, :], YI[:, b, :], ALU.add).then_inc(out_read, 1)
                    for b in range(4):
                        vec.wait_ge(mean_mm, b + 1)
                        vec.wait_ge(out_read, b + 1)
                        vec.scalar_tensor_tensor(DF[:, b, :], BANK[b][:, :], -1.0 / CHUNK, YF[:, b, :],
                                                 ALU.mult, ALU.add).then_inc(dev_ready, 1)
                    vec.wait_ge(ya_hi, 1)
                    vec.tensor_tensor(MIX_LO[:, 0:4, :], YA[:, :, :], MIX_HI[:, 0:4, :].bitcast(F32), ALU.subtract).then_inc(ya_lo, 1)
                    split_lo(u0 + AB_BLOCKS, 0)
                    split_lo(u0 + AB_BLOCKS + 1, 0)
                    def mixed_rest(b):
                        vec.wait_ge(mixed_hi, b + 1)
                        vec.tensor_tensor(MIX_LO[:, 4 + b, :], YF[:, b, :], MIX_HI[:, 4 + b, :].bitcast(F32),
                                          ALU.subtract).then_inc(mixed_lo, 1)

                    vec.wait_ge(decay_ready, 1)
                    for b in range(4):
                        step.link(vec.tensor_tensor(DF[:, b, :], DF[:, b, :], TMPQ[:, b, :], ALU.mult))
                        step.link(vec.scalar_tensor_tensor(DF[:, b, :], DF[:, b, :], par("rwkv_ln_w", b), BV[:, b, :], ALU.mult, ALU.add))
                        vec.wait_ge(g_mm, b + 1)
                        vec.scalar_tensor_tensor(YF[:, b, :], DF[:, b, :], par("rwkv_ln_b", b), BANK[b][:, :],
                                                 ALU.add, ALU.mult).then_inc(mixed_ready, 1)
                        if b:
                            mixed_rest(b - 1)
                    mixed_rest(3)
                    vec.wait_ge(mixed_lo, 4)
                    vec.wait_ge(ya_lo, 1)
                    vec.sem_inc(mixer_done[phase], 1)
                if phase == "c":
                    n, u0, q0 = norm_of[phase], base[phase], inv_base[phase]
                    vec.wait_ge(h_ready[1], KB // 2 * (n + 1))
                    vec.wait_ge(sum_ready, n + 1)
                    vec.memset(PAD[:, :, 0:3], 0.0).then_inc(pad_zero, 1)
                    vec.wait_ge(pad_zero, used["pad_zero"] + 1)
                    vec.wait_ge(c_tail_hi, 1)
                    vec.tensor_tensor(CTS[:, 1, :, :], CT[:, :, :], CTS[:, 0, :, :].bitcast(F32), ALU.subtract).then_inc(c_tail_lo, 1)
                    def tail():
                        vec.wait_ge(small_mm, used["small_mm"] + 2)
                        for k in range(2):
                            step.inc(vec.tensor_copy(TL[:, 10 + k], BANK[7][:, 0:64].rearrange("p (t k h) -> p t k h", t=TT, k=2)[:, :, k, :]))
                        step.wait()
                        vec.sem_inc(tail_scaled, 1)
                        db = PARAMS["dn_dt_bias"][0]
                        vec.tensor_tensor(TL[:, 4], TL[:, 11], PRM[:, db:db + HEADS].unsqueeze(1).to_broadcast([P, TT, HEADS]),
                                          ALU.add).then_inc(tail_scaled, 1)
                        vec.wait_ge(al_act, 1)
                        step.link(vec.tensor_scalar(TL[:, 7], TL[:, 6], 1.0, None, ALU.add))
                        vec.sem_inc(al_vec, 1)
                        step.link(vec.tensor_scalar(TL[:, 12], TL[:, 7], 1.0, None, ALU.subtract))
                        step.link(vec.tensor_scalar(TL[:, 13], TL[:, 12], 0.0, None, ALU.is_equal))
                        step.link(vec.tensor_tensor(TL[:, 12], TL[:, 12], TL[:, 13], ALU.add))
                        step.link(vec.reciprocal(TL[:, 14], TL[:, 12]))
                        vec.wait_ge(al_act, 3)
                        step.link(vec.tensor_tensor(TL[:, 15], TL[:, 8], TL[:, 13], ALU.add))
                        step.link(vec.tensor_tensor(TL[:, 15], TL[:, 15], TL[:, 6], ALU.mult))
                        step.link(vec.tensor_tensor(TL[:, 15], TL[:, 15], TL[:, 14], ALU.mult))
                        vec.wait_ge(tail_scaled, 2)
                        step.link(vec.tensor_scalar(TL[:, 16], TL[:, 4], 0.0, None, ALU.max))
                        step.link(vec.tensor_tensor(TL[:, 15], TL[:, 15], TL[:, 16], ALU.add))
                        vec.wait_ge(al_act, 2)
                        vec.scalar_tensor_tensor(TL[:, 3], TL[:, 15], -1.0, TL[:, 9, 0:1, :].to_broadcast([P, TT, HEADS]),
                                                 ALU.mult, ALU.mult).then_inc(decay_ready, 1)

                    for t in range(C_BLOCKS):
                        step.wait()
                        vec.wait_ge(unit_done, u0 + t + 1)
                        if t < 24:
                            pad = PAD[:, t % 2, :]
                            z = pad[:, 3:3 + SEQ]
                            if t >= 2:
                                vec.wait_ge(conv_ready, used["conv_ready"] + t - 1)
                        else:
                            z = GC_[:, t - 24, :]
                        vec.tensor_tensor(z, BANK[t % 2][:, :], RSTD[:, :], ALU.mult).then_inc(z_read, 1)
                        if 0 < t < C_BLOCKS - 2:
                            split_lo(u0 + t + 2, 0)
                        if t < 24:
                            vec.wait_ge(z_read, used["z_read"] + t + 1)
                            dst = (QC, KC, VC)[t // 8][:, t % 8, :]
                            step.link(vec.tensor_scalar(dst, z, par("dn_conv_w", 72 + t), None, ALU.mult))
                            for k in (2, 1, 0):
                                ins = vec.scalar_tensor_tensor(dst, pad[:, k:k + SEQ], par("dn_conv_w", 24 * k + t), dst,
                                                               ALU.mult, ALU.add)
                                if k:
                                    step.link(ins)
                            ins.then_inc(conv_ready, 1)
                        if t >= 15 and t % 2 and (t - 15) // 2 < HEADS:
                            unit_vectors((t - 15) // 2)
                        if t == 27:
                            vec.wait_ge(small_mm, used["small_mm"] + 1)
                            vec.tensor_tensor(TF[0:2 * HEADS, :], BANK[6][0:2 * HEADS, :], RSTD[0:2 * HEADS, :],
                                              ALU.mult).then_inc(tf_ready, 1)
                        if t == 29:
                            tail()
                    vec.wait_ge(gcum_mm, 1)
                    vec.tensor_copy(GSUM, BANK[7][:, 128:160].rearrange("p (t h) -> p t h", t=TT)).then_inc(gtok_ready, 1)
                    vec.wait_ge(gtok_ready, 1)
                    vec.tensor_tensor(KDEC, BANK[7][:, 192:224].rearrange("p (t h) -> p t h", t=TT), GSUM,
                                      ALU.subtract).then_inc(gtok_ready, 1)
                    for p in range(HEADS // 2):
                        q = q0 + p
                        for s in range(2):
                            h = 2 * p + s
                            vec.wait_ge(row_mm[s], 2 * p + 1)
                            if p:
                                vec.wait_ge(qk_scaled[s], 2 * p)
                            vec.tensor_tensor(KBETA[:, s, :], BANK[4 * s][:, :], KC[:, h, :], ALU.mult).then_inc(kbeta_ready[s], 1)
                            vec.wait_ge(row_mm[s], 2 * p + 2)
                            if p:
                                vec.wait_ge(att_ready[s], p)
                            for j in range(TT):
                                ins = vec.tensor_scalar(DT[:, s, j, :], BANK[4 * s + 1][:, j * P:(j + 1) * P],
                                                        GSUM[:, j, h:h + 1], 0.0, ALU.subtract, ALU.min)
                            ins.then_inc(dd_ready[s], 1)
                        for s in range(2):
                            h = 2 * p + s
                            vec.wait_ge(dexp_ready[s], p + 1)
                            vec.wait_ge(kq_mm[s], 2 * p + 1)
                            if q:
                                vec.wait_ge(tm_ready[s], 5 * q)
                            vec.tensor_tensor(INV[s]["TT"][:, :, :], BANK[4 * s + 2][:, :].rearrange("p (t c) -> p t c", t=TT),
                                              DT[:, s], ALU.mult).then_inc(mat_ready[s], 1)
                        for s in range(2):
                            h = 2 * p + s
                            vec.wait_ge(kq_mm[s], 2 * p + 2)
                            vec.tensor_tensor(ATT[:, h], BANK[4 * s + 3][:, :].rearrange("p (t c) -> p t c", t=TT),
                                              DT[:, s], ALU.mult).then_inc(att_ready[s], 1)
                            vec.wait_ge(erow_ready[s], p + 1)
                            step.link(vec.tensor_copy(CD[:, h, :], EROW[:, s, :].rearrange("p (c k) -> p c k", k=CHUNK)[:, :, CHUNK - 1]))
                            vec.tensor_tensor(QC[:, h, :], QC[:, h, :], EROW[:, s, :], ALU.mult).then_inc(qk_scaled[s], 1)
                            vec.wait_ge(token_mm[s], used["token_mm"] + 2 * p + 1)
                            vec.wait_ge(kbeta_ready[s], p + 1)
                            vec.tensor_tensor(KC[:, h, :], KBETA[:, s, :], EROW[:, s, :], ALU.mult).then_inc(qk_scaled[s], 1)
                        vec_inverse(q)
                    for s in range(2):
                        vec.wait_ge(token_mm[s], used["token_mm"] + 8)
                    step.link(vec.memset(SC[:, 0, :, :], 0.0))
                    for c in range(NCHUNK):
                        j, th = c // 2, slice(c % 2 * CHUNK, (c % 2 + 1) * CHUNK)
                        if c:
                            for g in range(2):
                                vec.wait_ge(predict_mm, used["predict_mm"] + 2 * (c - 1) + g + 1)
                                if c == 1:
                                    for s in range(2):
                                        vec.wait_ge(token_read[s], used["token_read"] + 8)
                                v = VTK[th, 4 * g:4 * g + 4, j, :]
                                vec.tensor_tensor(v, v, BANK[g][th, :].rearrange("p (h v) -> p h v", h=4),
                                                  ALU.subtract).then_inc(predict_added, 1)
                        if c < NCHUNK - 1:
                            for g in range(2):
                                vec.wait_ge(state_mm, used["state_mm"] + 2 * c + g + 1)
                                if c:
                                    vec.wait_ge(out_mm, used["out_mm"] + c)
                                for h in range(4 * g, 4 * g + 4):
                                    ins = vec.scalar_tensor_tensor(SC[:, (c + 1) % 2, h, :], SC[:, c % 2, h, :], CD[:, h, c:c + 1],
                                                                   BANK[4 + g][:, h % 4 * P:(h % 4 + 1) * P], ALU.mult, ALU.add)
                                ins.then_inc(state_ready, 1)
                            vec.wait_ge(state_ready, used["state_ready"] + 2 * c + 2)
                    split_lo(u0 + C_BLOCKS, 0)
                    split_lo(u0 + C_BLOCKS + 1, 0)
                    for h in range(HEADS):
                        vec.wait_ge(orn_ready, h + 1)
                        rn = (DT if h % 4 < 2 else DS)[:, h % 2].rearrange("p t c -> p (t c)")
                        step.link(vec.scalar_tensor_tensor(KC[:, h, :], KC[:, h, :], par("dn_norm"), rn, ALU.mult, ALU.mult))
                        vec.wait_ge(gate_c, h + 1)
                        vec.tensor_tensor(KC[:, h, :], KC[:, h, :], GC_[:, h, :], ALU.mult).then_inc(mixed_ready, 1)
                        if h:
                            vec.wait_ge(mixed_hi, used["mixed_hi"] + h)
                            vec.tensor_tensor(MIX_LO[:, h - 1, :], KC[:, h - 1, :], MIX_HI[:, h - 1, :].bitcast(F32),
                                              ALU.subtract).then_inc(mixed_lo, 1)
                    vec.wait_ge(mixed_hi, used["mixed_hi"] + HEADS)
                    vec.tensor_tensor(MIX_LO[:, HEADS - 1, :], KC[:, HEADS - 1, :], MIX_HI[:, HEADS - 1, :].bitcast(F32),
                                      ALU.subtract).then_inc(mixed_lo, 1)
                    vec.wait_ge(mixed_lo, used["mixed_lo"] + HEADS)
                    vec.sem_inc(mixer_done[phase], 1)
                if phase in ("ab", "c"):
                    c0 = base[phase] + (AB_BLOCKS if phase == "ab" else C_BLOCKS)
                    for m in range(KB):
                        residual_add(norm_of[phase] + 1, m // 2, m % 2, DOWN[m % 2], 1.0, c0 + m + 1)
                        if c0 + m + 2 < n_units:
                            split_lo(c0 + m + 2, 0)
                        if norm_of[phase] + 1 < n_norms - 1:
                            residual_split(norm_of[phase] + 1, m // 2, m % 2)
            n = n_norms - 1
            inverse_root(n)
            vec.wait_ge(rstd_ready, n + 1)
            for m in range(KB):
                w = norm_cols[n] + m
                vec.scalar_tensor_tensor(HF[:, m, :], X[:, m, :], PRM[:, w:w + 1], RSTD[:, :],
                                         ALU.mult, ALU.mult).then_inc(out_ready, 1)


def kernel(**inputs):
    import numpy as _np
    import concourse.bacc as _bacc
    from concourse import mybir as _mybir
    from concourse.bass_utils import run_bass_kernel_spmd as _run

    arrays = layout(inputs)
    nc = _bacc.Bacc("TRN2", target_bir_lowering=False, num_devices=1)
    args = [nc.dram_tensor(f"in_{k}", a.shape, _mybir.dt.from_np(a.dtype), kind="ExternalInput").ap()
            for k, a in arrays.items()]
    args.append(nc.dram_tensor("out_0_dram", (KB, P, SEQ), _mybir.dt.float32, kind="ExternalOutput").ap())
    hybrid_trunk_kernel(nc, *args)
    r = _run(nc, [{f"in_{k}": a for k, a in arrays.items()}], core_ids=[0])
    got = r.results[0]["out_0_dram"]
    return _np.ascontiguousarray(got.reshape(D_MODEL, SEQ).transpose(1, 0)).reshape(1, SEQ, D_MODEL)
```
